# Optimizing a Trainium2 kernel written in Bass

```python
import jax, jax.numpy as jnp
from jax import lax
import numpy as np
import math

D_MODEL = 1024
BATCH = 1
SEQ = 256
DEPTH = 1

D_MIX = D_MODEL
ATTN_HEADS = 8
HEAD_DIM = 64
D_ATTN = ATTN_HEADS * HEAD_DIM
CONV_GROUPS = 8
D_CONV = D_MIX - D_ATTN
CONV_WIDTH = 3
IDX_HEADS = 8
IDX_DIM = 64
MAX_TOPK = 256
Q_BLOCK = 128
PEER_HEADS = 8
PEER_KEYS = 128
PEER_EXPERTS = PEER_KEYS * PEER_KEYS
PEER_HALF = 128
PEER_QDIM = 2 * PEER_HALF
PEER_TOPK = 16
EPS = 1e-6

SPLITS = [D_ATTN, D_ATTN, D_ATTN, D_CONV, D_CONV, D_CONV, IDX_HEADS * IDX_DIM, IDX_DIM, IDX_HEADS]
D_IN = sum(SPLITS)


def rms_norm(x, w):
    xf = x.astype(jnp.float32)
    y = xf * lax.rsqrt(jnp.mean(xf * xf, axis=-1, keepdims=True) + EPS)
    return (y * w.astype(jnp.float32)).astype(x.dtype)

def _gather_rows(t, idx):
    return jax.vmap(lambda tb, ib: tb[ib])(t, idx)

def dsa_attention(q, k, v, iq, ik, iw):
    B, L = q.shape[0], q.shape[1]
    topk = min(MAX_TOPK, L // 4)
    n_blocks = L // Q_BLOCK
    s_pos = jnp.arange(L)
    att_scale = HEAD_DIM ** -0.5
    idx_scale = (IDX_DIM ** -0.5) * (IDX_HEADS ** -0.5)

    def block_fn(blk):
        start = blk * Q_BLOCK
        qb = lax.dynamic_slice_in_dim(q, start, Q_BLOCK, axis=1)
        iqb = lax.dynamic_slice_in_dim(iq, start, Q_BLOCK, axis=1)
        iwb = lax.dynamic_slice_in_dim(iw, start, Q_BLOCK, axis=1)
        t_pos = start + jnp.arange(Q_BLOCK)
        rel = jax.nn.relu(jnp.einsum('bqhd,bsd->bqhs', iqb, ik).astype(jnp.float32))
        score = jnp.einsum('bqhs,bqh->bqs', rel, iwb.astype(jnp.float32)) * idx_scale
        causal = s_pos[None, None, :] <= t_pos[None, :, None]
        score = jnp.where(causal, score, -jnp.inf)
        _, sel = lax.top_k(score, topk)
        k_sel = _gather_rows(k, sel)
        v_sel = _gather_rows(v, sel)
        logits = jnp.einsum('bqhd,bqkhd->bhqk', qb, k_sel).astype(jnp.float32) * att_scale
        valid = (sel <= t_pos[None, :, None])[:, None, :, :]
        logits = jnp.where(valid, logits, -jnp.inf)
        p = jax.nn.softmax(logits, axis=-1).astype(v.dtype)
        o = jnp.einsum('bhqk,bqkhd->bqhd', p, v_sel)
        return o.reshape(B, Q_BLOCK, ATTN_HEADS * HEAD_DIM)

    out = lax.map(block_fn, jnp.arange(n_blocks))
    return out.transpose(1, 0, 2, 3).reshape(B, L, ATTN_HEADS * HEAD_DIM)

def short_conv(b_gate, c_gate, xc, conv_w, conv_b):
    L = xc.shape[1]
    u = c_gate * xc
    up = jnp.pad(u, ((0, 0), (CONV_WIDTH - 1, 0), (0, 0)))
    y = conv_b
    for j in range(CONV_WIDTH):
        y = y + conv_w[j] * up[:, j:j + L]
    return b_gate * y

def peer_ffn(h, peer_wq, peer_subkeys, peer_u, peer_v):
    B, L, D = h.shape
    n_blocks = L // Q_BLOCK
    hb_all = h.reshape(B, n_blocks, Q_BLOCK, D).transpose(1, 0, 2, 3)

    def block_fn(hb):
        q = (hb @ peer_wq).reshape(B, Q_BLOCK, PEER_HEADS, 2, PEER_HALF)
        s = jnp.einsum('bqhpd,hpnd->bqhpn', q, peer_subkeys).astype(jnp.float32)
        vals, idx = lax.top_k(s, PEER_TOPK)
        combo = vals[..., 0, :, None] + vals[..., 1, None, :]
        ids = idx[..., 0, :, None] * PEER_KEYS + idx[..., 1, None, :]
        combo = combo.reshape(B, Q_BLOCK, PEER_HEADS, PEER_TOPK * PEER_TOPK)
        ids = ids.reshape(B, Q_BLOCK, PEER_HEADS, PEER_TOPK * PEER_TOPK)
        top_s, pos = lax.top_k(combo, PEER_TOPK)
        expert = jnp.take_along_axis(ids, pos, axis=-1)
        g = jax.nn.softmax(top_s, axis=-1).astype(hb.dtype)
        u_sel = peer_u[expert]
        a = jax.nn.gelu(jnp.einsum('bqhkd,bqd->bqhk', u_sel, hb))
        v_sel = peer_v[expert]
        return jnp.einsum('bqhk,bqhkd->bqd', g * a, v_sel)

    out = lax.map(block_fn, hb_all)
    return out.transpose(1, 0, 2, 3).reshape(B, L, D)

def first_inputs(seed: int = 0) -> dict:
    key = jax.random.key(seed)
    ks = jax.random.split(key, 20)
    f32 = jnp.float32
    nrm = lambda k, shape, s: jax.random.normal(k, shape, f32) * s
    return {
        "x": nrm(ks[0], (BATCH, SEQ, D_MODEL), 1.0),
        "c": nrm(ks[1], (BATCH, D_MODEL), 1.0),
        "norm1_w": 1.0 + nrm(ks[2], (D_MODEL,), 0.02),
        "norm2_w": 1.0 + nrm(ks[3], (D_MODEL,), 0.02),
        "w_ada": nrm(ks[4], (D_MODEL, 6 * D_MODEL), D_MODEL ** -0.5),
        "b_ada": nrm(ks[5], (6 * D_MODEL,), 0.02),
        "w_in": nrm(ks[6], (D_MODEL, D_IN), D_MODEL ** -0.5),
        "q_norm_w": 1.0 + nrm(ks[7], (HEAD_DIM,), 0.02),
        "k_norm_w": 1.0 + nrm(ks[8], (HEAD_DIM,), 0.02),
        "conv_w": nrm(ks[9], (CONV_WIDTH, D_CONV), CONV_WIDTH ** -0.5),
        "conv_b": nrm(ks[10], (D_CONV,), 0.01),
        "attn_out_norm_w": 1.0 + nrm(ks[11], (D_ATTN,), 0.02),
        "conv_out_norm_w": 1.0 + nrm(ks[12], (D_CONV,), 0.02),
        "w_out": nrm(ks[13], (D_MIX, D_MODEL), D_MIX ** -0.5),
        "peer_wq": nrm(ks[14], (D_MODEL, PEER_HEADS * PEER_QDIM), D_MODEL ** -0.5),
        "peer_subkeys": nrm(ks[15], (PEER_HEADS, 2, PEER_KEYS, PEER_HALF), PEER_HALF ** -0.5),
        "peer_u": nrm(ks[16], (PEER_EXPERTS, D_MODEL), D_MODEL ** -0.5),
        "peer_v": nrm(ks[17], (PEER_EXPERTS, D_MODEL), PEER_HEADS ** -0.5),
    }

def first_block(x, c, norm1_w, norm2_w, w_ada, b_ada, w_in, q_norm_w, k_norm_w,
              conv_w, conv_b, attn_out_norm_w, conv_out_norm_w, w_out,
              peer_wq, peer_subkeys, peer_u, peer_v):
    B, L, _ = x.shape
    mod = jax.nn.silu(c) @ w_ada + b_ada
    shift1, scale1, gate1, shift2, scale2, gate2 = [m[:, None, :] for m in jnp.split(mod, 6, axis=-1)]

    for _ in range(DEPTH):
        h = rms_norm(x, norm1_w) * (1.0 + scale1) + shift1
        proj = h @ w_in
        offs = np.cumsum(SPLITS)[:-1].tolist()
        q, k, v, cb, cc, cx, iq, ik, iw = jnp.split(proj, offs, axis=-1)
        q = rms_norm(q.reshape(B, L, ATTN_HEADS, HEAD_DIM), q_norm_w)
        k = rms_norm(k.reshape(B, L, ATTN_HEADS, HEAD_DIM), k_norm_w)
        v = v.reshape(B, L, ATTN_HEADS, HEAD_DIM)
        iq = iq.reshape(B, L, IDX_HEADS, IDX_DIM)
        y_attn = dsa_attention(q, k, v, iq, ik, iw)
        y_conv = short_conv(cb, cc, cx, conv_w, conv_b)
        y_mix = jnp.concatenate([rms_norm(y_attn, attn_out_norm_w),
                                 rms_norm(y_conv, conv_out_norm_w)], axis=-1)
        x = x + gate1 * (y_mix @ w_out)
        h2 = rms_norm(x, norm2_w) * (1.0 + scale2) + shift2
        x = x + gate2 * peer_ffn(h2, peer_wq, peer_subkeys, peer_u, peer_v)
    return x


DEPTH_2 = 2

N_Q_HEADS = 8
N_KV_HEADS = 2
ATTN_WIDTH = N_Q_HEADS * HEAD_DIM
KV_WIDTH = N_KV_HEADS * HEAD_DIM
WINDOW = 128
ATTN_BLOCK = 128
GMLP_GROUPS = 4
GMLP_GROUP_DIM = 128
GMLP_WIDTH = GMLP_GROUPS * GMLP_GROUP_DIM
CHUNK = 128
SPLITS_2 = (ATTN_WIDTH, KV_WIDTH, KV_WIDTH, ATTN_WIDTH,
          GMLP_WIDTH, GMLP_WIDTH, GMLP_WIDTH, D_MODEL, D_MODEL)
IN_WIDTH = sum(SPLITS_2)
ALPHA = (2 * DEPTH_2) ** 0.25
BETA = (8 * DEPTH_2) ** -0.25
LN_EPS = 1e-5


def layer_norm(x, g, b):
    xf = x.astype(jnp.float32)
    mu = xf.mean(-1, keepdims=True)
    var = jnp.square(xf - mu).mean(-1, keepdims=True)
    y = (xf - mu) * lax.rsqrt(var + LN_EPS)
    return (y * g.astype(jnp.float32) + b.astype(jnp.float32)).astype(x.dtype)

def alibi_slopes():
    h = jnp.arange(N_Q_HEADS, dtype=jnp.float32)
    return jnp.exp2(-8.0 * (h + 1.0) / N_Q_HEADS)

def split_columns(h):
    offs = [int(o) for o in np.cumsum(SPLITS_2)[:-1]]
    return jnp.split(h, offs, axis=-1)

def sliding_window_attention(q, k, v, sinks):
    B, S = q.shape[0], q.shape[1]
    nb = S // ATTN_BLOCK
    grp = N_Q_HEADS // N_KV_HEADS
    qb = q.reshape(B, nb, ATTN_BLOCK, N_KV_HEADS, grp, HEAD_DIM)

    def band(t):
        tb = t.reshape(B, nb, ATTN_BLOCK, N_KV_HEADS, HEAD_DIM)
        prev = jnp.pad(tb, ((0, 0), (1, 0), (0, 0), (0, 0), (0, 0)))[:, :-1]
        return jnp.concatenate([prev, tb], axis=2)

    kb, vb = band(k), band(v)
    scores = jnp.einsum('bnqhgd,bnkhd->bnhgqk', qb, kb).astype(jnp.float32) * (HEAD_DIM ** -0.5)
    qi = jnp.arange(ATTN_BLOCK)[:, None]
    kj = jnp.arange(2 * ATTN_BLOCK)[None, :]
    dist = qi + ATTN_BLOCK - kj
    blk = jnp.arange(nb)[:, None, None]
    key_pos = blk * ATTN_BLOCK + qi - dist
    valid = (dist >= 0) & (dist < WINDOW) & (key_pos >= 0)
    slopes = alibi_slopes().reshape(N_KV_HEADS, grp)
    scores = scores - slopes[:, :, None, None] * dist.astype(jnp.float32)
    scores = jnp.where(valid[None, :, None, None], scores, -jnp.inf)
    sink = sinks.astype(jnp.float32).reshape(N_KV_HEADS, grp)[None, None, :, :, None, None]
    m = jnp.maximum(scores.max(-1, keepdims=True), sink)
    p = jnp.exp(scores - m)
    denom = p.sum(-1, keepdims=True) + jnp.exp(sink - m)
    out = jnp.einsum('bnhgqk,bnkhd->bnqhgd', (p / denom).astype(v.dtype), vb)
    return out.reshape(B, S, ATTN_WIDTH)

def chunked_spatial_gating(u, v, ln_g, ln_b, w_s, b_s):
    B, S = v.shape[0], v.shape[1]
    nc = S // CHUNK
    vn = layer_norm(v, ln_g, ln_b).reshape(B, nc, CHUNK, GMLP_GROUPS, GMLP_GROUP_DIM)
    causal = jnp.tril(jnp.ones((CHUNK, CHUNK), dtype=bool))
    w = jnp.where(causal[None], w_s, jnp.zeros_like(w_s))
    mixed = jnp.einsum('gts,bcsgd->bctgd', w, vn) + b_s.T[None, None, :, :, None]
    return u * mixed.reshape(B, S, GMLP_WIDTH)

def second_inputs(seed: int = 0) -> dict:
    key = jax.random.key(seed)
    ks = jax.random.split(key, 16)
    f32 = jnp.float32
    x = jax.random.normal(ks[0], (BATCH, SEQ, D_MODEL), f32)
    w_in = jax.random.normal(ks[1], (DEPTH_2, D_MODEL, IN_WIDTH), f32) * D_MODEL ** -0.5
    b_in = jax.random.normal(ks[2], (DEPTH_2, IN_WIDTH), f32) * 0.02
    attn_sinks = jax.random.normal(ks[3], (DEPTH_2, N_Q_HEADS), f32) * 0.5
    gmlp_ln_g = 1.0 + 0.02 * jax.random.normal(ks[4], (DEPTH_2, GMLP_WIDTH), f32)
    gmlp_ln_b = 0.02 * jax.random.normal(ks[5], (DEPTH_2, GMLP_WIDTH), f32)
    w_spatial = jax.random.normal(ks[6], (DEPTH_2, GMLP_GROUPS, CHUNK, CHUNK), f32) * (0.5 * CHUNK ** -0.5)
    b_spatial = 1.0 + 0.02 * jax.random.normal(ks[7], (DEPTH_2, GMLP_GROUPS, CHUNK), f32)
    w_branch_attn = jax.random.normal(ks[8], (DEPTH_2, ATTN_WIDTH, D_MODEL), f32) * (ATTN_WIDTH ** -0.5 * BETA)
    w_branch_gmlp = jax.random.normal(ks[9], (DEPTH_2, GMLP_WIDTH, D_MODEL), f32) * (GMLP_WIDTH ** -0.5 * BETA)
    w_out = jax.random.normal(ks[10], (DEPTH_2, D_MODEL, D_MODEL), f32) * (D_MODEL ** -0.5 * BETA)
    b_out = 0.02 * jax.random.normal(ks[11], (DEPTH_2, D_MODEL), f32)
    ln_g = 1.0 + 0.02 * jax.random.normal(ks[12], (DEPTH_2, D_MODEL), f32)
    ln_b = 0.02 * jax.random.normal(ks[13], (DEPTH_2, D_MODEL), f32)
    return {"x": x, "w_in": w_in, "b_in": b_in, "attn_sinks": attn_sinks,
            "gmlp_ln_g": gmlp_ln_g, "gmlp_ln_b": gmlp_ln_b,
            "w_spatial": w_spatial, "b_spatial": b_spatial,
            "w_branch_attn": w_branch_attn, "w_branch_gmlp": w_branch_gmlp,
            "w_out": w_out, "b_out": b_out, "ln_g": ln_g, "ln_b": ln_b}

def second_block(x, w_in, b_in, attn_sinks, gmlp_ln_g, gmlp_ln_b, w_spatial, b_spatial,
              w_branch_attn, w_branch_gmlp, w_out, b_out, ln_g, ln_b):
    B, S = x.shape[0], x.shape[1]
    for l in range(DEPTH_2):
        h = jnp.einsum('bsd,de->bse', x, w_in[l]) + b_in[l]
        q, k, v, z_a, u_g, v_g, z_g, g_a, g_g = split_columns(h)
        y_a = sliding_window_attention(q.reshape(B, S, N_Q_HEADS, HEAD_DIM),
                                       k.reshape(B, S, N_KV_HEADS, HEAD_DIM),
                                       v.reshape(B, S, N_KV_HEADS, HEAD_DIM),
                                       attn_sinks[l]) * jax.nn.silu(z_a)
        y_g = chunked_spatial_gating(jax.nn.gelu(u_g, approximate=False),
                                     jax.nn.gelu(v_g, approximate=False),
                                     gmlp_ln_g[l], gmlp_ln_b[l],
                                     w_spatial[l], b_spatial[l]) * jax.nn.silu(z_g)
        br_a = jnp.einsum('bse,ed->bsd', y_a, w_branch_attn[l])
        br_g = jnp.einsum('bse,ed->bsd', y_g, w_branch_gmlp[l])
        merged = jax.nn.sigmoid(g_a) * br_a + jax.nn.sigmoid(g_g) * br_g
        out = jnp.einsum('bsd,de->bse', merged, w_out[l]) + b_out[l]
        x = layer_norm(ALPHA * x + out, ln_g[l], ln_b[l])
    return x


def setup_inputs(seed=0):
    out = dict(first_inputs(seed))
    for name, value in second_inputs(seed + 1).items():
        if name != "x":
            out[name + "_2"] = value
    return out


def reference(
    x, c, norm1_w, norm2_w, w_ada, b_ada, w_in, q_norm_w, k_norm_w, conv_w, conv_b,
    attn_out_norm_w, conv_out_norm_w, w_out, peer_wq, peer_subkeys, peer_u, peer_v, w_in_2,
    b_in_2, attn_sinks_2, gmlp_ln_g_2, gmlp_ln_b_2, w_spatial_2, b_spatial_2, w_branch_attn_2,
    w_branch_gmlp_2, w_out_2, b_out_2, ln_g_2, ln_b_2,
):
    x = first_block(
        x, c, norm1_w, norm2_w, w_ada, b_ada, w_in, q_norm_w, k_norm_w, conv_w, conv_b,
        attn_out_norm_w, conv_out_norm_w, w_out, peer_wq, peer_subkeys, peer_u, peer_v,
    )
    return second_block(
        x, w_in_2, b_in_2, attn_sinks_2, gmlp_ln_g_2, gmlp_ln_b_2, w_spatial_2, b_spatial_2,
        w_branch_attn_2, w_branch_gmlp_2, w_out_2, b_out_2, ln_g_2, ln_b_2,
    )


_drawn_inputs = setup_inputs


def setup_inputs(seed=0):
    import zlib

    import numpy as np

    out = dict(_drawn_inputs(seed))
    spreads = {}
    factors = {'norm2_w': 3.552,
     'q_norm_w': 8.0,
     'k_norm_w': 8.0,
     'conv_b': 8.0,
     'attn_out_norm_w': 4.049,
     'conv_out_norm_w': 4.512,
     'b_in_2': 8.0,
     'attn_sinks_2': 58.396,
     'gmlp_ln_g_2': 64.0,
     'gmlp_ln_b_2': 64.0,
     'b_spatial_2': 29.177,
     'b_out_2': 3.041}
    for name, (base, spread) in spreads.items():
        noise = np.random.default_rng([zlib.crc32(name.encode()), seed]).standard_normal(out[name].shape)
        drawn = base * np.exp(spread * noise) if base else spread * noise
        out[name] = __import__('jax').numpy.asarray(drawn.astype(out[name].dtype))
    for name, factor in factors.items():
        out[name] = (out[name] * factor).astype(out[name].dtype)
    return out
```

```python
from contextlib import ExitStack

import concourse.bass as bass
from concourse import mybir

ALU = mybir.AluOpType
ACT = mybir.ActivationFunctionType
AX = mybir.AxisListType.X
F32 = mybir.dt.float32
I32 = mybir.dt.int32
U32 = mybir.dt.uint32

P = 128
T = 256
NT = T // P
D = 1024
KC = D // P
HEADS, DH = 8, 64
HC = HEADS * DH // P
TOPK = 64
IDX_SCALE = (64 ** -0.5) * (8 ** -0.5)
ATT_SCALE = DH ** -0.5
EXPERT_HEADS, KEYS, PICKS = 8, 128, 16
LAYERS = 2
ALPHA = (2 * LAYERS) ** 0.25
RMS_EPS, LN_EPS = 1e-6, 1e-5
LOW = -3.0e38
MASKED = -1.0e30

RING = 4
WTILE = KC * 512
ADA_RING = 5
ADA_TILES = 6 * D // P
ROWS = 8

N1W, N2W, B_ADA, CONV_W, CONV_B, ATT_W, CNV_W, Q_W, K_W, COLS = 0, 8, 16, 64, 76, 80, 84, 88, 89, 90
BQ, BK, BUG, BZG, BZA, BGA, BGG, BOUT, LNG, LNB, LCOLS = 0, 4, 5, 9, 13, 17, 25, 33, 41, 49, 57
RV, RVG, RSP, LROWS = 0, 128, 640, 1152

TILES_1 = ["iq", "idx", "q", "k", "v", "cc", "cx", "cb", "out0", "out1", "wq0", "wq1", "wq2", "wq3", "sub"]
TILES_2 = ["q", "kv", "vg", "ug", "zg", "za", "ga0", "ga1", "gg0", "gg1",
           "ba0", "ba1", "bg0", "bg1", "out0", "out1"]
N1, N2 = len(TILES_1), len(TILES_2)
ROUTE_STEPS = 24
LAYER_STEPS = 32
assert N2 % RING == 0


def head1(h):
    return 2 * (h % 4) + h // 4


class Chain:

    def __init__(self, eng, sem, spare=None):
        self.eng, self.sem, self.base, self.n, self.spare = eng, sem, 0, 0, spare

    def mark(self, ins):
        self.n += 1
        ins.then_inc(self.sem, 1)

    def wait(self):
        self.eng.wait_ge(self.sem, self.base + self.n)
        if self.spare is not None:
            self.eng.sem_inc(self.spare)

    def link(self, ins):
        self.mark(ins)
        self.wait()

    def enter(self, i, per):
        self.start = self.base + self.n
        self.base, self.n, self.per = i * per + self.start, 0, per

    def leave(self, trips):
        assert self.n == self.per, (self.n, self.per)
        self.base, self.n, self.spare = self.start + trips * self.per, 0, None


def build(nc, a, out):
    ctx = ExitStack()
    with ctx:
        def sb(name, shape, dt=F32):
            return ctx.enter_context(nc.sbuf_tensor(name, shape, dt))

        def sem(name):
            return ctx.enter_context(nc.semaphore(name))

        wring = sb("wring", [P, RING, WTILE])
        rows = sb("rows", [P, 2 * ROWS, D])
        xT = sb("xT", [P, KC, T])
        hT = sb("hT", [P, KC, T])
        work = sb("work", [P, 8192])
        wsT = sb("wsT", [P, LAYERS * 4, P])
        lnv = sb("lnv", [P, LAYERS, 2, 512])
        brow = sb("brow", [1, LAYERS, LROWS])
        sink = sb("sink", [P, LAYERS, HEADS])
        cols = sb("cols", [P, COLS])
        lcol = sb("lcol", [P, LAYERS, LCOLS])
        mod = sb("mod", [P, 48])
        gain = sb("gain", [P, KC])
        eps = sb("eps", [P, 2])
        ident = sb("ident", [P, P])
        ones = sb("ones", [P, P])
        mean = sb("mean", [P, P])
        zeros = sb("zeros", [P, P])
        blk = sb("blk", [P, P])
        rstd = sb("rstd", [P, T])
        smax = sb("smax", [P, NT, HEADS])
        ssum = sb("ssum", [P, NT, HEADS])
        ssink = sb("ssink", [P, NT, HEADS])
        ystat = sb("ystat", [P, NT, 2])
        top8 = sb("top8", [P, 8])
        bn = sb("bn", [P, NT, 6])
        mv = sb("mv", [P, NT, 2])

        flat = rows[:, :, :].rearrange("p r d -> p (r d)")

        class Area:

            def __init__(self, ap, at=0):
                self.ap, self.at = ap, at

            def take(self, n):
                self.at += n
                assert self.at <= self.ap.shape[1]
                return self.ap[:, self.at - n:self.at]

        r1 = Area(flat)
        ada = r1.take(ADA_RING * D).rearrange("p (s d) -> p s d", s=ADA_RING)
        cbc = r1.take(D)
        sq = r1.take(KC * T).rearrange("p (c t) -> p c t", t=T)
        p_buf = [r1.take(HEADS * P), r1.take(HEADS * T)]
        pt_buf = [r1.take(HEADS * P), r1.take(HEADS * T)]
        cc = r1.take(HC * T).rearrange("p (c t) -> p c t", t=T)
        ytok = r1.take(NT * 512).rearrange("p (n f) -> p n f", n=NT)
        w1 = Area(work[:, :])
        iqT = w1.take(HC * T).rearrange("p (c t) -> p c t", t=T)
        ikT = w1.take(T)
        iw = w1.take(NT * HEADS).rearrange("p (n h) -> p n h", n=NT)
        qn = w1.take(HC * T).rearrange("p (c t) -> p c t", t=T)
        kn = w1.take(HC * T).rearrange("p (c t) -> p c t", t=T)
        v1 = w1.take(NT * 512).rearrange("p (n f) -> p n f", n=NT)
        score = [w1.take(P), w1.take(T)]
        left = [w1.take(P), w1.take(T)]
        keep = [w1.take(P), w1.take(T)]
        u = w1.take(HC * (T + 2)).rearrange("p (c t) -> p c t", t=T + 2)
        cb = w1.take(HC * T).rearrange("p (c t) -> p c t", t=T)
        yaT = iqT
        relu = p_buf
        w2 = Area(work[:, :])
        pqT = w2.take(2 * EXPERT_HEADS * T).rearrange("p (c t) -> p c t", t=T)
        s_all = w2.take(NT * EXPERT_HEADS * 2 * KEYS).rearrange("p (g k) -> p g k", k=2 * KEYS)
        w3 = Area(work[:, :])
        diag = w3.take(PICKS * P).rearrange("p (j q) -> p j q", q=P)
        s_cur = w3.take(2 * KEYS).rearrange("p (s k) -> p s k", s=2)
        s_left = w3.take(2 * KEYS).rearrange("p (s k) -> p s k", s=2)
        half_top = w3.take(2 * PICKS).rearrange("p (s k) -> p s k", s=2)
        half_idx = w3.take(2 * PICKS).bitcast(U32).rearrange("p (s k) -> p s k", s=2)
        combo = w3.take(PICKS * PICKS)
        combo_left = w3.take(PICKS * PICKS)
        top = w3.take(PICKS)
        pos = w3.take(PICKS).bitcast(U32)
        place = w3.take(2 * PICKS).bitcast(U32).rearrange("p (s k) -> p s k", s=2)
        hit = w3.take(2 * PICKS * PICKS).rearrange("p (s k n) -> p s k n", s=2, n=PICKS)
        picked = w3.take(2 * PICKS).rearrange("p (s k) -> p s k", s=2)
        expert = [w3.take(PICKS).bitcast(I32) for _ in range(2)]
        negtop = w3.take(1)
        gate = w3.take(PICKS)
        gate_sum = w3.take(1)
        gate_inv = w3.take(1)
        dots = w3.take(PICKS)
        act_dots = w3.take(PICKS)
        weight = w3.take(PICKS)
        assert w3.at <= 4096
        count16 = sb("count16", [P, PICKS], I32)
        peer_tok = rows[:, 0:NT, :]
        r4 = Area(flat)
        qT = r4.take(HC * T).rearrange("p (c t) -> p c t", t=T)
        kT = r4.take(T)
        v2 = r4.take(NT * P).rearrange("p (n f) -> p n f", n=NT)
        vg = r4.take(NT * 512).rearrange("p (n f) -> p n f", n=NT)
        p2_buf = [r4.take(HEADS * P), r4.take(HEADS * T)]
        pt2_buf = [r4.take(HEADS * P), r4.take(HEADS * T)]
        za = r4.take(HC * T).rearrange("p (c t) -> p c t", t=T)
        ug = r4.take(HC * T).rearrange("p (c t) -> p c t", t=T)
        zg = r4.take(HC * T).rearrange("p (c t) -> p c t", t=T)
        ytok2 = r4.take(NT * 512).rearrange("p (n f) -> p n f", n=NT)
        sgg = r4.take(KC * T).rearrange("p (c t) -> p c t", t=T)
        ya2T = qT
        sga = hT
        w4 = Area(work[:, :])
        xb = w4.take(KC * T).rearrange("p (c t) -> p c t", t=T)
        res = w4.take(KC * T).rearrange("p (c t) -> p c t", t=T)
        bias8 = w4.take(HEADS * T).rearrange("p (h k) -> p h k", k=T)
        sq2 = w4.take(KC * T).rearrange("p (c t) -> p c t", t=T)

        pj = ctx.enter_context(nc.psum_tensor("pj", [P, 2, 512], F32))
        aux = ctx.enter_context(nc.psum_tensor("aux", [P, 6, 512], F32))
        h2_tok = [pj[:, :, :].rearrange("p b n -> p (b n)"), aux[:, 0:2, :].rearrange("p b n -> p (b n)")]

        x_loaded, c_loaded, cols_loaded, par_loaded = sem("x_loaded"), sem("c_loaded"), sem("cols_loaded"), sem("par_loaded")
        w_loaded = [sem(f"w_loaded{s}") for s in range(RING)]
        ada_loaded = [sem(f"ada_loaded{s}") for s in range(ADA_RING)]
        ada_used = sem("ada_used")
        pool_chain, dve_chain, act_chain = sem("pool_chain"), sem("dve_chain"), sem("act_chain")
        pool_spare, dve_spare = sem("pool_spare"), sem("dve_spare")
        const_ready = sem("const_ready")
        c_silu = sem("c_silu")
        squares = sem("squares")
        sums = sem("sums")
        std_ready = sem("std_ready")
        h_ready = sem("h_ready")
        h_scaled = sem("h_scaled")
        proj = sem("proj")
        taken_act, taken_dve = sem("taken_act"), sem("taken_dve")
        idx_raw, idx_relu, idx_score, idx_causal, keep_ready = (
            sem("idx_raw"), sem("idx_relu"), sem("idx_score"), sem("idx_causal"), sem("keep_ready"))
        qk_sq, qk_sum, qk_std, qk_ready = sem("qk_sq"), sem("qk_sum"), sem("qk_std"), sem("qk_ready")
        u_ready, conv_y, conv_sq, conv_sum, conv_std, conv_done = (
            sem("u_ready"), sem("conv_y"), sem("conv_sq"), sem("conv_sum"), sem("conv_std"), sem("conv_done"))

        def at(l, per, k):
            return k if l is None else l * per + k

        names = ("logits", "negmax", "probs", "p_turned", "p_out", "summed", "y_ready",
                 "y_sq", "y_std", "y_turned", "y_done", "sink_in", "sink_exp")
        att1 = {s: sem(f"att1_{s}") for s in names}
        att2 = {s: sem(f"att2_{s}") for s in names}
        expert_scores, scores_out = sem("expert_scores"), sem("scores_out")
        h2_turned = sem("h2_turned")
        s_taken, routed, gate_exp, dots_act, diag_ready = (
            sem("s_taken"), sem("routed"), sem("gate_exp"), sem("dots_act"), sem("diag_ready"))
        u_loaded = [sem(f"u_loaded{s}") for s in range(ROWS)]
        v_loaded = [sem(f"v_loaded{s}") for s in range(ROWS)]
        u_used, v_used = sem("u_used"), sem("v_used")
        peer_out, peer_turned, x_ready = sem("peer_out"), sem("peer_turned"), sem("x_ready")
        bias_iota, bias_lin, bias_ready = sem("bias_iota"), sem("bias_lin"), sem("bias_ready")
        vn_ready, vn_std, vn_stat = sem("vn_ready"), sem("vn_std"), sem("vn_stat")
        mixed, yg_ready, gated = sem("mixed"), sem("yg_ready"), sem("gated")
        xb_ready = sem("xb_ready")
        means, centred, centred_sq, variances, ln_std, ln_scaled = (
            sem("means"), sem("centred"), sem("centred_sq"), sem("variances"), sem("ln_std"), sem("ln_scaled"))
        stored = sem("stored")

        OWN_1 = ["a"] * (4 + 2 + 4 + 4 + NT + 4 + 4 + 4) + ["d"] * 8 + ["a"] * 16
        OWN_2 = ["a"] * (4 + 1 + 1 + NT + 4 + 4 + 4 + 8 + 8) + ["d"] * 24
        M1, M2 = len(OWN_1), len(OWN_2)
        assert M1 % 2 == 0 and M2 % 2 == 0
        PER_1 = {"idx": 2, "v": NT, "sub": 0}
        PER_2 = {"kv": 2, "vg": NT}
        DONE_1 = [sum(PER_1.get(x, 4) for x in TILES_1[:n + 1]) for n in range(N1)]
        DONE_2 = [sum(PER_2.get(x, 4) for x in TILES_2[:n + 1]) for n in range(N2)]
        assert DONE_1[-1] == M1 and DONE_2[-1] == M2
        A1, D1 = OWN_1.count("a"), OWN_1.count("d")
        A2, D2 = OWN_2.count("a"), OWN_2.count("d")

        def bank_free(pe, m, l=None):
            if l is None:
                if m >= 2:
                    own = OWN_1[m - 2]
                    pe.wait_ge({"a": taken_act, "d": taken_dve}[own], OWN_1[:m - 1].count(own))
            elif m >= 2:
                own = OWN_2[m - 2]
                n = OWN_2[:m - 1].count(own)
                if own == "a":
                    pe.wait_ge(taken_act, l * A2 + A1 + n)
                else:
                    pe.wait_ge(taken_dve, l * D2 + D1 + n)

        def w_wait(eng, n, l=None):
            if l is None:
                eng.wait_ge(w_loaded[n % RING], 16 * (n // RING + 1))
            else:
                eng.wait_ge(w_loaded[(N1 + n) % RING], l * (16 * N2 // RING) + 16 * ((N1 + n) // RING + 1))

        def w_slot(n, width, l=None, chunks=KC):
            s = n % RING if l is None else (N1 + n) % RING
            return wring[:, s, 0:chunks * width].rearrange("p (k n) -> p k n", n=width)

        def q1(h, t):
            return qn[64 * (h // 4):64 * (h // 4) + 64, h % 4, t * P:(t + 1) * P]

        def k1(h, s):
            return kn[64 * (h // 4):64 * (h // 4) + 64, h % 4, 0:s]

        def q2(h, t):
            return qT[64 * (h // 4):64 * (h // 4) + 64, h % 4, t * P:(t + 1) * P]

        def k2(h, s):
            return kT[64 * (h // 4):64 * (h // 4) + 64, 0:s]

        def probs(buf, t, h):
            s = (t + 1) * P
            return buf[t][:, h * s:(h + 1) * s]

        def probs_T(buf, t, s):
            return buf[t][:, s * HEADS * P:(s + 1) * HEADS * P].rearrange("p (h q) -> p h q", q=P)

        def logit_bank(t, h):
            return aux[:, h // 4, (h % 4) * P:(h % 4 + 1) * P] if t == 0 else \
                aux[:, 2 + h // 2, (h % 2) * T:(h % 2 + 1) * T]

        block = ctx.enter_context(nc.Block())

        @block.sync
        def _(sp):
            sp.dma_start(xT[:, :, :], a["xT"].rearrange("c p t -> p c t")).then_inc(x_loaded, 16)
            width = {"idx": KC * 136, "sub": 2 * EXPERT_HEADS * KEYS}
            order = {n: i for i, n in enumerate(["iq", "q", "k", "v", "cc", "cx", "cb"])}
            for n, name in enumerate(TILES_1):
                if n >= RING:
                    sp.wait_ge(proj, DONE_1[n - RING])
                if n == 2:
                    sp.wait_ge(ada_used, 10)
                if name in order:
                    src = a["w_in"][order[name]]
                elif name == "idx":
                    src = a["w_idx"]
                elif name.startswith("out"):
                    src = a["w_out"][int(name[3:])]
                elif name.startswith("wq"):
                    src = a["wq"][int(name[2:])]
                else:
                    src = a["subkeys"]
                sp.dma_start(wring[:, n % RING, 0:width.get(name, WTILE)], src).then_inc(w_loaded[n % RING], 16)
            main = ["q", "vg", "ug", "zg", "za", "ga0", "ga1", "gg0", "gg1"]
            with sp.Fori(0, LAYERS) as l:
                for j, name in enumerate(TILES_2):
                    slot = (N1 + j) % RING
                    if j >= RING:
                        sp.wait_ge(proj, l * M2 + (M1 + DONE_2[j - RING]))
                    elif j < RING - 1:
                        sp.wait_ge(proj, l * M2 + DONE_1[N1 - RING + j])
                    else:
                        sp.wait_ge(proj, l * M2 + M1)
                        sp.wait_ge(expert_scores, NT * 4)
                    if name in main:
                        src, n = a["w_in2"][bass.ds(l, 1), main.index(name)], WTILE
                    elif name == "kv":
                        src, n = a["w_kv2"][bass.ds(l, 1), 0], KC * 256
                    elif name[0] == "b":
                        src, n = a["w_br2"][bass.ds(l, 1), 2 * (name[1] == "g") + int(name[2])], WTILE // 2
                    else:
                        src, n = a["w_out2"][bass.ds(l, 1), int(name[3:])], WTILE
                    sp.dma_start(wring[:, slot, 0:n], src.rearrange("o p n -> (o p) n")).then_inc(w_loaded[slot], 16)
            sp.wait_ge(x_ready, KC * (1 + LAYERS))
            sp.dma_start(out.rearrange("c p t -> p c t"), xT[:, :, :]).then_inc(stored, 16)
            sp.wait_ge(stored, 16)

        @block.gpsimd
        def _(pool):
            chain = Chain(pool, pool_chain)
            spare = pool_spare
            pool.memset(eps[:, 0:1], RMS_EPS).then_inc(const_ready, 1)
            pool.memset(eps[:, 1:2], LN_EPS).then_inc(const_ready, 1)
            pool.memset(ones[:, :], 1.0).then_inc(const_ready, 1)
            pool.memset(zeros[:, 0:1], 0.0).then_inc(u_used, ROWS)
            pool.memset(zeros[:, 1:], 0.0).then_inc(v_used, ROWS)

            def load_ada(n):
                if n >= ADA_RING:
                    pool.wait_ge(ada_used, n - ADA_RING + 1)
                pool.dma_start(ada[:, n % ADA_RING, :], a["w_ada"][n]) \
                    .then_inc(ada_loaded[n % ADA_RING], 16)

            for n in range(ADA_RING):
                load_ada(n)
            pool.memset(mean[:, :], 1.0 / D).then_inc(const_ready, 1)
            chain.link(pool.memset(ident[:, :], 0.0))
            pool.affine_select(out=ident[:, :], in_=ident[:, :], compare_op=ALU.not_equal, fill=1.0, base=0,
                               pattern=[[-1, P]], channel_multiplier=1).then_inc(const_ready, 1)
            chain.link(pool.memset(blk[:, :], 1.0))
            pool.affine_select(out=blk[:, 0:DH], in_=blk[:, 0:DH], compare_op=ALU.is_ge, fill=0.0, base=DH - 1,
                               pattern=[[0, DH]], channel_multiplier=-1).then_inc(const_ready, 1)
            pool.affine_select(out=blk[:, DH:], in_=blk[:, DH:], compare_op=ALU.is_ge, fill=0.0, base=-DH,
                               pattern=[[0, DH]], channel_multiplier=1).then_inc(const_ready, 1)
            pool.iota(count16[:, :], pattern=[[1, PICKS]], base=0, channel_multiplier=0).then_inc(const_ready, 1)
            pool.memset(u[:, :, 0:2], 0.0).then_inc(const_ready, 1)
            pool.wait_ge(par_loaded, 64)
            pool.affine_select(out=wsT[:, :, :], in_=wsT[:, :, :], compare_op=ALU.is_ge, fill=0.0, base=0,
                               pattern=[[0, LAYERS * 4], [1, P]], channel_multiplier=-1).then_inc(const_ready, 1)
            for n in range(ADA_RING, 5 * KC + ADA_RING):
                load_ada(n)
            for t in range(NT):
                pool.wait_ge(idx_score, t + 1)
                pool.affine_select(out=score[t], in_=score[t], compare_op=ALU.is_ge, fill=LOW, base=t * P,
                                   pattern=[[-1, (t + 1) * P]], channel_multiplier=1).then_inc(idx_causal, 1)
            base = 4 + 2 + 4 + 4 + NT
            for c in range(HC):
                pool.wait_ge(taken_act, base + 4 + c + 1)
                pool.tensor_tensor(u[:, c, 2:], u[:, c, 2:], cc[:, c, :], ALU.mult).then_inc(u_ready, 1)
            for c in range(HC):
                y, tmp = cc[:, c, :], sq[:, 4 + c, :]
                pool.wait_ge(u_ready, c + 1)
                chain.mark(pool.tensor_scalar(y, u[:, c, 2:T + 2], cols[:, CONV_W + 2 * HC + c:CONV_W + 2 * HC + c + 1],
                                              cols[:, CONV_B + c:CONV_B + c + 1], ALU.mult, ALU.add))
                for tap in (1, 0):
                    pool.wait_ge(qk_ready, 2)
                    chain.link(pool.tensor_scalar(tmp, u[:, c, tap:T + tap],
                                                  cols[:, CONV_W + tap * HC + c:CONV_W + tap * HC + c + 1], None, ALU.mult))
                    chain.link(pool.tensor_tensor(y, y, tmp, ALU.add))
                pool.wait_ge(taken_act, base + 8 + c + 1)
                pool.tensor_tensor(y, y, cb[:, c, :], ALU.mult).then_inc(conv_y, 1)
            for n in range(5 * KC + ADA_RING, ADA_TILES):
                load_ada(n)
            for t in range(NT):
                with pool.Fori(0, EXPERT_HEADS // 2) as i:
                    for par in range(2):
                        pool.wait_ge(routed, 2 * i + (t * EXPERT_HEADS + par + 1))
                        for table, dst, loaded, used in ((a["peer_u"], 0, u_loaded, u_used), (a["peer_v"], ROWS, v_loaded, v_used)):
                            for j in range(PICKS):
                                pool.wait_ge(used, i * (2 * PICKS) + ((t * EXPERT_HEADS + par) * PICKS + j + 1))
                                pool.sem_inc(spare)
                                pool.indirect_dma_start(
                                    out=rows[:, dst + j % ROWS, :], out_offset=None, in_=table,
                                    in_offset=bass.IndirectOffsetOnAxis(ap=expert[par][:, j:j + 1], axis=0)) \
                                    .then_inc(loaded[j % ROWS], 16)
            pool.wait_ge(s_taken, NT * EXPERT_HEADS)
            pool.iota(sq2[:, 0, :].bitcast(I32), pattern=[[-1, T]], base=P, channel_multiplier=1).then_inc(bias_iota, 1)
            pool.wait_ge(bias_lin, HEADS)
            chain.link(pool.affine_select(out=bias8[:, :, :], in_=bias8[:, :, :], compare_op=ALU.is_ge, fill=MASKED,
                                          base=P, pattern=[[0, HEADS], [-1, T]], channel_multiplier=1))
            pool.affine_select(out=bias8[:, :, :], in_=bias8[:, :, :], compare_op=ALU.is_ge, fill=MASKED,
                               base=-1, pattern=[[0, HEADS], [1, T]], channel_multiplier=-1).then_inc(bias_ready, 1)
            with pool.Fori(0, LAYERS) as l:
                pool.wait_ge(x_ready, l * KC + KC)
                pool.wait_ge(taken_dve, l * D2 + D1)
                pool.sem_inc(spare)
                for c in range(KC):
                    ins = pool.tensor_scalar(xb[:, c, :], xT[:, c, :], ALPHA, None, ALU.mult)
                    ins.then_inc(xb_ready, 1)

        @block.scalar
        def _(act):
            chain = Chain(act, act_chain)
            act.dma_start(cbc, a["c"].partition_broadcast(P).rearrange("p o d -> p (o d)")).then_inc(c_loaded, 16)
            act.dma_start(cols[:, :], a["cols"]).then_inc(cols_loaded, 16)
            act.dma_start(wsT[:, :, :], a["wsT"].rearrange("g s t -> s g t")).then_inc(par_loaded, 16)
            act.dma_start(lnv[:, :, :, :].rearrange("p l k f -> p (l k f)"),
                          a["lnv"].partition_broadcast(P).rearrange("p o d -> p (o d)")).then_inc(par_loaded, 16)
            act.dma_start(brow[:, :, :].rearrange("o l n -> o (l n)"), a["brow"]).then_inc(par_loaded, 16)
            act.dma_start(sink[:, :, :].rearrange("p l h -> p (l h)"),
                          a["sink"].partition_broadcast(P).rearrange("p o d -> p (o d)")).then_inc(par_loaded, 16)
            act.dma_start(lcol[:, :, :], a["lcol"]).then_inc(cols_loaded, 16)
            act.wait_ge(c_loaded, 16)
            nc.scalar.activation(cbc, cbc, ACT.Silu).then_inc(c_silu, 1)

            act.wait_ge(x_loaded, 16)
            for c in range(KC):
                nc.scalar.activation(sq[:, c, :], xT[:, c, :], ACT.Square).then_inc(squares, 1)
            act.wait_ge(const_ready, 2)
            act.wait_ge(sums, 1)
            nc.scalar.activation(rstd[:, :], aux[:, 0, 0:T], ACT.Sqrt, bias=eps[:, 0:1], scale=1.0 / D).then_inc(std_ready, 1)
            for c in range(KC):
                act.wait_ge(h_scaled, c + 1)
                nc.scalar.activation(hT[:, c, :], hT[:, c, :], ACT.Identity, bias=mod[:, c:c + 1]).then_inc(h_ready, 1)

            taken = [0]

            def take(dst, func=ACT.Copy, l=None, cols_=slice(0, T), sq_to=None, **kw):
                m = taken[0]
                taken[0] += 1
                if l is None:
                    act.wait_ge(proj, m + 1)
                else:
                    act.wait_ge(proj, l * M2 + (M1 + m + 1))
                if sq_to is not None:
                    nc.scalar.activation(sq_to, pj[:, m % 2, cols_], ACT.Square).then_inc(qk_sq, 1)
                nc.scalar.activation(dst, pj[:, m % 2, cols_], func, **kw).then_inc(taken_act, 1)

            for c in range(4):
                take(iqT[:, c, :])
            take(ikT)
            take(iw[:, :, :].rearrange("p n h -> p (n h)"), cols_=slice(0, NT * HEADS))
            for b in range(6):
                act.wait_ge(idx_raw, b + 1)
                dst = relu[0][:, b * 512:(b + 1) * 512] if b < 2 else relu[1][:, (b - 2) * 512:(b - 1) * 512]
                nc.scalar.activation(dst, aux[:, b, :], ACT.Relu).then_inc(idx_relu, 1)
            for c in range(4):
                take(qn[:, c, :], sq_to=sq[:, c, :])
            for c in range(4):
                take(kn[:, c, :], sq_to=sq[:, 4 + c, :])

            def qk_root(n):
                for b in range(2):
                    act.wait_ge(qk_sum, 2 * n + b + 1)
                    nc.scalar.activation(sq[:, 4 * n + 2 * b:4 * n + 2 * b + 2, :].rearrange("p c t -> p (c t)"),
                                         aux[:, 2 * n + b, :], ACT.Sqrt, bias=eps[:, 0:1], scale=1.0 / DH).then_inc(qk_std, 1)

            qk_root(0)
            for t in range(NT):
                take(v1[:, t, :], cols_=slice(0, 512))
            qk_root(1)
            for c in range(4):
                take(cc[:, c, :])
            def exps(s, buf, t, l=None):
                act.wait_ge(s["negmax"], at(l, NT, t + 1))
                for h in range(HEADS):
                    nc.scalar.activation(probs(buf, t, h), probs(buf, t, h), ACT.Exp, bias=smax[:, t, h:h + 1],
                                         accum_out=ssum[:, t, h:h + 1]).then_inc(s["probs"], 1)

            def p_out(s, buf, t, l=None):
                for k in range(t + 1):
                    for hh in range(2):
                        b = 2 * t + 2 * k + hh
                        act.wait_ge(s["p_turned"], at(l, 6, b + 1))
                        nc.scalar.copy(probs_T(buf, t, k)[:, 4 * hh:4 * hh + 4, :].rearrange("p h q -> p (h q)"), aux[:, b, :]) \
                            .then_inc(s["p_out"], 1)

            for t in range(NT):
                for c in range(2):
                    take(u[:, 2 * t + c, 2:T + 2])
                exps(att1, p_buf, t)
            for t in range(NT):
                p_out(att1, pt_buf, t)
            for c in range(4):
                take(cb[:, c, :])
            for t in range(NT):
                act.wait_ge(att1["y_sq"], t + 1)
                nc.scalar.activation(ystat[:, t, 1:2], ystat[:, t, 0:1], ACT.Sqrt, bias=eps[:, 0:1], scale=1.0 / 512) \
                    .then_inc(att1["y_std"], 1)
            for t in range(NT):
                act.wait_ge(att1["y_turned"], t + 1)
                for c in range(HC):
                    nc.scalar.activation(yaT[:, c, t * P:(t + 1) * P], aux[:, 2 + t, c * P:(c + 1) * P], ACT.Copy,
                                         scale=cols[:, ATT_W + c:ATT_W + c + 1]).then_inc(att1["y_done"], 1)
            for c in range(HC):
                act.wait_ge(conv_y, c + 1)
                nc.scalar.activation(sq[:, c, :], cc[:, c, :], ACT.Square).then_inc(conv_sq, 1)
            act.wait_ge(conv_sum, 1)
            nc.scalar.activation(rstd[:, :], aux[:, 4, 0:T], ACT.Sqrt, bias=eps[:, 0:1], scale=1.0 / 512).then_inc(conv_std, 1)
            taken[0] += 8
            for c in range(KC):
                act.wait_ge(taken_dve, c + 1)
                nc.scalar.activation(sq[:, c, :], xT[:, c, :], ACT.Square).then_inc(squares, 1)
            act.wait_ge(sums, 2)
            nc.scalar.activation(rstd[:, :], aux[:, 5, 0:T], ACT.Sqrt, bias=eps[:, 0:1], scale=1.0 / D).then_inc(std_ready, 1)
            for c in range(KC):
                act.wait_ge(h_scaled, KC + c + 1)
                nc.scalar.activation(hT[:, c, :], hT[:, c, :], ACT.Identity, bias=mod[:, 3 * KC + c:3 * KC + c + 1]).then_inc(h_ready, 1)
            for c in range(2 * EXPERT_HEADS):
                take(pqT[:, c, :])
            for n in range(NT * 4):
                act.wait_ge(expert_scores, n + 1)
                nc.scalar.copy(s_all[:, 2 * n:2 * n + 2, :].rearrange("p g k -> p (g k)"), aux[:, 4 + n % 2, :]).then_inc(scores_out, 1)

            for t in range(NT):
                with act.Fori(0, EXPERT_HEADS // 2) as i:
                    for par in range(2):
                        g = t * EXPERT_HEADS + par
                        act.wait_ge(scores_out, NT * 4)
                        nc.scalar.copy(s_cur[:, :, :].rearrange("p s k -> p (s k)"),
                                       s_all[:, bass.ds(2 * i + g, 1), :].rearrange("p o k -> p (o k)")).then_inc(s_taken, 1)
                        act.wait_ge(routed, 2 * i + (g + 1))
                        nc.scalar.activation(gate, top, ACT.Exp, bias=negtop, accum_out=gate_sum).then_inc(gate_exp, 1)
                        act.wait_ge(u_used, i * (2 * PICKS) + ((g + 1) * PICKS + ROWS))
                        nc.scalar.activation(act_dots, dots, ACT.Gelu_apprx_tanh).then_inc(dots_act, 1)
            for t in range(NT):
                act.wait_ge(v_used, (t + 1) * EXPERT_HEADS * PICKS + ROWS)
                act.wait_ge(u_used, NT * EXPERT_HEADS * PICKS + ROWS)
                for b in range(2):
                    nc.scalar.copy(peer_tok[:, t, b * 512:(b + 1) * 512], aux[:, 2 + 2 * t + b, :]).then_inc(peer_out, 1)

            with act.Fori(0, LAYERS) as l:
                taken[0] = 0

                def col(n):
                    return lcol[:, bass.ds(l, 1), n:n + 1].rearrange("p o n -> p (o n)")

                for c in range(4):
                    take(qT[:, c, :], ACT.Identity, l, bias=col(BQ + c))
                take(kT, ACT.Identity, l, bias=col(BK))
                take(v2[:, :, :].rearrange("p n f -> p (n f)"), ACT.Copy, l)
                for t in range(NT):
                    take(vg[:, t, :], ACT.Gelu, l, cols_=slice(0, 512))
                for t in range(NT):
                    for c in range(2):
                        take(ug[:, 2 * t + c, :], ACT.Gelu, l, bias=col(BUG + 2 * t + c))
                    exps(att2, p2_buf, t, l)
                    act.wait_ge(att2["sink_in"], l * NT + (t + 1))
                    nc.scalar.activation(ssink[:, t, :], ssink[:, t, :], ACT.Exp).then_inc(att2["sink_exp"], 1)
                for t in range(NT):
                    act.wait_ge(vn_stat, l * NT + (t + 1))
                    nc.scalar.activation(mv[:, t, 1:2], mv[:, t, 1:2], ACT.Sqrt, bias=eps[:, 1:2]).then_inc(vn_std, 1)
                for c in range(4):
                    take(zg[:, c, :], ACT.Silu, l, bias=col(BZG + c))
                for t in range(NT):
                    p_out(att2, pt2_buf, t, l)
                for c in range(4):
                    take(za[:, c, :], ACT.Silu, l, bias=col(BZA + c))
                for c in range(KC):
                    take(sga[:, c, :], ACT.Sigmoid, l, bias=col(BGA + c))
                for c in range(KC):
                    take(sgg[:, c, :], ACT.Sigmoid, l, bias=col(BGG + c))
                for c in range(KC):
                    act.wait_ge(centred, l * KC + (c + 1))
                    nc.scalar.activation(sq2[:, c, :], res[:, c, :], ACT.Square).then_inc(centred_sq, 1)
                act.wait_ge(variances, l + 1)
                nc.scalar.activation(rstd[:, :], aux[:, 1, 0:T], ACT.Sqrt, bias=eps[:, 1:2]).then_inc(ln_std, 1)
                for c in range(KC):
                    act.wait_ge(ln_scaled, l * KC + (c + 1))
                    nc.scalar.activation(xT[:, c, :], res[:, c, :], ACT.Identity, bias=col(LNB + c)).then_inc(x_ready, 1)

        @block.tensor
        def _(pe):
            mm = nc.tensor.matmul
            chunk = [0]

            tile = [0]

            def next_tile(width, l=None, chunks=KC):
                n = tile[0]
                tile[0] += 1
                w_wait(pe, n, l)
                return w_slot(n, width, l, chunks)

            def x_of(src):
                return lambda k: src[:, k, :]

            def whole(src, n, width=512, l=None, chunks=KC):
                w = next_tile(width, l, chunks)
                for j in range(n):
                    m = chunk[0]
                    chunk[0] += 1
                    bank_free(pe, m, l)
                    for k in range(chunks):
                        ins = mm(pj[:, m % 2, 0:T], w[:, k, j * P:(j + 1) * P], src(k), start=(k == 0), stop=(k == chunks - 1))
                    ins.then_inc(proj, 1)

            pe.wait_ge(const_ready, 7)
            pe.wait_ge(squares, KC)
            for c in range(KC):
                ins = mm(aux[:, 0, 0:T], ones[:, :], sq[:, c, :], start=(c == 0), stop=(c == KC - 1))
            ins.then_inc(sums, 1)
            pe.wait_ge(h_ready, KC)
            whole(x_of(hT), 4)
            w = next_tile(136)
            m = chunk[0]
            chunk[0] += 2
            bank_free(pe, m)
            for k in range(KC):
                ins = mm(pj[:, m % 2, 0:T], w[:, k, 0:P], hT[:, k, :], start=(k == 0), stop=(k == KC - 1))
            ins.then_inc(proj, 1)
            bank_free(pe, m + 1)
            for t in range(NT):
                for k in range(KC):
                    ins = mm(pj[:, (m + 1) % 2, t * HEADS:(t + 1) * HEADS], hT[:, k, t * P:(t + 1) * P], w[:, k, P:136],
                             start=(k == 0), stop=(k == KC - 1))
            ins.then_inc(proj, 1)
            pe.wait_ge(taken_act, 5)
            for t in range(NT):
                for h in range(HEADS):
                    r = slice(64 * (h // 4), 64 * (h // 4) + 64)
                    ins = mm(logit_bank(t, h), iqT[r, h % 4, t * P:(t + 1) * P], ikT[r, 0:(t + 1) * P], start=True, stop=True)
                    if h % (4 >> t) == (4 >> t) - 1:
                        ins.then_inc(idx_raw, 1)
            whole(x_of(hT), 4)
            whole(x_of(hT), 4)

            def qk_sums(n):
                pe.wait_ge(qk_sq, 4 * n + 4)
                pe.wait_ge(idx_relu, 2 + 2 * n)
                for b in range(2):
                    mm(aux[:, 2 * n + b, :], blk[:, :], sq[:, 4 * n + 2 * b:4 * n + 2 * b + 2, :].rearrange("p c t -> p (c t)"),
                       start=True, stop=True).then_inc(qk_sum, 1)

            qk_sums(0)
            w = next_tile(512)
            for t in range(NT):
                m = chunk[0]
                chunk[0] += 1
                bank_free(pe, m)
                for k in range(KC):
                    ins = mm(pj[:, m % 2, :], hT[:, k, t * P:(t + 1) * P], w[:, k, :], start=(k == 0), stop=(k == KC - 1))
                ins.then_inc(proj, 1)
            qk_sums(1)
            whole(x_of(hT), 4)

            def logits(s, q, k, l=None):
                for t in range(NT):
                    for h in range(HEADS):
                        ins = mm(logit_bank(t, h), q(h, t), k(h, (t + 1) * P), start=True, stop=True)
                        if h % (4 >> t) == (4 >> t) - 1:
                            ins.then_inc(s["logits"], 1)

            def turn_p(s, buf, l=None):
                for t in range(NT):
                    pe.wait_ge(s["probs"], at(l, NT * HEADS, (t + 1) * HEADS))
                    for k in range(t + 1):
                        for h in range(HEADS):
                            b = 2 * t + 2 * k + h // 4
                            ins = nc.tensor.transpose(aux[:, b, (h % 4) * P:(h % 4 + 1) * P], probs(buf, t, h)[:, k * P:(k + 1) * P], ident[:, :])
                            if h % 4 == 3:
                                ins.then_inc(s["p_turned"], 1)

            def sum_v(s, buf, v, l=None):
                for t in range(NT):
                    pe.wait_ge(s["p_out"], at(l, 6, 2 if t == 0 else 6))
                    for h in range(HEADS):
                        for k in range(t + 1):
                            ins = mm(aux[:, t, h * DH:(h + 1) * DH], probs_T(buf, t, k)[:, h, :], v(h, k), start=(k == 0), stop=(k == t))
                    ins.then_inc(s["summed"], 1)

            def turn_y(s, y, l=None):
                for t in range(NT):
                    pe.wait_ge(s["y_ready"], at(l, NT, t + 1))
                    for c in range(HC):
                        ins = nc.tensor.transpose(aux[:, 2 + t, c * P:(c + 1) * P], y[:, t, c * P:(c + 1) * P], ident[:, :])
                    ins.then_inc(s["y_turned"], 1)

            pe.wait_ge(qk_ready, 2)
            pe.wait_ge(idx_relu, 6)
            pe.wait_ge(qk_std, 4)
            logits(att1, q1, k1)
            whole(x_of(hT), 4)
            turn_p(att1, p_buf)
            whole(x_of(hT), 4)
            sum_v(att1, pt_buf, lambda h, k: v1[:, k, head1(h) * DH:(head1(h) + 1) * DH])
            turn_y(att1, ytok)
            pe.wait_ge(conv_sq, HC)
            for c in range(HC):
                ins = mm(aux[:, 4, 0:T], ones[:, :], sq[:, c, :], start=(c == 0), stop=(c == HC - 1))
            ins.then_inc(conv_sum, 1)
            pe.wait_ge(att1["y_done"], NT * HC)
            pe.wait_ge(conv_done, HC)
            for n in range(2):
                whole(lambda k: yaT[:, k, :] if k < HC else cc[:, k - HC, :], 4)
            pe.wait_ge(squares, 2 * KC)
            for c in range(KC):
                ins = mm(aux[:, 5, 0:T], ones[:, :], sq[:, c, :], start=(c == 0), stop=(c == KC - 1))
            ins.then_inc(sums, 1)
            pe.wait_ge(h_ready, 2 * KC)
            for n in range(4):
                whole(x_of(hT), 4)
            w = next_tile(KEYS, chunks=2 * EXPERT_HEADS)
            pe.wait_ge(taken_act, A1)
            for t in range(NT):
                for n in range(4):
                    i = 4 * t + n
                    if i >= 2:
                        pe.wait_ge(scores_out, i - 1)
                    for j in range(4):
                        hp = 4 * n + j
                        ins = mm(aux[:, 4 + i % 2, j * KEYS:(j + 1) * KEYS], pqT[:, hp, t * P:(t + 1) * P], w[:, hp, :], start=True, stop=True)
                    ins.then_inc(expert_scores, 1)
            pe.wait_ge(scores_out, NT * 4)
            for t in range(NT):
                for c in range(KC):
                    ins = nc.tensor.transpose(h2_tok[t][:, c * P:(c + 1) * P], hT[:, c, t * P:(t + 1) * P], ident[:, :])
                ins.then_inc(h2_turned, 1)
            for t in range(NT):
                for b in range(2):
                    mm(aux[:, 2 + 2 * t + b, :], zeros[:, :], hT[:, 0:2, :].rearrange("p c t -> p (c t)"),
                       start=True, stop=False, skip_group_check=True)
                with pe.Fori(0, EXPERT_HEADS // 2) as i:
                    for par in range(2):
                        g = t * EXPERT_HEADS + par
                        pe.wait_ge(diag_ready, 2 * i + (g + 1))
                        for j in range(PICKS):
                            pe.wait_ge(v_loaded[j % ROWS], i * 64 + 16 * (2 * g + j // ROWS + 1))
                            for b in range(2):
                                ins = mm(aux[:, 2 + 2 * t + b, :], diag[:, j, :], rows[:, ROWS + j % ROWS, b * 512:(b + 1) * 512],
                                         start=False, stop=False, skip_group_check=True)
                            ins.then_inc(v_used, 1)
            for t in range(NT):
                pe.wait_ge(peer_out, 2 * t + 2)
                for b in range(2):
                    for c in range(4):
                        ins = nc.tensor.transpose(aux[:, b, c * P:(c + 1) * P] if t == 0 else pj[:, b, c * P:(c + 1) * P],
                                                  peer_tok[:, t, (4 * b + c) * P:(4 * b + c + 1) * P], ident[:, :])
                    ins.then_inc(peer_turned, 1)

            with pe.Fori(0, LAYERS) as l:
                chunk[0], tile[0] = 0, 0
                pe.wait_ge(x_ready, l * KC + KC)
                pe.wait_ge(const_ready, 10)

                def bias_row(n, width):
                    return brow[:, bass.ds(l, 1), n:n + width].rearrange("o l n -> o (l n)")

                whole(x_of(xT), 4, l=l)
                w = next_tile(256, l)
                m = chunk[0]
                chunk[0] += 2
                bank_free(pe, m, l)
                for k in range(KC):
                    ins = mm(pj[:, m % 2, 0:T], w[:, k, 0:P], xT[:, k, :], start=(k == 0), stop=(k == KC - 1))
                ins.then_inc(proj, 1)
                bank_free(pe, m + 1, l)
                for t in range(NT):
                    for k in range(KC):
                        mm(pj[:, (m + 1) % 2, t * P:(t + 1) * P], xT[:, k, t * P:(t + 1) * P], w[:, k, P:2 * P], start=(k == 0), stop=False)
                    ins = mm(pj[:, (m + 1) % 2, t * P:(t + 1) * P], ones[0:1, :], bias_row(RV, P), start=False, stop=True)
                ins.then_inc(proj, 1)
                w = next_tile(512, l)
                for t in range(NT):
                    m = chunk[0]
                    chunk[0] += 1
                    bank_free(pe, m, l)
                    for k in range(KC):
                        mm(pj[:, m % 2, :], xT[:, k, t * P:(t + 1) * P], w[:, k, :], start=(k == 0), stop=False)
                    mm(pj[:, m % 2, :], ones[0:1, :], bias_row(RVG, 512), start=False, stop=True).then_inc(proj, 1)
                pe.wait_ge(taken_act, l * A2 + (A1 + 6))
                logits(att2, q2, k2, l)
                whole(x_of(xT), 4, l=l)
                whole(x_of(xT), 4, l=l)
                turn_p(att2, p2_buf, l)
                whole(x_of(xT), 4, l=l)
                sum_v(att2, pt2_buf, lambda h, k: v2[:, k, (h // 4) * DH:(h // 4 + 1) * DH], l)
                for n in range(2):
                    whole(x_of(xT), 4, l=l)
                turn_y(att2, ytok2, l)
                for t in range(NT):
                    pe.wait_ge(vn_ready, l * NT + (t + 1))
                    for g in range(4):
                        o = aux[:, 4 + t, g * P:(g + 1) * P]
                        mm(o, vg[:, t, g * P:(g + 1) * P], wsT[:, bass.ds(l * 4 + g, 1), :].rearrange("p o t -> p (o t)"), start=True, stop=False)
                        ins = mm(o, ones[0:1, :], bias_row(RSP + g * P, P), start=False, stop=True)
                    ins.then_inc(mixed, 1)
                for n in range(2):
                    whole(x_of(xT), 4, l=l)
                pe.wait_ge(att2["y_done"], l * NT + NT)
                for n in range(2):
                    whole(x_of(ya2T), 4, l=l, chunks=HC)
                pe.wait_ge(yg_ready, l * NT + NT)
                for n in range(2):
                    whole(x_of(ug), 4, l=l, chunks=HC)
                pe.wait_ge(gated, l * KC + KC)
                for n in range(2):
                    whole(x_of(sga), 4, l=l)
                pe.wait_ge(taken_dve, l * D2 + (D1 + 3 * KC))
                for c in range(KC):
                    ins = mm(aux[:, 0, 0:T], mean[:, :], res[:, c, :], start=(c == 0), stop=(c == KC - 1))
                ins.then_inc(means, 1)
                pe.wait_ge(centred_sq, l * KC + KC)
                for c in range(KC):
                    ins = mm(aux[:, 1, 0:T], mean[:, :], sq2[:, c, :], start=(c == 0), stop=(c == KC - 1))
                ins.then_inc(variances, 1)

        @block.vector
        def _(dve):
            v = nc.vector
            spare = dve_spare
            chain = Chain(dve, dve_chain)

            def ada_tiles(lo, hi):
                for n in range(lo, hi):
                    dve.wait_ge(ada_loaded[n % ADA_RING], 16 * (n // ADA_RING + 1))
                    tile = ada[:, n % ADA_RING, :]
                    v.tensor_tensor_reduce(tile, tile, cbc, 1.0, 0.0, ALU.mult, ALU.add, mod[:, n:n + 1]).then_inc(ada_used, 1)
                dve.wait_ge(ada_used, hi)
                chain.link(v.tensor_tensor(mod[:, lo:hi], mod[:, lo:hi], cols[:, B_ADA + lo:B_ADA + hi], ALU.add))

            def part(n):
                return mod[:, n * KC:(n + 1) * KC]

            def norm(n, weight, scale):
                chain.link(v.tensor_scalar(gain[:, :], part(scale), 1.0, None, ALU.add))
                chain.link(v.tensor_tensor(gain[:, :], gain[:, :], cols[:, weight:weight + KC], ALU.mult))
                dve.wait_ge(std_ready, n + 1)
                chain.link(v.reciprocal(rstd[:, :], rstd[:, :]))
                for c in range(KC):
                    v.scalar_tensor_tensor(hT[:, c, :], xT[:, c, :], gain[:, c:c + 1], rstd[:, :], ALU.mult, ALU.mult).then_inc(h_scaled, 1)

            dve.wait_ge(c_silu, 1)
            dve.wait_ge(cols_loaded, 32)
            ada_tiles(0, 2 * KC)
            dve.wait_ge(x_loaded, 16)
            norm(0, N1W, 1)
            ada_tiles(2 * KC, 5 * KC)

            dve.wait_ge(taken_act, 6)
            for t in range(NT):
                for h in range(HEADS):
                    dve.wait_ge(idx_relu, 2 * t + h // (4 >> t) + 1)
                    w, r = iw[:, t, head1(h):head1(h) + 1], probs(relu, t, h)
                    if h == 0:
                        chain.link(v.tensor_scalar(score[t], r, w, None, ALU.mult))
                    else:
                        chain.link(v.scalar_tensor_tensor(score[t], r, w, score[t], ALU.mult, ALU.add))
                v.tensor_scalar(score[t], score[t], IDX_SCALE, None, ALU.mult).then_inc(idx_score, 1)
            for t in range(NT):
                dve.wait_ge(idx_causal, t + 1)
                for n in range(TOPK // 8):
                    src = score[t] if n == 0 else left[t]
                    chain.link(v.max(top8[:, :], src))
                    chain.link(v.match_replace(left[t], top8[:, :], src, LOW))
                chain.link(v.tensor_tensor(keep[t], score[t], left[t], ALU.is_gt))
                v.tensor_scalar(keep[t], keep[t], 1.0, -MASKED, ALU.subtract, ALU.mult).then_inc(keep_ready, 1)
            for n, (z, w) in enumerate(((qn, Q_W), (kn, K_W))):
                dve.wait_ge(qk_std, 2 * n + 2)
                r = sq[:, 4 * n:4 * n + 4, :].rearrange("p c t -> p (c t)")
                z = z.rearrange("p c t -> p (c t)")
                chain.link(v.reciprocal(r, r))
                v.scalar_tensor_tensor(z, z, cols[:, w:w + 1], r, ALU.mult, ALU.mult).then_inc(qk_ready, 1)

            def mask_logits(s, buf, bias, t, l=None):
                for h in range(HEADS):
                    dve.wait_ge(s["logits"], at(l, 6, 2 * t + h // (4 >> t) + 1))
                    if l is not None:
                        dve.sem_inc(spare)
                    chain.mark(v.tensor_tensor_reduce(probs(buf, t, h), logit_bank(t, h), bias(t, h), ATT_SCALE, LOW,
                                                      ALU.add, ALU.max, smax[:, t, h:h + 1]))
                chain.wait()

            dve.wait_ge(keep_ready, 2)
            for t in range(NT):
                mask_logits(att1, p_buf, lambda t, h: keep[t], t)
                v.tensor_scalar(smax[:, t, :], smax[:, t, :], -1.0, None, ALU.mult).then_inc(att1["negmax"], 1)

            def over_sums(s, y, t, l=None):
                chain.link(v.reciprocal(ssum[:, t, :], ssum[:, t, :]))
                dve.wait_ge(s["summed"], at(l, NT, t + 1))
                return v.tensor_tensor(y[:, t, :].rearrange("p (h d) -> p h d", d=DH),
                                       aux[:, t, :].rearrange("p (h d) -> p h d", d=DH),
                                       ssum[:, t, :].unsqueeze(2).broadcast_to([P, HEADS, DH]), ALU.mult)

            for t in range(NT):
                dve.wait_ge(att1["probs"], (t + 1) * HEADS)
                chain.link(over_sums(att1, ytok, t))
                v.tensor_tensor_reduce(p_buf[t][:, 0:512], ytok[:, t, :], ytok[:, t, :], 1.0, 0.0, ALU.mult, ALU.add,
                                       ystat[:, t, 0:1]).then_inc(att1["y_sq"], 1)
            for t in range(NT):
                dve.wait_ge(att1["y_std"], t + 1)
                chain.link(v.reciprocal(ystat[:, t, 1:2], ystat[:, t, 1:2]))
                v.tensor_scalar(ytok[:, t, :], ytok[:, t, :], ystat[:, t, 1:2], None, ALU.mult).then_inc(att1["y_ready"], 1)
            dve.wait_ge(conv_std, 1)
            chain.link(v.reciprocal(rstd[:, :], rstd[:, :]))
            for c in range(HC):
                v.scalar_tensor_tensor(cc[:, c, :], cc[:, c, :], cols[:, CNV_W + c:CNV_W + c + 1], rstd[:, :], ALU.mult, ALU.mult) \
                    .then_inc(conv_done, 1)
            for c in range(KC):
                m = M1 - 2 * EXPERT_HEADS - KC + c
                dve.wait_ge(proj, m + 1)
                v.scalar_tensor_tensor(xT[:, c, :], pj[:, m % 2, 0:T], mod[:, 2 * KC + c:2 * KC + c + 1], xT[:, c, :], ALU.mult, ALU.add) \
                    .then_inc(taken_dve, 1)
            dve.wait_ge(taken_dve, KC)
            norm(1, N2W, 4)
            ada_tiles(5 * KC, 6 * KC)

            def flat2(ap):
                return ap.rearrange("p s k -> p (s k)")

            def top16(src, rest, values, index):
                for half in range(2):
                    hs = slice(8 * half, 8 * half + 8)
                    cur = src if half == 0 else rest
                    chain.link(v.max(values[:, hs], cur))
                    chain.mark(v.max_index(index[:, hs], values[:, hs], cur))
                    if half == 0:
                        chain.mark(v.match_replace(rest, values[:, hs], cur, LOW))
                    chain.wait()

            def route(par, i, g):
                dve.wait_ge(s_taken, 2 * i + (g + 1))
                dve.sem_inc(spare)
                for s in range(2):
                    top16(s_cur[:, s, :], s_left[:, s, :], half_top[:, s, :], half_idx[:, s, :])
                chain.link(v.tensor_tensor(combo.rearrange("p (k n) -> p k n", n=PICKS),
                                           half_top[:, 0, :].unsqueeze(2).broadcast_to([P, PICKS, PICKS]),
                                           half_top[:, 1, :].unsqueeze(1).broadcast_to([P, PICKS, PICKS]), ALU.add))
                top16(combo, combo_left, top, pos)
                chain.mark(v.tensor_scalar(negtop, top[:, 0:1], -1.0, None, ALU.mult))
                chain.mark(v.tensor_scalar(place[:, 0, :], pos, 4, None, ALU.logical_shift_right))
                chain.link(v.tensor_scalar(place[:, 1, :], pos, PICKS - 1, None, ALU.bitwise_and))
                rows_ = hit.rearrange("p s k n -> p (s k) n")
                chain.link(v.tensor_tensor(rows_, count16[:, :].unsqueeze(1).broadcast_to([P, 2 * PICKS, PICKS]),
                                           flat2(place).unsqueeze(2).broadcast_to([P, 2 * PICKS, PICKS]), ALU.is_equal))
                chain.link(v.tensor_tensor(hit, hit, half_idx.unsqueeze(2).broadcast_to([P, 2, PICKS, PICKS]), ALU.mult))
                chain.link(v.tensor_reduce(flat2(picked), rows_, AX, ALU.add))
                v.scalar_tensor_tensor(expert[par], picked[:, 0, :], float(KEYS), picked[:, 1, :], ALU.mult, ALU.add).then_inc(routed, 1)

            for t in range(NT):
                dve.wait_ge(h2_turned, t + 1)
                with dve.Fori(0, EXPERT_HEADS // 2) as i:
                    chain.enter(i, 2 * ROUTE_STEPS)
                    chain.spare = spare
                    for par in range(2):
                        g = t * EXPERT_HEADS + par
                        route(par, i, g)
                        for j in range(PICKS):
                            dve.wait_ge(u_loaded[j % ROWS], i * 64 + 16 * (2 * g + j // ROWS + 1))
                            row = rows[:, j % ROWS, :]
                            v.tensor_tensor_reduce(row, row, h2_tok[t], 1.0, 0.0, ALU.mult, ALU.add, dots[:, j:j + 1]).then_inc(u_used, 1)
                        dve.wait_ge(gate_exp, 2 * i + (g + 1))
                        chain.link(v.reciprocal(gate_inv, gate_sum))
                        dve.wait_ge(dots_act, 2 * i + (g + 1))
                        chain.link(v.scalar_tensor_tensor(weight, act_dots, gate_inv, gate, ALU.mult, ALU.mult))
                        dve.wait_ge(v_used, i * (2 * PICKS) + (g * PICKS + ROWS))
                        v.tensor_tensor(diag, ident[:, :].unsqueeze(1).broadcast_to([P, PICKS, P]),
                                        weight.unsqueeze(2).broadcast_to([P, PICKS, P]), ALU.mult).then_inc(diag_ready, 1)
                chain.leave(EXPERT_HEADS // 2)
            dve.wait_ge(bias_iota, 1)
            for h in range(HEADS):
                v.tensor_scalar(bias8[:, h, :], sq2[:, 0, :].bitcast(I32), -(2.0 ** -(h + 1)) / ATT_SCALE, None, ALU.mult).then_inc(bias_lin, 1)
            for b in range(2):
                for j in range(4):
                    c = 4 * b + j
                    for t in range(NT):
                        dve.wait_ge(peer_turned, 2 * t + b + 1)
                        bank = aux if t == 0 else pj
                        x = xT[:, c, t * P:(t + 1) * P]
                        ins = v.scalar_tensor_tensor(x, bank[:, b, j * P:(j + 1) * P], mod[:, 5 * KC + c:5 * KC + c + 1], x, ALU.mult, ALU.add)
                        if t == 0:
                            chain.mark(ins)
                    ins.then_inc(x_ready, 1)
            dve.wait_ge(bias_ready, 1)

            with dve.Fori(0, LAYERS) as l:
                chain.enter(l, LAYER_STEPS)
                chain.spare = spare

                def taken(n):
                    dve.wait_ge(taken_act, l * A2 + (A1 + n))

                def col(n):
                    return lcol[:, bass.ds(l, 1), n:n + 1].rearrange("p o n -> p (o n)")

                for t in range(NT):
                    taken(6 + t + 1)
                    chain.link(v.bn_stats(bn[:, t, :], vg[:, t, :]))
                    v.bn_aggr(mv[:, t, :], bn[:, t, :]).then_inc(vn_stat, 1)
                for t in range(NT):
                    mask_logits(att2, p2_buf, lambda t, h: bias8[:, h, (NT - 1 - t) * P:], t, l)
                    sk = sink[:, bass.ds(l, 1), :].rearrange("p o h -> p (o h)")
                    chain.link(v.tensor_tensor(smax[:, t, :], smax[:, t, :], sk, ALU.max))
                    v.tensor_scalar(smax[:, t, :], smax[:, t, :], -1.0, None, ALU.mult).then_inc(att2["negmax"], 1)
                    dve.wait_ge(att2["negmax"], l * NT + (t + 1))
                    v.tensor_tensor(ssink[:, t, :], smax[:, t, :], sk, ALU.add).then_inc(att2["sink_in"], 1)
                for t in range(NT):
                    dve.wait_ge(vn_std, l * NT + (t + 1))
                    chain.link(v.reciprocal(mv[:, t, 1:2], mv[:, t, 1:2]))
                    chain.link(v.tensor_scalar(vg[:, t, :], vg[:, t, :], mv[:, t, 0:1], mv[:, t, 1:2], ALU.subtract, ALU.mult))
                    chain.link(v.tensor_tensor(vg[:, t, :], vg[:, t, :], lnv[:, bass.ds(l, 1), 0, :].rearrange("p o f -> p (o f)"), ALU.mult))
                    v.tensor_tensor(vg[:, t, :], vg[:, t, :], lnv[:, bass.ds(l, 1), 1, :].rearrange("p o f -> p (o f)"), ALU.add) \
                        .then_inc(vn_ready, 1)
                for t in range(NT):
                    dve.wait_ge(att2["sink_exp"], l * NT + (t + 1))
                    chain.link(v.tensor_tensor(ssum[:, t, :], ssum[:, t, :], ssink[:, t, :], ALU.add))
                    over_sums(att2, ytok2, t, l).then_inc(att2["y_ready"], 1)
                taken(8 + 8)
                chain.link(v.tensor_tensor(ug.rearrange("p c t -> p (c t)"), ug.rearrange("p c t -> p (c t)"), zg.rearrange("p c t -> p (c t)"), ALU.mult))
                taken(8 + 12)
                for t in range(NT):
                    ts = slice(t * P, (t + 1) * P)
                    dve.wait_ge(att2["y_turned"], l * NT + (t + 1))
                    v.tensor_tensor(ya2T[:, :, ts], aux[:, 2 + t, :].rearrange("p (c q) -> p c q", q=P), za[:, :, ts], ALU.mult) \
                        .then_inc(att2["y_done"], 1)
                for t in range(NT):
                    ts = slice(t * P, (t + 1) * P)
                    dve.wait_ge(mixed, l * NT + (t + 1))
                    v.tensor_tensor(ug[:, :, ts], aux[:, 4 + t, :].rearrange("p (c q) -> p c q", q=P), ug[:, :, ts], ALU.mult) \
                        .then_inc(yg_ready, 1)
                taken(A2)
                for c in range(2 * KC):
                    m = A2 + c
                    dve.wait_ge(proj, l * M2 + (M1 + m + 1))
                    gate_ = (sga if c < KC else sgg)[:, c % KC, :]
                    v.tensor_tensor(gate_, pj[:, m % 2, 0:T], gate_, ALU.mult).then_inc(taken_dve, 1)
                    if c >= KC:
                        dve.wait_ge(taken_dve, l * D2 + (D1 + c + 1))
                        v.tensor_tensor(sga[:, c % KC, :], sga[:, c % KC, :], gate_, ALU.add).then_inc(gated, 1)
                for c in range(KC):
                    m = A2 + 2 * KC + c
                    dve.wait_ge(xb_ready, l * KC + (c + 1))
                    dve.wait_ge(proj, l * M2 + (M1 + m + 1))
                    v.scalar_tensor_tensor(res[:, c, :], pj[:, m % 2, 0:T], col(BOUT + c), xb[:, c, :], ALU.add, ALU.add).then_inc(taken_dve, 1)
                dve.wait_ge(means, l + 1)
                for c in range(KC):
                    v.tensor_tensor(res[:, c, :], res[:, c, :], aux[:, 0, 0:T], ALU.subtract).then_inc(centred, 1)
                dve.wait_ge(ln_std, l + 1)
                chain.link(v.reciprocal(rstd[:, :], rstd[:, :]))
                for c in range(KC):
                    v.scalar_tensor_tensor(res[:, c, :], res[:, c, :], col(LNG + c), rstd[:, :], ALU.mult, ALU.mult).then_inc(ln_scaled, 1)
            chain.leave(LAYERS)


def kernel(**inputs):
    import numpy as np
    import concourse.bacc as bacc
    from concourse.bass_utils import run_bass_kernel_spmd

    x = {k: np.ascontiguousarray(z) for k, z in inputs.items()}

    def tiles(w, width=512):
        k, n = w.shape
        return w.reshape(k // P, P, n // width, width).transpose(2, 1, 0, 3).reshape(n // width, P, -1)

    def col(z):
        return z.reshape(-1, P).T

    w_in = x["w_in"]
    part = {n: w_in[:, 512 * i:512 * i + 512] for i, n in enumerate(["q", "k", "v", "cb", "cc", "cx", "iq"])}
    ik, iw = w_in[:, 3584:3648], w_in[:, 3648:3656]
    w2, b2 = x["w_in_2"], x["b_in_2"]
    order = np.concatenate([np.arange(64) + 64 * h for c in range(4) for h in (c, c + 4)])
    order1 = np.concatenate([np.arange(DH) + DH * head1(h) for h in range(HEADS)])
    at2 = dict(k=512, v=640, za=768, ug=1280, vg=1792, zg=2304, ga=2816, gg=3840, end=4864)

    def cut(z, n, width):
        return z[..., at2[n]:at2[n] + width]

    arrays = {
        "xT": x["x"][0].T.reshape(KC, P, T),
        "c": x["c"],
        "w_ada": x["w_ada"].T.reshape(ADA_TILES, P, D),
        "w_in": np.concatenate([tiles(part[n]) for n in ("iq", "q", "k", "v", "cc", "cx", "cb")]),
        "w_idx": tiles(np.concatenate([ik, ik, iw], 1), 136)[0],
        "w_out": tiles(np.concatenate([x["w_out"][:512][order1], x["w_out"][512:]])),
        "wq": tiles(x["peer_wq"]),
        "subkeys": x["peer_subkeys"].reshape(2 * EXPERT_HEADS, KEYS, P).transpose(2, 0, 1).reshape(P, -1),
        "peer_u": x["peer_u"],
        "peer_v": x["peer_v"],
        "cols": np.concatenate([col(x["norm1_w"]), col(x["norm2_w"]), col(x["b_ada"]), col(x["conv_w"].reshape(-1)), col(x["conv_b"]),
                                col(x["attn_out_norm_w"][order1]), col(x["conv_out_norm_w"]),
                                col(np.concatenate([x["q_norm_w"]] * 2)), col(np.concatenate([x["k_norm_w"]] * 2))], 1),
        "w_in2": np.stack([np.concatenate([tiles(w2[l][:, order]), tiles(cut(w2[l], "vg", 512)), tiles(cut(w2[l], "ug", 512)),
                                           tiles(cut(w2[l], "zg", 512)), tiles(cut(w2[l], "za", 512)),
                                           tiles(cut(w2[l], "ga", D)), tiles(cut(w2[l], "gg", D))]) for l in range(LAYERS)]),
        "w_kv2": np.stack([tiles(w2[l][:, 512:768], 256) for l in range(LAYERS)]),
        "w_br2": np.stack([np.concatenate([tiles(x["w_branch_attn_2"][l]), tiles(x["w_branch_gmlp_2"][l])]) for l in range(LAYERS)]),
        "w_out2": np.stack([tiles(x["w_out_2"][l]) for l in range(LAYERS)]),
        "wsT": x["w_spatial_2"].reshape(LAYERS * 4, P, P).transpose(0, 2, 1),
        "lnv": np.stack([x["gmlp_ln_g_2"], x["gmlp_ln_b_2"]], 1).reshape(1, -1),
        "brow": np.concatenate([cut(b2, "v", 128), cut(b2, "vg", 512), x["b_spatial_2"].reshape(LAYERS, -1)], 1).reshape(1, -1),
        "sink": x["attn_sinks_2"].reshape(1, -1),
        "lcol": np.stack([np.concatenate([col(z) for z in (b2[l][order], b2[l][512:640], cut(b2[l], "ug", 512), cut(b2[l], "zg", 512),
                                                           cut(b2[l], "za", 512), cut(b2[l], "ga", D), cut(b2[l], "gg", D),
                                                           x["b_out_2"][l], x["ln_g_2"][l], x["ln_b_2"][l])], 1)
                          for l in range(LAYERS)], 1),
    }
    nc = bacc.Bacc("TRN2", target_bir_lowering=False, num_devices=1)
    aps = {}
    for name, z in arrays.items():
        arrays[name] = z = np.ascontiguousarray(z)
        aps[name] = nc.dram_tensor("in_" + name, z.shape, mybir.dt.from_np(z.dtype), kind="ExternalInput").ap()
    out = nc.dram_tensor("out_T", (KC, P, T), F32, kind="ExternalOutput").ap()
    build(nc, aps, out)
    done = run_bass_kernel_spmd(nc, [{"in_" + n: z for n, z in arrays.items()}], core_ids=[0])
    return done.results[0]["out_T"].reshape(D, T).T.reshape(1, T, D)
```

```python
from collections import namedtuple
from contextlib import ExitStack

import concourse.bass as bass
from concourse import mybir

ALU = mybir.AluOpType
ACT = mybir.ActivationFunctionType
AX = mybir.AxisListType.X
F32 = mybir.dt.float32
F32R = mybir.dt.float32r
I32 = mybir.dt.int32
U32 = mybir.dt.uint32

P = 128
T = 256
NT = T // P
D = 1024
KC = D // P
HEADS, DH = 8, 64
HC = HEADS * DH // P
TOPK = 64
IDX_SCALE = (64 ** -0.5) * (8 ** -0.5)
ATT_SCALE = DH ** -0.5
EXPERT_HEADS, KEYS, PICKS = 8, 128, 16
LAYERS = 2
ALPHA = (2 * LAYERS) ** 0.25
RMS_EPS, LN_EPS = 1e-6, 1e-5
LOW = -3.0e38
MASKED = -1.0e30

RING = 4
PRING = 4
WUNIT = KC * 256
WPIECE = KC * P
ADA_RING = 5
ADA_TILES = 6 * D // P
ROWS = 8

N1W, N2W, B_ADA, CONV_W, CONV_B, ATT_W, CNV_W, Q_W, K_W, COLS = 0, 8, 16, 64, 76, 80, 84, 88, 89, 90
BQ, BK, BUG, BZG, BZA, BGA, BGG, BOUT, LNG, LNB, LCOLS = 0, 4, 5, 9, 13, 17, 25, 33, 41, 49, 57
RV, RVG, RSP, LROWS = 0, 128, 640, 1152

def halves(name, n=512, chunks=KC, width=256):
    return [(name, at, min(width, n - at), chunks) for at in range(0, n, width)]


UNITS_1 = halves("iq") + [("idx", 0, 136, KC)]
for name in ("q", "k", "v", "cc", "cx", "cb"):
    UNITS_1 += halves(name)
UNITS_1 += halves("out", D)
MIX_UNITS = len(UNITS_1)
for h in range(0, EXPERT_HEADS, 2):
    UNITS_1 += [("sub", h * 2 * KEYS, 4 * KEYS, 1), ("wq", h * 256, 256, KC), ("wq", h * 256 + 256, 256, KC)]
UNITS_2 = halves("q") + [("k", 0, P, KC), ("v", 0, P, KC)] + halves("vg") + halves("ug") + halves("zg") + halves("za") + \
    halves("ga", D) + halves("gg", D) + halves("ba", D, HC) + halves("bg", D, HC) + halves("out", D)
N1, N2 = len(UNITS_1), len(UNITS_2)
Piece = namedtuple("Piece", "unit column chunks place")


def pieces(units):
    out, place = [], 0
    for n, (name, at, width, chunks) in enumerate(units):
        for j in range(width // P):
            out.append(Piece(n, j * P, chunks, place))
            place += 1
        place += name == "idx"
    return out, -(-place // PRING) * PRING


ADA_AFTER = {3: range(16, 21), 6: (21, 22), 7: (23, 24), 8: (25, 26), 9: (27, 28), 18: range(29, 45), 22: range(45, 48)}
PIECES_1, SPAN_1 = pieces(UNITS_1[:MIX_UNITS])
PIECES_2, SPAN_2 = pieces(UNITS_2)
LO_1 = "p" * 21 + "d" * 16
HI_2 = "p" * 4 + "a" * 10 + "p" * 8 + "a" * 40
LO_2 = "d" * 38 + "p" * 20 + "d" * 4
assert len(LO_1) == len(PIECES_1) and len(LO_2) == len(PIECES_2)


def starts(units):
    at = [0]
    for _, _, width, chunks in units:
        at.append(at[-1] + width * chunks)
    return at


AT_1, AT_2 = starts(UNITS_1), starts(UNITS_2)
EARLY_HEADS = (4, 6, 8)
ROUTE_STEPS = 24
LAYER_STEPS = 32
assert N2 % RING == 0


def head1(h):
    return 2 * (h % 4) + h // 4


class Chain:

    def __init__(self, eng, sem, spare=None):
        self.eng, self.sem, self.base, self.n, self.spare = eng, sem, 0, 0, spare

    def mark(self, ins):
        self.n += 1
        ins.then_inc(self.sem, 1)

    def wait(self, back=0):
        self.eng.wait_ge(self.sem, self.base + self.n - back)
        if self.spare is not None:
            self.eng.sem_inc(self.spare)

    def link(self, ins):
        self.mark(ins)
        self.wait()

    def enter(self, i, per):
        self.start = self.base + self.n
        self.base, self.n, self.per = i * per + self.start, 0, per

    def leave(self, trips):
        assert self.n == self.per, (self.n, self.per)
        self.base, self.n, self.spare = self.start + trips * self.per, 0, None


def build(nc, a, out):
    ctx = ExitStack()
    with ctx:
        def sb(name, shape, dt=F32):
            return ctx.enter_context(nc.sbuf_tensor(name, shape, dt))

        def sem(name):
            return ctx.enter_context(nc.semaphore(name))

        wring = sb("wring", [P, RING, WUNIT])
        whi = sb("whi", [P, PRING, WPIECE], F32R)
        wlo = sb("wlo", [P, PRING, WPIECE], F32R)
        xh = sb("xh", [P, KC, T], F32R)
        xl = sb("xl", [P, KC, T], F32R)
        rows = sb("rows", [P, 2 * ROWS, D])
        xT = sb("xT", [P, KC, T])
        hT = sb("hT", [P, KC, T])
        work = sb("work", [P, 8192])
        wsT = sb("wsT", [P, LAYERS * 4, P])
        pq = sb("pq", [P, 2, 2, T])
        sink = sb("sink", [P, LAYERS, HEADS])
        cols = sb("cols", [P, COLS])
        lcol = sb("lcol", [P, LAYERS, LCOLS])
        mod = sb("mod", [P, 48])
        gain = sb("gain", [P, KC])
        eps = sb("eps", [P, 2])
        ident = sb("ident", [P, P])
        ones = sb("ones", [P, P])
        mean = sb("mean", [P, P])
        zeros = sb("zeros", [P, P])
        blk = sb("blk", [P, P])
        rstd = sb("rstd", [P, T])
        smax = sb("smax", [P, NT, HEADS])
        ssum = sb("ssum", [P, NT, HEADS])
        ssink = sb("ssink", [P, NT, HEADS])
        warm = sb("warm", [P, 1])
        ystat = sb("ystat", [P, NT, 2])
        top8 = sb("top8", [P, NT, 8])
        bn = sb("bn", [P, NT, 6])
        mv = sb("mv", [P, NT, 2])

        flat = rows[:, :, :].rearrange("p r d -> p (r d)")

        class Area:

            def __init__(self, ap, at=0):
                self.ap, self.at = ap, at

            def take(self, n):
                self.at += n
                assert self.at <= self.ap.shape[1]
                return self.ap[:, self.at - n:self.at]

        r1 = Area(flat)
        ada = r1.take(ADA_RING * D).rearrange("p (s d) -> p s d", s=ADA_RING)
        cbc = r1.take(D)
        sq = r1.take(KC * T).rearrange("p (c t) -> p c t", t=T)
        p_buf = [r1.take(HEADS * P), r1.take(HEADS * T)]
        pt_buf = [r1.take(HEADS * P), r1.take(HEADS * T)]
        cc = r1.take(HC * T).rearrange("p (c t) -> p c t", t=T)
        ytok = r1.take(NT * 512).rearrange("p (n f) -> p n f", n=NT)
        w1 = Area(work[:, :])
        iqT = w1.take(HC * T).rearrange("p (c t) -> p c t", t=T)
        ikT = w1.take(T)
        iw = w1.take(NT * HEADS).rearrange("p (n h) -> p n h", n=NT)
        qn = w1.take(HC * T).rearrange("p (c t) -> p c t", t=T)
        kn = w1.take(HC * T).rearrange("p (c t) -> p c t", t=T)
        v1 = w1.take(NT * 512).rearrange("p (n f) -> p n f", n=NT)
        score = [w1.take(P), w1.take(T)]
        left = [w1.take(P), w1.take(T)]
        keep = [w1.take(P), w1.take(T)]
        u = w1.take(HC * (T + 2)).rearrange("p (c t) -> p c t", t=T + 2)
        cb = w1.take(HC * T).rearrange("p (c t) -> p c t", t=T)
        yaT = iqT
        relu = p_buf
        w2 = Area(work[:, :])
        w2.take(4096)
        s_all = w2.take(NT * EXPERT_HEADS * 2 * KEYS).rearrange("p (g k) -> p g k", k=2 * KEYS)
        w3 = Area(work[:, :])
        diag = w3.take(PICKS * P).rearrange("p (j q) -> p j q", q=P)
        s_cur = w3.take(2 * KEYS).rearrange("p (s k) -> p s k", s=2)
        s_left = w3.take(2 * KEYS).rearrange("p (s k) -> p s k", s=2)
        half_top = w3.take(2 * PICKS).rearrange("p (s k) -> p s k", s=2)
        half_idx = w3.take(2 * PICKS).bitcast(U32).rearrange("p (s k) -> p s k", s=2)
        combo = w3.take(PICKS * PICKS)
        combo_left = w3.take(PICKS * PICKS)
        top = w3.take(PICKS)
        pos = w3.take(PICKS).bitcast(U32)
        place = w3.take(2 * PICKS).bitcast(U32).rearrange("p (s k) -> p s k", s=2)
        hit = w3.take(2 * PICKS * PICKS).rearrange("p (s k n) -> p s k n", s=2, n=PICKS)
        picked = w3.take(2 * PICKS).rearrange("p (s k) -> p s k", s=2)
        expert = [w3.take(PICKS).bitcast(I32) for _ in range(2)]
        negtop = w3.take(1)
        gate = w3.take(PICKS)
        gate_sum = w3.take(1)
        gate_inv = w3.take(1)
        dots = w3.take(PICKS)
        act_dots = w3.take(PICKS)
        weight = w3.take(PICKS)
        assert w3.at <= 4096
        count16 = sb("count16", [P, PICKS], I32)
        peer_tok = pq[:, :, :, :].rearrange("p h s t -> p (h s t)")
        r4 = Area(flat)
        qT = r4.take(HC * T).rearrange("p (c t) -> p c t", t=T)
        kT = r4.take(T)
        v2 = r4.take(NT * P).rearrange("p (n f) -> p n f", n=NT)
        vg = r4.take(NT * 512).rearrange("p (n f) -> p n f", n=NT)
        p2 = r4.take(HEADS * (P + T))
        p2_buf = [p2[:, 0:HEADS * P], p2[:, HEADS * P:]]
        pt2 = r4.take(HEADS * (P + T))
        pt2_buf = [pt2[:, 0:HEADS * P], pt2[:, HEADS * P:]]
        za = r4.take(HC * T).rearrange("p (c t) -> p c t", t=T)
        ug = r4.take(HC * T).rearrange("p (c t) -> p c t", t=T)
        zg = r4.take(HC * T).rearrange("p (c t) -> p c t", t=T)
        ytok2 = r4.take(NT * 512).rearrange("p (n f) -> p n f", n=NT)
        sgg = p2[:, 0:KC * T].rearrange("p (c t) -> p c t", t=T)
        brow = r4.take(LAYERS * LROWS)[0:1].rearrange("o (l n) -> o l n", l=LAYERS)
        ya2T = qT
        sga = hT
        w4 = Area(work[:, :])
        xb = w4.take(KC * T).rearrange("p (c t) -> p c t", t=T)
        res = w4.take(KC * T).rearrange("p (c t) -> p c t", t=T)
        bias8 = w4.take(HEADS * T).rearrange("p (h k) -> p h k", k=T)
        sq2 = pt2[:, 0:KC * T].rearrange("p (c t) -> p c t", t=T)
        lnv = w4.take(LAYERS * 2 * 512).rearrange("p (l k f) -> p l k f", l=LAYERS, k=2)
        distance = rstd[:, :].bitcast(I32)

        def full(ap):
            return ap.bitcast(F32)

        pj = ctx.enter_context(nc.psum_tensor("pj", [P, 2, 512], F32))
        aux = ctx.enter_context(nc.psum_tensor("aux", [P, 6, 512], F32))
        h2_tok = [pj[:, :, :].rearrange("p b n -> p (b n)"), aux[:, 0:2, :].rearrange("p b n -> p (b n)")]

        x_loaded, c_loaded, cols_loaded, par_loaded = sem("x_loaded"), sem("c_loaded"), sem("cols_loaded"), sem("par_loaded")
        w_loaded = [sem(f"w_loaded{s}") for s in range(RING)]
        ada_loaded = [sem(f"ada_loaded{s}") for s in range(ADA_RING)]
        ada_used = sem("ada_used")
        pool_chain, dve_chain, act_chain = sem("pool_chain"), sem("dve_chain"), sem("act_chain")
        pool_spare, dve_spare = sem("pool_spare"), sem("dve_spare")
        const_ready = sem("const_ready")
        c_silu = sem("c_silu")
        squares = sem("squares")
        sums = sem("sums")
        std_ready = sem("std_ready")
        h_ready = sem("h_ready")
        h_scaled = sem("h_scaled")
        proj = sem("proj")
        w_hi = {"a": sem("w_hi_act"), "p": sem("w_hi_pool")}
        w_lo = {"d": sem("w_lo_dve"), "p": sem("w_lo_pool")}
        h_split, mix_hi, mix_split = sem("h_split"), sem("mix_hi"), sem("mix_split")
        xh_ready, x_split = sem("xh_ready"), sem("x_split")
        y_hi, y_split, merged_hi, merged_split = sem("y_hi"), sem("y_split"), sem("merged_hi"), sem("merged_split")
        taken_act, taken_dve = sem("taken_act"), sem("taken_dve")
        idx_raw, idx_relu, idx_score, idx_causal, keep_ready = (
            sem("idx_raw"), sem("idx_relu"), sem("idx_score"), sem("idx_causal"), sem("keep_ready"))
        qk_sq, qk_sum, qk_std, qk_ready = sem("qk_sq"), sem("qk_sum"), sem("qk_std"), sem("qk_ready")
        u_ready, conv_y, conv_sq, conv_sum, conv_std, conv_done = (
            sem("u_ready"), sem("conv_y"), sem("conv_sq"), sem("conv_sum"), sem("conv_std"), sem("conv_done"))

        def at(l, per, k):
            return k if l is None else l * per + k

        names = ("logits", "negmax", "probs", "p_turned", "p_out", "summed", "y_ready",
                 "y_sq", "y_std", "y_turned", "y_done", "sink_in", "sink_exp")
        att1 = {s: sem(f"att1_{s}") for s in names}
        att2 = {s: sem(f"att2_{s}") for s in names}
        queries, queries_out = sem("queries"), sem("queries_out")
        expert_scores, scores_out = sem("expert_scores"), sem("scores_out")
        late_loaded = sem("late_loaded")
        h2_turned = sem("h2_turned")
        s_taken, routed, gate_exp, dots_act, diag_ready = (
            sem("s_taken"), sem("routed"), sem("gate_exp"), sem("dots_act"), sem("diag_ready"))
        u_loaded = [sem(f"u_loaded{s}") for s in range(ROWS)]
        v_loaded = [sem(f"v_loaded{s}") for s in range(ROWS)]
        u_used, v_used = sem("u_used"), sem("v_used")
        peer_out, peer_turned, x_ready = sem("peer_out"), sem("peer_turned"), sem("x_ready")
        bias_iota, bias_lin, bias_ready = sem("bias_iota"), sem("bias_lin"), sem("bias_ready")
        vn_ready, vn_std, vn_stat = sem("vn_ready"), sem("vn_std"), sem("vn_stat")
        mixed, yg_ready, gated = sem("mixed"), sem("yg_ready"), sem("gated")
        xb_ready = sem("xb_ready")
        means, centred, centred_sq, variances, ln_std, ln_scaled = (
            sem("means"), sem("centred"), sem("centred_sq"), sem("variances"), sem("ln_std"), sem("ln_scaled"))
        stored = sem("stored")

        BANKS_1 = [2] * 2 + [1] * 2 + [2] * 4 + [1] * NT + [2] * 6 + [2] * 4
        BANKS_2 = [2] * 2 + [1] * 2 + [1] * NT + [2] * 6 + [2] * 8 + [2] * 12
        OWN_1 = ["a"] * (4 + 2 + 4 + 4 + NT + 4 + 4 + 4) + ["d"] * 8
        OWN_2 = ["a"] * (4 + 1 + 1 + NT + 4 + 4 + 4 + 8 + 8) + ["d"] * 24
        M1, M2 = len(OWN_1), len(OWN_2)
        assert len(BANKS_1) % 2 == 0 and len(BANKS_2) % 2 == 0

        def seats(banks):
            out, m = [], 0
            for b, n in enumerate(banks):
                out += [(b, j, m, m + n) for j in range(n)]
                m += n
            return out

        SEATS_1, SEATS_2 = seats(BANKS_1), seats(BANKS_2)
        assert len(SEATS_1) == M1 and len(SEATS_2) == M2

        def chunk_out(m, l=None, width=T):
            b, j, _, _ = (SEATS_1 if l is None else SEATS_2)[m]
            return pj[:, b % 2, j * T:j * T + width]

        def chunk_wait(eng, m, l=None):
            if l is None:
                eng.wait_ge(proj, SEATS_1[m][3])
            else:
                eng.wait_ge(proj, l * M2 + (M1 + SEATS_2[m][3]))

        def done(units, token_major):
            n, out = 0, []
            for name, at, width, _ in units:
                for j in range(width // P):
                    if name not in token_major:
                        n += 1
                        out.append(n)
                    else:
                        n += NT if at and j == 0 else 0
                        out.append(n if at else n + 1)
                n += name == "idx"
            return out

        DONE_1 = done(UNITS_1[:MIX_UNITS], ("v",))
        DONE_2 = done(UNITS_2, ("vg",))
        assert DONE_1[-1] == M1 and DONE_2[-1] == M2
        A1, D1 = OWN_1.count("a"), OWN_1.count("d")
        A2, D2 = OWN_2.count("a"), OWN_2.count("d")

        def bank_free(pe, m, l=None):
            own, at_ = (OWN_1, SEATS_1) if l is None else (OWN_2, SEATS_2)
            b, j, first, _ = at_[m]
            if j == 0 and b >= 2:
                last = at_[first - 1][2]
                who = own[last - 1]
                n = own[:last].count(who)
                taken_ = {"a": taken_act, "d": taken_dve}[who]
                if l is None:
                    pe.wait_ge(taken_, n)
                else:
                    pe.wait_ge(taken_, l * {"a": A2, "d": D2}[who] + {"a": A1, "d": D1}[who] + n)

        def w_wait(eng, n, l=None):
            if l is None:
                eng.wait_ge(w_loaded[n % RING], 16 * (n // RING + 1))
            else:
                eng.wait_ge(w_loaded[(N1 + n) % RING], l * (16 * N2 // RING) + 16 * ((N1 + n) // RING + 1))

        def w_slot(n, l=None):
            _, _, width, chunks = (UNITS_1 if l is None else UNITS_2)[n]
            s = n % RING if l is None else (N1 + n) % RING
            return wring[:, s, 0:chunks * width].rearrange("p (k n) -> p k n", n=width)

        def parts(n, l=None):
            piece = (PIECES_1 if l is None else PIECES_2)[n]
            return [z[:, piece.place % PRING, 0:piece.chunks * P].rearrange("p (k n) -> p k n", n=P) for z in (whi, wlo)]

        def part_pairs(n):
            def at_(k, l):
                s = (PIECES_1 if l is None else PIECES_2)[n].place % PRING
                return [z[:, s:s + 2, k * P:(k + 1) * P] for z in (whi, wlo)]
            return at_

        def piece_of_unit(n, l=None):
            piece = (PIECES_1 if l is None else PIECES_2)[n]
            return w_slot(piece.unit, l)[:, :, piece.column:piece.column + P]

        def split_hi(eng, n, l=None):
            plan, span = (PIECES_1, 0) if l is None else (PIECES_2, SPAN_2)
            if plan[n].column == 0:
                w_wait(eng, plan[n].unit, l)
            before = [k for k, z in enumerate(plan) if z.place <= plan[n].place - PRING]
            if before:
                if l is None:
                    eng.wait_ge(proj, DONE_1[before[-1]])
                else:
                    eng.wait_ge(proj, l * M2 + (M1 + DONE_2[before[-1]]))
            elif l is not None:
                last = [k for k, z in enumerate(plan) if z.place <= plan[n].place - PRING + span][-1]
                eng.wait_ge(proj, l * M2 + (M1 + DONE_2[last] - M2))
            if l is None or HI_2[n] == "a":
                nc.scalar.copy(parts(n, l)[0], piece_of_unit(n, l)).then_inc(w_hi["a"], 1)
            else:
                eng.sem_inc(pool_spare)
                eng.tensor_copy(parts(n, l)[0], piece_of_unit(n, l)).then_inc(w_hi["p"], 1)

        def split_lo(eng, who, n, l=None):
            assert (LO_1 if l is None else LO_2)[n] == who
            if l is None:
                eng.wait_ge(w_hi["a"], n + 1)
            else:
                by = HI_2[n]
                eng.wait_ge(w_hi[by], l * HI_2.count(by) + ((len(LO_1) if by == "a" else 0) + HI_2[:n + 1].count(by)))
            hi, lo = parts(n, l)
            eng.tensor_tensor(lo, piece_of_unit(n, l), full(hi), ALU.subtract).then_inc(w_lo[who], 1)

        def split_wait(eng, n, l=None):
            if l is None:
                eng.wait_ge(w_lo[LO_1[n]], LO_1[:n + 1].count(LO_1[n]))
            else:
                who = LO_2[n]
                eng.wait_ge(w_lo[who], l * LO_2.count(who) + (LO_1.count(who) + LO_2[:n + 1].count(who)))

        def last_piece(u, plan):
            return max(n for n, z in enumerate(plan) if z.unit == u)

        def q1(h, t):
            return qn[64 * (h // 4):64 * (h // 4) + 64, h % 4, t * P:(t + 1) * P]

        def k1(h, s):
            return kn[64 * (h // 4):64 * (h // 4) + 64, h % 4, 0:s]

        def q2(h, t):
            return qT[64 * (h // 4):64 * (h // 4) + 64, h % 4, t * P:(t + 1) * P]

        def k2(h, s):
            return kT[64 * (h // 4):64 * (h // 4) + 64, 0:s]

        def probs(buf, t, h):
            s = (t + 1) * P
            return buf[t][:, h * s:(h + 1) * s]

        def probs_T(buf, t, s):
            return buf[t][:, s * HEADS * P:(s + 1) * HEADS * P].rearrange("p (h q) -> p h q", q=P)

        def logit_bank(t, h):
            return aux[:, h // 4, (h % 4) * P:(h % 4 + 1) * P] if t == 0 else \
                aux[:, 2 + h // 2, (h % 2) * T:(h % 2 + 1) * T]

        block = ctx.enter_context(nc.Block())

        @block.sync
        def _(sp):
            sp.dma_start(xT[:, :, :], a["xT"].rearrange("c p t -> p c t")).then_inc(x_loaded, 16)

            def load_ada(n):
                if n >= ADA_RING:
                    sp.wait_ge(ada_used, n - ADA_RING + 1)
                sp.dma_start(ada[:, n % ADA_RING, :], a["w_ada"][n]).then_inc(ada_loaded[n % ADA_RING], 16)

            for n in range(2 * KC):
                load_ada(n)
            for n, (name, at, width, chunks) in enumerate(UNITS_1):
                if n >= RING:
                    was = n - RING
                    if was < MIX_UNITS:
                        split_wait(sp, last_piece(was, PIECES_1))
                        if UNITS_1[was][0] == "idx":
                            sp.wait_ge(proj, DONE_1[last_piece(was, PIECES_1)] + 1)
                    elif UNITS_1[was][0] == "wq":
                        sp.wait_ge(queries, UNITS_1[was][1] // P + 2)
                    else:
                        sp.wait_ge(expert_scores, UNITS_1[was][1] // (2 * KEYS) + 2)
                sp.dma_start(wring[:, n % RING, 0:width * chunks], a["w1"][:, AT_1[n]:AT_1[n + 1]]).then_inc(w_loaded[n % RING], 16)
                for k in ADA_AFTER.get(n, ()):
                    load_ada(k)
            sp.wait_ge(queries, 2 * EXPERT_HEADS)
            sp.wait_ge(expert_scores, EXPERT_HEADS)
            with sp.Fori(0, LAYERS) as l:
                for n, (name, at, width, chunks) in enumerate(UNITS_2):
                    slot = (N1 + n) % RING
                    if n >= RING:
                        split_wait(sp, last_piece(n - RING, PIECES_2), l)
                    else:
                        k = last_piece(n - RING + N2, PIECES_2)
                        who = LO_2[k]
                        sp.wait_ge(w_lo[who], l * LO_2.count(who) + (LO_1.count(who) - LO_2[k + 1:].count(who)))
                    sp.dma_start(wring[:, slot, 0:width * chunks],
                                 a["w2"][bass.ds(l, 1), :, AT_2[n]:AT_2[n + 1]].rearrange("o p n -> (o p) n")).then_inc(w_loaded[slot], 16)
            sp.wait_ge(x_ready, KC * (1 + LAYERS))
            sp.dma_start(out.rearrange("c p t -> p c t"), xT[:, :, :]).then_inc(stored, 16)
            sp.wait_ge(stored, 16)

        @block.gpsimd
        def _(pool):
            chain = Chain(pool, pool_chain)
            spare = pool_spare
            pool.memset(eps[:, 0:1], RMS_EPS).then_inc(const_ready, 1)
            pool.memset(eps[:, 1:2], LN_EPS).then_inc(const_ready, 1)
            pool.memset(ones[:, :], 1.0).then_inc(const_ready, 1)
            pool.memset(zeros[:, 0:1], 0.0).then_inc(u_used, ROWS)
            pool.memset(zeros[:, 1:], 0.0).then_inc(v_used, ROWS)

            pool.memset(mean[:, :], 1.0 / D).then_inc(const_ready, 1)
            chain.link(pool.memset(ident[:, :], 0.0))
            pool.affine_select(out=ident[:, :], in_=ident[:, :], compare_op=ALU.not_equal, fill=1.0, base=0,
                               pattern=[[-1, P]], channel_multiplier=1).then_inc(const_ready, 1)
            chain.link(pool.memset(blk[:, :], 1.0))
            pool.affine_select(out=blk[:, 0:DH], in_=blk[:, 0:DH], compare_op=ALU.is_ge, fill=0.0, base=DH - 1,
                               pattern=[[0, DH]], channel_multiplier=-1).then_inc(const_ready, 1)
            pool.affine_select(out=blk[:, DH:], in_=blk[:, DH:], compare_op=ALU.is_ge, fill=0.0, base=-DH,
                               pattern=[[0, DH]], channel_multiplier=1).then_inc(const_ready, 1)
            pool.iota(count16[:, :], pattern=[[1, PICKS]], base=0, channel_multiplier=0).then_inc(const_ready, 1)
            pool.memset(u[:, :, 0:2], 0.0).then_inc(const_ready, 1)
            for n in range(10):
                split_lo(pool, "p", n)
            for t in range(NT):
                pool.wait_ge(idx_score, t + 1)
                pool.affine_select(out=score[t], in_=score[t], compare_op=ALU.is_ge, fill=LOW, base=t * P,
                                   pattern=[[-1, (t + 1) * P]], channel_multiplier=1).then_inc(idx_causal, 1)
                split_lo(pool, "p", 10 + t)
            for n in range(12, LO_1.count("p")):
                split_lo(pool, "p", n)
            pool.wait_ge(par_loaded, 48)
            pool.affine_select(out=wsT[:, :, :], in_=wsT[:, :, :], compare_op=ALU.is_ge, fill=0.0, base=0,
                               pattern=[[0, LAYERS * 4], [1, P]], channel_multiplier=-1).then_inc(const_ready, 1)
            base = 4 + 2 + 4 + 4 + NT
            for c in range(HC):
                pool.wait_ge(taken_act, base + 4 + c + 1)
                pool.tensor_tensor(u[:, c, 2:], u[:, c, 2:], cc[:, c, :], ALU.mult).then_inc(u_ready, 1)
            for t in range(NT):
                with pool.Fori(0, EXPERT_HEADS // 2) as i:
                    for par in range(2):
                        pool.wait_ge(routed, 2 * i + (t * EXPERT_HEADS + par + 1))
                        for table, dst, loaded, used in ((a["peer_u"], 0, u_loaded, u_used), (a["peer_v"], ROWS, v_loaded, v_used)):
                            for j in range(PICKS):
                                pool.wait_ge(used, i * (2 * PICKS) + ((t * EXPERT_HEADS + par) * PICKS + j + 1))
                                pool.sem_inc(spare)
                                pool.indirect_dma_start(
                                    out=rows[:, dst + j % ROWS, :], out_offset=None, in_=table,
                                    in_offset=bass.IndirectOffsetOnAxis(ap=expert[par][:, j:j + 1], axis=0)) \
                                    .then_inc(loaded[j % ROWS], 16)
            pool.wait_ge(s_taken, NT * EXPERT_HEADS)
            pool.iota(distance, pattern=[[-1, T]], base=P, channel_multiplier=1).then_inc(bias_iota, 1)
            pool.wait_ge(bias_lin, HEADS)
            chain.link(pool.affine_select(out=bias8[:, :, :], in_=bias8[:, :, :], compare_op=ALU.is_ge, fill=MASKED,
                                          base=P, pattern=[[0, HEADS], [-1, T]], channel_multiplier=1))
            pool.affine_select(out=bias8[:, :, :], in_=bias8[:, :, :], compare_op=ALU.is_ge, fill=MASKED,
                               base=-1, pattern=[[0, HEADS], [1, T]], channel_multiplier=-1).then_inc(bias_ready, 1)
            with pool.Fori(0, LAYERS) as l:
                for n in range(PRING):
                    split_hi(pool, n, l)
                pool.wait_ge(x_ready, l * KC + KC)
                pool.wait_ge(taken_dve, l * D2 + D1)
                pool.sem_inc(spare)
                for c in range(KC):
                    ins = pool.tensor_scalar(xb[:, c, :], xT[:, c, :], ALPHA, None, ALU.mult)
                    ins.then_inc(xb_ready, 1)
                for n in range(14, 22):
                    split_hi(pool, n, l)
                for n in range(38, 58):
                    split_lo(pool, "p", n, l)

        @block.scalar
        def _(act):
            chain = Chain(act, act_chain)
            act.dma_start(cbc, a["c"].partition_broadcast(P).rearrange("p o d -> p (o d)")).then_inc(c_loaded, 16)
            act.dma_start(cols[:, :], a["cols"]).then_inc(cols_loaded, 16)
            act.wait_ge(c_loaded, 16)
            nc.scalar.activation(cbc, cbc, ACT.Silu).then_inc(c_silu, 1)

            act.wait_ge(x_loaded, 16)
            for c in range(KC):
                nc.scalar.activation(sq[:, c, :], xT[:, c, :], ACT.Square).then_inc(squares, 1)
            act.wait_ge(const_ready, 2)
            act.wait_ge(sums, 1)
            nc.scalar.activation(rstd[:, :], aux[:, 0, 0:T], ACT.Sqrt, bias=eps[:, 0:1], scale=1.0 / D).then_inc(std_ready, 1)
            rounded = [0]

            def round_to(n, l=None):
                for k in range(rounded[0], n):
                    if l is None or HI_2[k] == "a":
                        split_hi(act, k, l)
                rounded[0] = n

            round_to(2)
            for c in range(KC):
                act.wait_ge(h_scaled, c + 1)
                nc.scalar.activation(xh[:, c, :], hT[:, c, :], ACT.Identity, bias=mod[:, c:c + 1])
                nc.scalar.activation(hT[:, c, :], hT[:, c, :], ACT.Identity, bias=mod[:, c:c + 1]).then_inc(h_ready, 1)
            round_to(PRING)
            act.dma_start(wsT[:, :, :], a["wsT"].rearrange("g s t -> s g t")).then_inc(par_loaded, 16)
            act.dma_start(sink[:, :, :].rearrange("p l h -> p (l h)"),
                          a["sink"].partition_broadcast(P).rearrange("p o d -> p (o d)")).then_inc(par_loaded, 16)
            act.dma_start(lcol[:, :, :], a["lcol"]).then_inc(par_loaded, 16)

            taken = [0]

            def take(dst, func=ACT.Copy, l=None, width=T, sq_to=None, **kw):
                m = taken[0]
                taken[0] += 1
                chunk_wait(act, m, l)
                if sq_to is not None:
                    nc.scalar.activation(sq_to, chunk_out(m, l, width), ACT.Square).then_inc(qk_sq, 1)
                nc.scalar.activation(dst, chunk_out(m, l, width), func, **kw).then_inc(taken_act, 1)

            for c in range(4):
                take(iqT[:, c, :])
                if c % 2:
                    round_to(c + 5)
            take(ikT)
            take(iw[:, :, :].rearrange("p n h -> p (n h)"), width=NT * HEADS)
            round_to(9)
            for b in range(6):
                act.wait_ge(idx_raw, b + 1)
                dst = relu[0][:, b * 512:(b + 1) * 512] if b < 2 else relu[1][:, (b - 2) * 512:(b - 1) * 512]
                nc.scalar.activation(dst, aux[:, b, :], ACT.Relu).then_inc(idx_relu, 1)
            for c in range(4):
                take(qn[:, c, :], sq_to=sq[:, c, :])
                if c % 2:
                    round_to(c + 10)
            for c in range(4):
                take(kn[:, c, :], sq_to=sq[:, 4 + c, :])
                if c % 2:
                    round_to(c + 14)

            def qk_root(n):
                for b in range(2):
                    act.wait_ge(qk_sum, 2 * n + b + 1)
                    nc.scalar.activation(sq[:, 4 * n + 2 * b:4 * n + 2 * b + 2, :].rearrange("p c t -> p (c t)"),
                                         aux[:, 2 * n + b, :], ACT.Sqrt, bias=eps[:, 0:1], scale=1.0 / DH).then_inc(qk_std, 1)

            qk_root(0)
            for t in range(NT):
                take(v1[:, t, :], width=512)
                round_to(19 + 2 * t)
            qk_root(1)
            for c in range(4):
                take(cc[:, c, :])
                if c % 2:
                    round_to(c + 22)

            def exps(s, buf, t, l=None):
                act.wait_ge(s["negmax"], at(l, NT, t + 1))
                for h in range(HEADS):
                    nc.scalar.activation(probs(buf, t, h), probs(buf, t, h), ACT.Exp, bias=smax[:, t, h:h + 1],
                                         accum_out=ssum[:, t, h:h + 1]).then_inc(s["probs"], 1)

            def p_out(s, buf, t, l=None):
                for k in range(t + 1):
                    for hh in range(2):
                        b = 2 * t + 2 * k + hh
                        act.wait_ge(s["p_turned"], at(l, 6, b + 1))
                        nc.scalar.copy(probs_T(buf, t, k)[:, 4 * hh:4 * hh + 4, :].rearrange("p h q -> p (h q)"), aux[:, b, :]) \
                            .then_inc(s["p_out"], 1)

            for t in range(NT):
                for c in range(2):
                    take(u[:, 2 * t + c, 2:T + 2])
                round_to(27 + 2 * t)
                exps(att1, p_buf, t)
            nc.scalar.activation(warm[:, :], eps[:, 0:1], ACT.Sqrt)
            for c in range(4):
                take(cb[:, c, :])
                if c % 2:
                    round_to(c + 30)
            for t in range(NT):
                p_out(att1, pt_buf, t)
            for c in range(HC):
                act.wait_ge(conv_y, c + 1)
                nc.scalar.activation(sq[:, c, :], cc[:, c, :], ACT.Square).then_inc(conv_sq, 1)
            for t in range(NT):
                act.wait_ge(att1["y_sq"], t + 1)
                nc.scalar.activation(ystat[:, t, 1:2], ystat[:, t, 0:1], ACT.Sqrt, bias=eps[:, 0:1], scale=1.0 / 512) \
                    .then_inc(att1["y_std"], 1)
            act.wait_ge(conv_sum, 1)
            nc.scalar.activation(rstd[:, :], aux[:, 4, 0:T], ACT.Sqrt, bias=eps[:, 0:1], scale=1.0 / 512).then_inc(conv_std, 1)
            for t in range(NT):
                ts = slice(t * P, (t + 1) * P)
                act.wait_ge(att1["y_turned"], t + 1)
                for c in range(HC):
                    nc.scalar.activation(yaT[:, c, ts], aux[:, 2 + t, c * P:(c + 1) * P], ACT.Copy,
                                         scale=cols[:, ATT_W + c:ATT_W + c + 1]).then_inc(att1["y_done"], 1)
                act.wait_ge(att1["y_done"], (t + 1) * HC)
                nc.scalar.copy(xh[:, 0:HC, ts], yaT[:, :, ts]).then_inc(mix_hi, 1)
            for c in range(HC):
                act.wait_ge(conv_done, c + 1)
                nc.scalar.copy(xh[:, HC + c, :], cc[:, c, :]).then_inc(mix_hi, 1)
            for c in range(KC):
                act.wait_ge(taken_dve, c + 1)
                nc.scalar.activation(sq[:, c, :], xT[:, c, :], ACT.Square).then_inc(squares, 1)
                if c in (1, 3):
                    round_to(c + 34)
            act.wait_ge(sums, 2)
            nc.scalar.activation(rstd[:, :], aux[:, 5, 0:T], ACT.Sqrt, bias=eps[:, 0:1], scale=1.0 / D).then_inc(std_ready, 1)
            for c in range(KC):
                act.wait_ge(h_scaled, KC + c + 1)
                nc.scalar.activation(hT[:, c, :], hT[:, c, :], ACT.Identity, bias=mod[:, 3 * KC + c:3 * KC + c + 1]).then_inc(h_ready, 1)
            def next_head(g):
                nc.scalar.copy(s_cur[:, :, :].rearrange("p s k -> p (s k)"),
                               s_all[:, bass.ds(g, 1), :].rearrange("p o k -> p (o k)")).then_inc(s_taken, 1)

            def scored(lo, hi):
                for h in range(lo, hi):
                    for s in range(2):
                        act.wait_ge(queries, 2 * h + s + 1)
                        if h >= 2:
                            act.wait_ge(expert_scores, h - 1)
                        nc.scalar.copy(pq[:, h % 2, s, :], aux[:, 4 + s, 0:T]).then_inc(queries_out, 1)
                    act.wait_ge(expert_scores, h + 1)
                    nc.scalar.copy(s_all[:, h::EXPERT_HEADS, :], aux[:, h % 2, :].rearrange("p (n k) -> p n k", n=NT)).then_inc(scores_out, 1)

            def gates(t, par, i, last=False):
                g = t * EXPERT_HEADS + par
                act.wait_ge(routed, 2 * i + (g + 1))
                nc.scalar.activation(gate, top, ACT.Exp, bias=negtop, accum_out=gate_sum).then_inc(gate_exp, 1)
                if not last:
                    next_head(2 * i + (g + 1))
                act.wait_ge(u_used, i * (2 * PICKS) + ((g + 1) * PICKS + ROWS))
                nc.scalar.activation(act_dots, dots, ACT.Gelu_apprx_tanh).then_inc(dots_act, 1)

            def sums_out(t):
                act.wait_ge(v_used, (t + 1) * EXPERT_HEADS * PICKS + ROWS)
                if t:
                    act.wait_ge(peer_turned, 2 * t)
                for b in range(2):
                    nc.scalar.copy(peer_tok[:, b * 512:(b + 1) * 512], aux[:, 2 + 2 * t + b, :]).then_inc(peer_out, 1)

            scored(0, 1)
            act.wait_ge(scores_out, 1)
            next_head(0)
            scored(1, EARLY_HEADS[0])
            act.wait_ge(scores_out, EARLY_HEADS[0])
            gates(0, 0, 0)
            scored(EARLY_HEADS[0], EARLY_HEADS[1])
            gates(0, 1, 0)
            scored(EARLY_HEADS[1], EARLY_HEADS[2])
            act.wait_ge(scores_out, EXPERT_HEADS)
            with act.Fori(1, EXPERT_HEADS // 2) as i:
                for par in range(2):
                    gates(0, par, i)
            sums_out(0)
            with act.Fori(0, EXPERT_HEADS // 2 - 1) as i:
                for par in range(2):
                    gates(1, par, i)
            for par in range(2):
                gates(1, par, EXPERT_HEADS // 2 - 1, last=par == 1)
            act.wait_ge(s_taken, NT * EXPERT_HEADS)
            act.dma_start(lnv.rearrange("p l k f -> p (l k f)"),
                          a["lnv"].partition_broadcast(P).rearrange("p o d -> p (o d)")).then_inc(late_loaded, 16)
            sums_out(1)
            act.wait_ge(u_used, NT * EXPERT_HEADS * PICKS + ROWS)
            act.dma_start(brow.rearrange("o l n -> o (l n)"), a["brow"]).then_inc(late_loaded, 16)

            with act.Fori(0, LAYERS) as l:
                taken[0] = 0

                def col(n):
                    return lcol[:, bass.ds(l, 1), n:n + 1].rearrange("p o n -> p (o n)")

                rounded[0] = PRING
                for c in range(KC):
                    act.wait_ge(x_ready, l * KC + (c + 1))
                    nc.scalar.copy(xh[:, c, :], xT[:, c, :]).then_inc(xh_ready, 1)
                for c in range(4):
                    take(qT[:, c, :], ACT.Identity, l, bias=col(BQ + c))
                    if c % 2:
                        round_to(c + 5, l)
                take(kT, ACT.Identity, l, bias=col(BK))
                round_to(9, l)
                take(v2[:, :, :].rearrange("p n f -> p (n f)"), ACT.Copy, l)
                round_to(10, l)
                for t in range(NT):
                    take(vg[:, t, :], ACT.Gelu, l, width=512)
                    round_to(12 + 2 * t, l)
                for c in range(4):
                    take(ug[:, c, :], ACT.Gelu, l, bias=col(BUG + c))
                    if c % 2:
                        round_to(c + 15, l)
                for t in range(NT):
                    exps(att2, p2_buf, t, l)
                for t in range(NT):
                    act.wait_ge(att2["sink_in"], l * NT + (t + 1))
                    nc.scalar.activation(ssink[:, t, :], ssink[:, t, :], ACT.Exp).then_inc(att2["sink_exp"], 1)
                for t in range(NT):
                    act.wait_ge(vn_stat, l * NT + (t + 1))
                    nc.scalar.activation(mv[:, t, 1:2], mv[:, t, 1:2], ACT.Sqrt, bias=eps[:, 1:2]).then_inc(vn_std, 1)
                for c in range(4):
                    take(zg[:, c, :], ACT.Silu, l, bias=col(BZG + c))
                    if c % 2:
                        round_to(c + 19, l)
                for t in range(NT):
                    p_out(att2, pt2_buf, t, l)
                for c in range(4):
                    take(za[:, c, :], ACT.Silu, l, bias=col(BZA + c))
                    if c % 2:
                        round_to(c + 23, l)
                for c in range(KC):
                    take(sga[:, c, :], ACT.Sigmoid, l, bias=col(BGA + c))
                    if c % 2:
                        round_to(c + 27, l)
                for c in range(KC):
                    take(sgg[:, c, :], ACT.Sigmoid, l, bias=col(BGG + c))
                    if c % 2:
                        round_to(c + 35, l)
                act.wait_ge(att2["y_done"], l * NT + NT)
                act.wait_ge(yg_ready, l * NT + NT)
                for c in range(2 * HC):
                    nc.scalar.copy(xh[:, c, :], (ya2T if c < HC else ug)[:, c % HC, :]).then_inc(y_hi, 1)
                for n in range(44, 52, 2):
                    round_to(n, l)
                for c in range(KC):
                    if c % 2 == 0:
                        round_to(52 + c, l)
                    if c < HC:
                        act.wait_ge(gated, l * KC + (c + 1))
                        nc.scalar.copy(xh[:, c, :], sga[:, c, :]).then_inc(merged_hi, 1)
                for c in range(HC, KC):
                    act.wait_ge(gated, l * KC + (c + 1))
                    nc.scalar.copy(xh[:, c, :], sga[:, c, :]).then_inc(merged_hi, 1)
                nc.scalar.activation(warm[:, :], eps[:, 0:1], ACT.Sqrt)
                round_to(60, l)
                round_to(62, l)
                for c in range(KC):
                    act.wait_ge(centred, l * KC + (c + 1))
                    nc.scalar.activation(sq2[:, c, :], res[:, c, :], ACT.Square).then_inc(centred_sq, 1)
                act.wait_ge(variances, l + 1)
                nc.scalar.activation(rstd[:, :], aux[:, 1, 0:T], ACT.Sqrt, bias=eps[:, 1:2]).then_inc(ln_std, 1)
                for c in range(KC):
                    act.wait_ge(ln_scaled, l * KC + (c + 1))
                    nc.scalar.activation(xT[:, c, :], res[:, c, :], ACT.Identity, bias=col(LNB + c)).then_inc(x_ready, 1)

        @block.tensor
        def _(pe):
            mm = nc.tensor.matmul
            chunk = [0]

            tile = [0]

            def next_unit(l=None):
                n = tile[0]
                tile[0] += 1
                w_wait(pe, n, l)
                return w_slot(n, l)

            def next_unit():
                n = tile[0]
                tile[0] += 1
                w_wait(pe, n)
                return w_slot(n)

            piece = [0]

            def next_pieces(n, l=None):
                first = piece[0]
                piece[0] += n
                for k in range(first, first + n):
                    split_wait(pe, k, l)
                return first

            def by_parts(o, w, x, start=True, stop=True):
                mm(o, w[0], x[0], start=start, stop=False)
                mm(o, w[0], x[1], start=False, stop=False)
                return mm(o, w[1], x[0], start=False, stop=stop)

            def input_parts(ready, count, at=0):
                seen = set()

                def chunk_parts(k):
                    if k not in seen:
                        pe.wait_ge(ready, count(k))
                        seen.add(k)
                    return xh[:, at + k, :], xl[:, at + k, :]
                return chunk_parts

            def whole(x, n, l=None):
                for _ in range(n):
                    hi, lo = parts(next_pieces(1, l), l)
                    chunks = hi.shape[1]
                    m = chunk[0]
                    chunk[0] += 1
                    bank_free(pe, m, l)
                    for k in range(chunks):
                        ins = by_parts(chunk_out(m, l), (hi[:, k, :], lo[:, k, :]), x(k), k == 0, k == chunks - 1)
                    ins.then_inc(proj, 1)

            def token_major(x, bias=None, l=None):
                m = chunk[0]
                chunk[0] += NT
                for half in range(2):
                    w = part_pairs(next_pieces(2, l))
                    for t in range(NT):
                        if half == 0:
                            bank_free(pe, m + t, l)
                        o = chunk_out(m + t, l, 512)[:, half * 256:half * 256 + 256]
                        for k in range(KC):
                            ins = by_parts(o.rearrange("p (s n) -> p s n", s=2), [z[:, t * P:(t + 1) * P] for z in x(k)], w(k, l),
                                           k == 0, k == KC - 1 and bias is None)
                        if bias is not None:
                            ins = mm(o, ones[0:1, :], bias(half * 256, 256), start=False, stop=True)
                        if half == 1:
                            ins.then_inc(proj, 1)

            pe.wait_ge(const_ready, 7)
            for c in range(KC):
                pe.wait_ge(squares, c + 1)
                ins = mm(aux[:, 0, 0:T], ones[:, :], sq[:, c, :], start=(c == 0), stop=(c == KC - 1))
            ins.then_inc(sums, 1)
            h_in = input_parts(h_split, lambda k: k + 1)
            whole(h_in, 4)
            whole(h_in, 1)
            m = chunk[0]
            chunk[0] += 1
            bank_free(pe, m)
            w = w_slot(2)
            w_wait(pe, 2)
            for t in range(NT):
                for k in range(KC):
                    ins = mm(chunk_out(m)[:, t * HEADS:(t + 1) * HEADS], hT[:, k, t * P:(t + 1) * P], w[:, k, P:P + HEADS],
                             start=(k == 0), stop=(k == KC - 1))
            ins.then_inc(proj, 1)
            pe.wait_ge(taken_act, 5)
            for t in range(NT):
                for h in range(HEADS):
                    r = slice(64 * (h // 4), 64 * (h // 4) + 64)
                    ins = mm(logit_bank(t, h), iqT[r, h % 4, t * P:(t + 1) * P], ikT[r, 0:(t + 1) * P], start=True, stop=True)
                    if h % (4 >> t) == (4 >> t) - 1:
                        ins.then_inc(idx_raw, 1)
            whole(h_in, 4)
            whole(h_in, 4)

            def qk_sums(n):
                pe.wait_ge(qk_sq, 4 * n + 4)
                pe.wait_ge(idx_relu, 2 + 2 * n)
                for b in range(2):
                    mm(aux[:, 2 * n + b, :], blk[:, :], sq[:, 4 * n + 2 * b:4 * n + 2 * b + 2, :].rearrange("p c t -> p (c t)"),
                       start=True, stop=True).then_inc(qk_sum, 1)

            qk_sums(0)
            token_major(h_in)
            qk_sums(1)
            whole(h_in, 4)

            def logits(s, q, k, l=None):
                for t in range(NT):
                    for h in range(HEADS):
                        ins = mm(logit_bank(t, h), q(h, t), k(h, (t + 1) * P), start=True, stop=True)
                        if h % (4 >> t) == (4 >> t) - 1:
                            ins.then_inc(s["logits"], 1)

            def turn_p(s, buf, l=None):
                for t in range(NT):
                    pe.wait_ge(s["probs"], at(l, NT * HEADS, (t + 1) * HEADS))
                    for k in range(t + 1):
                        for h in range(HEADS):
                            b = 2 * t + 2 * k + h // 4
                            ins = nc.tensor.transpose(aux[:, b, (h % 4) * P:(h % 4 + 1) * P], probs(buf, t, h)[:, k * P:(k + 1) * P], ident[:, :])
                            if h % 4 == 3:
                                ins.then_inc(s["p_turned"], 1)

            def sum_v(s, buf, v, l=None):
                for t in range(NT):
                    pe.wait_ge(s["p_out"], at(l, 6, 2 if t == 0 else 6))
                    for h in range(HEADS):
                        for k in range(t + 1):
                            ins = mm(aux[:, t, h * DH:(h + 1) * DH], probs_T(buf, t, k)[:, h, :], v(h, k), start=(k == 0), stop=(k == t))
                    ins.then_inc(s["summed"], 1)

            def turn_y(s, y, l=None):
                for t in range(NT):
                    pe.wait_ge(s["y_ready"], at(l, NT, t + 1))
                    for c in range(HC):
                        ins = nc.tensor.transpose(aux[:, 2 + t, c * P:(c + 1) * P], y[:, t, c * P:(c + 1) * P], ident[:, :])
                    ins.then_inc(s["y_turned"], 1)

            pe.wait_ge(qk_ready, 2)
            pe.wait_ge(idx_relu, 6)
            pe.wait_ge(qk_std, 4)
            logits(att1, q1, k1)
            whole(h_in, 4)
            whole(h_in, 4)
            turn_p(att1, p_buf)
            sum_v(att1, pt_buf, lambda h, k: v1[:, k, head1(h) * DH:(head1(h) + 1) * DH])
            for c in range(HC):
                pe.wait_ge(conv_sq, c + 1)
                ins = mm(aux[:, 4, 0:T], ones[:, :], sq[:, c, :], start=(c == 0), stop=(c == HC - 1))
            ins.then_inc(conv_sum, 1)
            turn_y(att1, ytok)
            whole(input_parts(mix_split, lambda k: max(k + 1 + NT - HC, NT)), KC)
            for c in range(KC):
                pe.wait_ge(squares, KC + c + 1)
                ins = mm(aux[:, 5, 0:T], ones[:, :], sq[:, c, :], start=(c == 0), stop=(c == KC - 1))
            ins.then_inc(sums, 1)
            pe.wait_ge(h_ready, 2 * KC)
            def turn_h2(t):
                for c in range(KC):
                    ins = nc.tensor.transpose(h2_tok[t][:, c * P:(c + 1) * P], hT[:, c, t * P:(t + 1) * P], ident[:, :])
                ins.then_inc(h2_turned, 1)

            tile[0] = MIX_UNITS

            def score_heads(lo, hi):
                for h in range(lo, hi):
                    if h % 2 == 0:
                        sub[0] = next_unit()
                    w = next_unit()
                    for s in range(2):
                        if h:
                            pe.wait_ge(queries_out, 2 * h + s - 1)
                        for k in range(KC):
                            ins = mm(aux[:, 4 + s, 0:T], w[:, k, s * P:(s + 1) * P], hT[:, k, :], start=(k == 0), stop=(k == KC - 1))
                        ins.then_inc(queries, 1)
                    pe.wait_ge(queries_out, 2 * h + 2)
                    if h >= 2:
                        pe.wait_ge(scores_out, h - 1)
                    for t in range(NT):
                        for s in range(2):
                            ins = mm(aux[:, h % 2, (2 * t + s) * KEYS:(2 * t + s + 1) * KEYS], pq[:, h % 2, s, t * P:(t + 1) * P],
                                     sub[0][:, 0, (2 * (h % 2) + s) * KEYS:(2 * (h % 2) + s + 1) * KEYS], start=True, stop=True)
                    ins.then_inc(expert_scores, 1)

            def zero_sums(t):
                for b in range(2):
                    mm(aux[:, 2 + 2 * t + b, :], zeros[:, :], hT[:, 0:2, :].rearrange("p c t -> p (c t)"),
                       start=True, stop=False, skip_group_check=True)

            def sum_rows(t, par, i):
                g = t * EXPERT_HEADS + par
                pe.wait_ge(diag_ready, 2 * i + (g + 1))
                for j in range(PICKS):
                    pe.wait_ge(v_loaded[j % ROWS], i * 64 + 16 * (2 * g + j // ROWS + 1))
                    for b in range(2):
                        ins = mm(aux[:, 2 + 2 * t + b, :], diag[:, j, :], rows[:, ROWS + j % ROWS, b * 512:(b + 1) * 512],
                                 start=False, stop=False, skip_group_check=True)
                    ins.then_inc(v_used, 1)

            def turn_sums(t):
                for b in range(2):
                    pe.wait_ge(peer_out, 2 * t + b + 1)
                    for c in range(4):
                        ins = nc.tensor.transpose(h2_tok[t][:, (4 * b + c) * P:(4 * b + c + 1) * P],
                                                  peer_tok[:, (4 * b + c) * P:(4 * b + c + 1) * P], ident[:, :])
                    ins.then_inc(peer_turned, 1)

            sub = [None]
            score_heads(0, 1)
            turn_h2(0)
            score_heads(1, EARLY_HEADS[0])
            zero_sums(0)
            sum_rows(0, 0, 0)
            score_heads(EARLY_HEADS[0], EARLY_HEADS[1])
            sum_rows(0, 1, 0)
            score_heads(EARLY_HEADS[1], EARLY_HEADS[2])
            pe.wait_ge(scores_out, EXPERT_HEADS)
            turn_h2(1)
            with pe.Fori(1, EXPERT_HEADS // 2) as i:
                for par in range(2):
                    sum_rows(0, par, i)
            zero_sums(1)
            turn_sums(0)
            with pe.Fori(0, EXPERT_HEADS // 2) as i:
                for par in range(2):
                    sum_rows(1, par, i)
            turn_sums(1)

            with pe.Fori(0, LAYERS) as l:
                chunk[0], piece[0] = 0, 0
                pe.wait_ge(const_ready, 10)

                def bias_row(n, width):
                    return brow[:, bass.ds(l, 1), n:n + width].rearrange("o l n -> o (l n)")

                x = input_parts(x_split, lambda k: l * KC + (k + 1))
                whole(x, 4, l)
                whole(x, 1, l)
                pe.wait_ge(late_loaded, 32)
                hi, lo = parts(next_pieces(1, l), l)
                m = chunk[0]
                chunk[0] += 1
                bank_free(pe, m, l)
                for t in range(NT):
                    ts = slice(t * P, (t + 1) * P)
                    for k in range(KC):
                        by_parts(chunk_out(m, l)[:, ts], [z[:, ts] for z in x(k)], (hi[:, k, :], lo[:, k, :]), k == 0, False)
                    ins = mm(chunk_out(m, l)[:, ts], ones[0:1, :], bias_row(RV, P), start=False, stop=True)
                ins.then_inc(proj, 1)
                token_major(x, lambda at, n: bias_row(RVG + at, n), l)
                pe.wait_ge(taken_act, l * A2 + (A1 + 6))
                logits(att2, q2, k2, l)
                whole(x, 4, l)
                whole(x, 4, l)
                turn_p(att2, p2_buf, l)
                whole(x, 4, l)
                sum_v(att2, pt2_buf, lambda h, k: v2[:, k, (h // 4) * DH:(h // 4 + 1) * DH], l)
                whole(x, 8, l)
                turn_y(att2, ytok2, l)
                for t in range(NT):
                    pe.wait_ge(vn_ready, l * NT + (t + 1))
                    for g in range(4):
                        o = aux[:, 4 + t, g * P:(g + 1) * P]
                        mm(o, vg[:, t, g * P:(g + 1) * P], wsT[:, bass.ds(l * 4 + g, 1), :].rearrange("p o t -> p (o t)"), start=True, stop=False)
                        ins = mm(o, ones[0:1, :], bias_row(RSP + g * P, P), start=False, stop=True)
                    ins.then_inc(mixed, 1)
                whole(x, 8, l)
                whole(input_parts(y_split, lambda k: l * 2 * HC + (k + 1)), KC, l)
                whole(input_parts(y_split, lambda k: l * 2 * HC + (HC + k + 1), HC), KC, l)
                merged = input_parts(merged_split, lambda k: l * KC + (k + 1))
                for c in range(0, KC + 2, 2):
                    if c < KC:
                        whole(merged, 2, l)
                    for k in range(max(c - 2, 0), c):
                        pe.wait_ge(taken_dve, l * D2 + (D1 + 2 * KC + k + 1))
                        ins = mm(aux[:, 0, 0:T], mean[:, :], res[:, k, :], start=(k == 0), stop=(k == KC - 1))
                ins.then_inc(means, 1)
                for c in range(KC):
                    pe.wait_ge(centred_sq, l * KC + (c + 1))
                    ins = mm(aux[:, 1, 0:T], mean[:, :], sq2[:, c, :], start=(c == 0), stop=(c == KC - 1))
                ins.then_inc(variances, 1)

        @block.vector
        def _(dve):
            v = nc.vector
            spare = dve_spare
            chain = Chain(dve, dve_chain)

            def ada_dots(lo, hi):
                for n in range(lo, hi):
                    dve.wait_ge(ada_loaded[n % ADA_RING], 16 * (n // ADA_RING + 1))
                    tile = ada[:, n % ADA_RING, :]
                    v.tensor_tensor_reduce(tile, tile, cbc, 1.0, 0.0, ALU.mult, ALU.add, mod[:, n:n + 1]).then_inc(ada_used, 1)

            def ada_bias(lo, hi):
                dve.wait_ge(ada_used, hi)
                chain.link(v.tensor_tensor(mod[:, lo:hi], mod[:, lo:hi], cols[:, B_ADA + lo:B_ADA + hi], ALU.add))

            def ada_tiles(lo, hi):
                ada_dots(lo, hi)
                ada_bias(lo, hi)

            def part(n):
                return mod[:, n * KC:(n + 1) * KC]

            def norm(n, weight, scale):
                chain.link(v.tensor_scalar(gain[:, :], part(scale), 1.0, None, ALU.add))
                chain.link(v.tensor_tensor(gain[:, :], gain[:, :], cols[:, weight:weight + KC], ALU.mult))
                dve.wait_ge(std_ready, n + 1)
                chain.link(v.reciprocal(rstd[:, :], rstd[:, :]))
                for c in range(KC):
                    v.scalar_tensor_tensor(hT[:, c, :], xT[:, c, :], gain[:, c:c + 1], rstd[:, :], ALU.mult, ALU.mult).then_inc(h_scaled, 1)

            dve.wait_ge(c_silu, 1)
            dve.wait_ge(cols_loaded, 16)
            ada_tiles(0, 2 * KC)
            dve.wait_ge(x_loaded, 16)
            norm(0, N1W, 1)
            for c in range(KC):
                dve.wait_ge(h_ready, c + 1)
                v.tensor_tensor(xl[:, c, :], hT[:, c, :], full(xh[:, c, :]), ALU.subtract).then_inc(h_split, 1)
            ada_tiles(2 * KC, 3 * KC)

            dve.wait_ge(taken_act, 6)
            for h in range(HEADS):
                for t in range(NT):
                    dve.wait_ge(idx_relu, 2 * t + h // (4 >> t) + 1)
                    w, r = iw[:, t, head1(h):head1(h) + 1], probs(relu, t, h)
                    if h == 0:
                        chain.mark(v.tensor_scalar(score[t], r, w, None, ALU.mult))
                    else:
                        chain.wait(back=1)
                        chain.mark(v.scalar_tensor_tensor(score[t], r, w, score[t], ALU.mult, ALU.add))
            for t in range(NT):
                chain.wait(back=1 - t)
                v.tensor_scalar(score[t], score[t], IDX_SCALE, None, ALU.mult).then_inc(idx_score, 1)
            dve.wait_ge(idx_causal, NT)
            for n in range(TOPK // 8):
                for t in range(NT):
                    if n:
                        chain.wait(back=1)
                    chain.mark(v.max(top8[:, t, :], score[t] if n == 0 else left[t]))
                for t in range(NT):
                    chain.wait(back=1)
                    chain.mark(v.match_replace(left[t], top8[:, t, :], score[t] if n == 0 else left[t], LOW))
            for t in range(NT):
                chain.wait(back=1)
                chain.mark(v.tensor_tensor(keep[t], score[t], left[t], ALU.is_gt))
            for t in range(NT):
                chain.wait(back=1 - t)
                v.tensor_scalar(keep[t], keep[t], 1.0, -MASKED, ALU.subtract, ALU.mult).then_inc(keep_ready, 1)
            for n, (z, w) in enumerate(((qn, Q_W), (kn, K_W))):
                dve.wait_ge(qk_std, 2 * n + 2)
                r = sq[:, 4 * n:4 * n + 4, :].rearrange("p c t -> p (c t)")
                z = z.rearrange("p c t -> p (c t)")
                chain.link(v.reciprocal(r, r))
                v.scalar_tensor_tensor(z, z, cols[:, w:w + 1], r, ALU.mult, ALU.mult).then_inc(qk_ready, 1)

            def mask_logits(s, buf, bias, t, l=None):
                for h in range(HEADS):
                    dve.wait_ge(s["logits"], at(l, 6, 2 * t + h // (4 >> t) + 1))
                    if l is not None:
                        dve.sem_inc(spare)
                    chain.mark(v.tensor_tensor_reduce(probs(buf, t, h), logit_bank(t, h), bias(t, h), ATT_SCALE, LOW,
                                                      ALU.add, ALU.max, smax[:, t, h:h + 1]))
                chain.wait()

            lowered = [LO_1.count("p")]

            def low_to(n, l=None):
                for k in range(lowered[0], n):
                    split_lo(dve, "d", k, l)
                lowered[0] = n

            low_to(25)
            ada_dots(3 * KC, 3 * KC + ADA_RING)
            dve.wait_ge(keep_ready, 2)
            for t in range(NT):
                mask_logits(att1, p_buf, lambda t, h: keep[t], t)
                v.tensor_scalar(smax[:, t, :], smax[:, t, :], -1.0, None, ALU.mult).then_inc(att1["negmax"], 1)
                low_to(27 + 2 * t)

            def over_sums(s, y, t, l=None):
                chain.link(v.reciprocal(ssum[:, t, :], ssum[:, t, :]))
                dve.wait_ge(s["summed"], at(l, NT, t + 1))
                return v.tensor_tensor(y[:, t, :].rearrange("p (h d) -> p h d", d=DH),
                                       aux[:, t, :].rearrange("p (h d) -> p h d", d=DH),
                                       ssum[:, t, :].unsqueeze(2).broadcast_to([P, HEADS, DH]), ALU.mult)

            for c in range(HC):
                dve.wait_ge(u_ready, c + 1)
                chain.mark(v.tensor_scalar(cc[:, c, :], u[:, c, 2:T + 2], cols[:, CONV_W + 2 * HC + c:CONV_W + 2 * HC + c + 1],
                                           cols[:, CONV_B + c:CONV_B + c + 1], ALU.mult, ALU.add))
            for tap in (1, 0):
                for c in range(HC):
                    chain.wait(back=HC - 1)
                    chain.mark(v.scalar_tensor_tensor(cc[:, c, :], u[:, c, tap:T + tap], cols[:, CONV_W + tap * HC + c:CONV_W + tap * HC + c + 1],
                                                      cc[:, c, :], ALU.mult, ALU.add))
            low_to(31)
            base = 4 + 2 + 4 + 4 + NT
            for c in range(HC):
                dve.wait_ge(taken_act, base + 8 + c + 1)
                chain.wait(back=HC - 1 - c)
                v.tensor_tensor(cc[:, c, :], cc[:, c, :], cb[:, c, :], ALU.mult).then_inc(conv_y, 1)
                if c == 1:
                    low_to(33)
            for t in range(NT):
                dve.wait_ge(att1["probs"], (t + 1) * HEADS)
                chain.link(over_sums(att1, ytok, t))
                v.tensor_tensor_reduce(p_buf[t][:, 0:512], ytok[:, t, :], ytok[:, t, :], 1.0, 0.0, ALU.mult, ALU.add,
                                       ystat[:, t, 0:1]).then_inc(att1["y_sq"], 1)
            for t in range(NT):
                dve.wait_ge(att1["y_std"], t + 1)
                chain.link(v.reciprocal(ystat[:, t, 1:2], ystat[:, t, 1:2]))
                v.tensor_scalar(ytok[:, t, :], ytok[:, t, :], ystat[:, t, 1:2], None, ALU.mult).then_inc(att1["y_ready"], 1)
            dve.wait_ge(conv_std, 1)
            chain.link(v.reciprocal(rstd[:, :], rstd[:, :]))
            for c in range(HC):
                v.scalar_tensor_tensor(cc[:, c, :], cc[:, c, :], cols[:, CNV_W + c:CNV_W + c + 1], rstd[:, :], ALU.mult, ALU.mult) \
                    .then_inc(conv_done, 1)
            for t in range(NT):
                ts = slice(t * P, (t + 1) * P)
                dve.wait_ge(mix_hi, t + 1)
                v.tensor_tensor(xl[:, 0:HC, ts], yaT[:, :, ts], full(xh[:, 0:HC, ts]), ALU.subtract).then_inc(mix_split, 1)
            for c in range(HC):
                dve.wait_ge(mix_hi, NT + c + 1)
                v.tensor_tensor(xl[:, HC + c, :], cc[:, c, :], full(xh[:, HC + c, :]), ALU.subtract).then_inc(mix_split, 1)
            late = 4 * KC
            ada_dots(3 * KC + ADA_RING, late)
            for c in range(KC):
                if c in (2, 4):
                    low_to(33 + c)
                m = M1 - KC + c
                chunk_wait(dve, m)
                v.scalar_tensor_tensor(xT[:, c, :], chunk_out(m), mod[:, 2 * KC + c:2 * KC + c + 1], xT[:, c, :], ALU.mult, ALU.add) \
                    .then_inc(taken_dve, 1)
                ada_dots(late + c, late + c + 1)
            ada_bias(3 * KC, 5 * KC)
            dve.wait_ge(taken_dve, KC)
            norm(1, N2W, 4)
            ada_tiles(5 * KC, 6 * KC)

            def flat2(ap):
                return ap.rearrange("p s k -> p (s k)")

            def top16(*lists):
                n = len(lists)
                for half in range(2):
                    hs = slice(8 * half, 8 * half + 8)
                    for k, (src, rest, values, index) in enumerate(lists):
                        if half:
                            chain.wait(back=2 * (n - 1) - k)
                        chain.mark(v.max(values[:, hs], rest if half else src))
                    for k, (src, rest, values, index) in enumerate(lists):
                        chain.wait(back=n - 1 + (k if half == 0 else 0))
                        chain.mark(v.max_index(index[:, hs], values[:, hs], rest if half else src))
                        if half == 0:
                            chain.mark(v.match_replace(rest, values[:, hs], src, LOW))
                chain.wait()

            def route(par, i, g):
                dve.wait_ge(s_taken, 2 * i + (g + 1))
                dve.sem_inc(spare)
                top16(*[(s_cur[:, s, :], s_left[:, s, :], half_top[:, s, :], half_idx[:, s, :]) for s in range(2)])
                chain.link(v.tensor_tensor(combo.rearrange("p (k n) -> p k n", n=PICKS),
                                           half_top[:, 0, :].unsqueeze(2).broadcast_to([P, PICKS, PICKS]),
                                           half_top[:, 1, :].unsqueeze(1).broadcast_to([P, PICKS, PICKS]), ALU.add))
                top16((combo, combo_left, top, pos))
                chain.mark(v.tensor_scalar(negtop, top[:, 0:1], -1.0, None, ALU.mult))
                chain.mark(v.tensor_scalar(place[:, 0, :], pos, 4, None, ALU.logical_shift_right))
                chain.link(v.tensor_scalar(place[:, 1, :], pos, PICKS - 1, None, ALU.bitwise_and))
                rows_ = hit.rearrange("p s k n -> p (s k) n")
                chain.link(v.tensor_tensor(rows_, count16[:, :].unsqueeze(1).broadcast_to([P, 2 * PICKS, PICKS]),
                                           flat2(place).unsqueeze(2).broadcast_to([P, 2 * PICKS, PICKS]), ALU.is_equal))
                chain.link(v.tensor_tensor(hit, hit, half_idx.unsqueeze(2).broadcast_to([P, 2, PICKS, PICKS]), ALU.mult))
                chain.link(v.tensor_reduce(flat2(picked), rows_, AX, ALU.add))
                v.scalar_tensor_tensor(expert[par], picked[:, 0, :], float(KEYS), picked[:, 1, :], ALU.mult, ALU.add).then_inc(routed, 1)

            for t in range(NT):
                dve.wait_ge(h2_turned, t + 1)
                with dve.Fori(0, EXPERT_HEADS // 2) as i:
                    chain.enter(i, 2 * ROUTE_STEPS)
                    chain.spare = spare
                    for par in range(2):
                        g = t * EXPERT_HEADS + par
                        route(par, i, g)
                        for j in range(PICKS):
                            dve.wait_ge(u_loaded[j % ROWS], i * 64 + 16 * (2 * g + j // ROWS + 1))
                            row = rows[:, j % ROWS, :]
                            v.tensor_tensor_reduce(row, row, h2_tok[t], 1.0, 0.0, ALU.mult, ALU.add, dots[:, j:j + 1]).then_inc(u_used, 1)
                        dve.wait_ge(gate_exp, 2 * i + (g + 1))
                        chain.link(v.reciprocal(gate_inv, gate_sum))
                        dve.wait_ge(dots_act, 2 * i + (g + 1))
                        chain.link(v.scalar_tensor_tensor(weight, act_dots, gate_inv, gate, ALU.mult, ALU.mult))
                        dve.wait_ge(v_used, i * (2 * PICKS) + (g * PICKS + ROWS))
                        v.tensor_tensor(diag, ident[:, :].unsqueeze(1).broadcast_to([P, PICKS, P]),
                                        weight.unsqueeze(2).broadcast_to([P, PICKS, P]), ALU.mult).then_inc(diag_ready, 1)
                chain.leave(EXPERT_HEADS // 2)
            def join(t, b):
                dve.wait_ge(peer_turned, 2 * t + b + 1)
                for c in range(4 * b, 4 * b + 4):
                    x = xT[:, c, t * P:(t + 1) * P]
                    ins = v.scalar_tensor_tensor(x, h2_tok[t][:, c * P:(c + 1) * P], mod[:, 5 * KC + c:5 * KC + c + 1], x, ALU.mult, ALU.add)
                    if t:
                        ins.then_inc(x_ready, 1)

            for b in range(2):
                join(0, b)
            dve.wait_ge(bias_iota, 1)
            for h in range(HEADS):
                v.tensor_scalar(bias8[:, h, :], distance, -(2.0 ** -(h + 1)) / ATT_SCALE, None, ALU.mult).then_inc(bias_lin, 1)
            for b in range(2):
                join(1, b)

            with dve.Fori(0, LAYERS) as l:
                chain.enter(l, LAYER_STEPS)
                chain.spare = spare

                def taken(n):
                    dve.wait_ge(taken_act, l * A2 + (A1 + n))

                def col(n):
                    return lcol[:, bass.ds(l, 1), n:n + 1].rearrange("p o n -> p (o n)")

                lowered[0] = 0

                def merged_low(c):
                    dve.wait_ge(merged_hi, l * KC + (c + 1))
                    v.tensor_tensor(xl[:, c, :], sga[:, c, :], full(xh[:, c, :]), ALU.subtract).then_inc(merged_split, 1)

                low_to(2, l)
                for c in range(KC):
                    dve.wait_ge(xh_ready, l * KC + (c + 1))
                    v.tensor_tensor(xl[:, c, :], xT[:, c, :], full(xh[:, c, :]), ALU.subtract).then_inc(x_split, 1)
                low_to(12, l)
                for t in range(NT):
                    taken(6 + t + 1)
                    chain.link(v.bn_stats(bn[:, t, :], vg[:, t, :]))
                    v.bn_aggr(mv[:, t, :], bn[:, t, :]).then_inc(vn_stat, 1)
                low_to(14, l)
                dve.wait_ge(bias_ready, 1)
                for t in range(NT):
                    mask_logits(att2, p2_buf, lambda t, h: bias8[:, h, (NT - 1 - t) * P:], t, l)
                    sk = sink[:, bass.ds(l, 1), :].rearrange("p o h -> p (o h)")
                    chain.link(v.tensor_tensor(smax[:, t, :], smax[:, t, :], sk, ALU.max))
                    v.tensor_scalar(smax[:, t, :], smax[:, t, :], -1.0, None, ALU.mult).then_inc(att2["negmax"], 1)
                    dve.wait_ge(att2["negmax"], l * NT + (t + 1))
                    v.tensor_tensor(ssink[:, t, :], smax[:, t, :], sk, ALU.add).then_inc(att2["sink_in"], 1)
                    low_to(16 + 2 * t, l)
                for t in range(NT):
                    dve.wait_ge(vn_std, l * NT + (t + 1))
                    chain.link(v.reciprocal(mv[:, t, 1:2], mv[:, t, 1:2]))
                    chain.link(v.tensor_scalar(vg[:, t, :], vg[:, t, :], mv[:, t, 0:1], mv[:, t, 1:2], ALU.subtract, ALU.mult))
                    chain.link(v.tensor_tensor(vg[:, t, :], vg[:, t, :], lnv[:, bass.ds(l, 1), 0, :].rearrange("p o f -> p (o f)"), ALU.mult))
                    v.tensor_tensor(vg[:, t, :], vg[:, t, :], lnv[:, bass.ds(l, 1), 1, :].rearrange("p o f -> p (o f)"), ALU.add) \
                        .then_inc(vn_ready, 1)
                low_to(26, l)
                for t in range(NT):
                    dve.wait_ge(att2["sink_exp"], l * NT + (t + 1))
                    chain.link(v.tensor_tensor(ssum[:, t, :], ssum[:, t, :], ssink[:, t, :], ALU.add))
                    over_sums(att2, ytok2, t, l).then_inc(att2["y_ready"], 1)
                low_to(28, l)
                taken(8 + 8)
                chain.link(v.tensor_tensor(ug.rearrange("p c t -> p (c t)"), ug.rearrange("p c t -> p (c t)"), zg.rearrange("p c t -> p (c t)"), ALU.mult))
                low_to(32, l)
                taken(8 + 12)
                for t in range(NT):
                    ts = slice(t * P, (t + 1) * P)
                    dve.wait_ge(att2["y_turned"], l * NT + (t + 1))
                    v.tensor_tensor(ya2T[:, :, ts], aux[:, 2 + t, :].rearrange("p (c q) -> p c q", q=P), za[:, :, ts], ALU.mult) \
                        .then_inc(att2["y_done"], 1)
                for t in range(NT):
                    ts = slice(t * P, (t + 1) * P)
                    dve.wait_ge(mixed, l * NT + (t + 1))
                    v.tensor_tensor(ug[:, :, ts], aux[:, 4 + t, :].rearrange("p (c q) -> p c q", q=P), ug[:, :, ts], ALU.mult) \
                        .then_inc(yg_ready, 1)
                low_to(LO_2.index("p"), l)
                for c in range(2 * HC):
                    dve.wait_ge(y_hi, l * 2 * HC + (c + 1))
                    v.tensor_tensor(xl[:, c, :], (ya2T if c < HC else ug)[:, c % HC, :], full(xh[:, c, :]), ALU.subtract).then_inc(y_split, 1)
                taken(A2)
                for c in range(2 * KC):
                    m = A2 + c
                    chunk_wait(dve, m, l)
                    gate_ = (sga if c < KC else sgg)[:, c % KC, :]
                    v.tensor_tensor(gate_, chunk_out(m, l), gate_, ALU.mult).then_inc(taken_dve, 1)
                    if c >= KC:
                        dve.wait_ge(taken_dve, l * D2 + (D1 + c + 1))
                        v.tensor_tensor(sga[:, c % KC, :], sga[:, c % KC, :], gate_, ALU.add).then_inc(gated, 1)
                    if KC + 2 <= c < KC + 2 + HC:
                        merged_low(c - KC - 2)
                for c in range(HC, KC):
                    merged_low(c)
                lowered[0] = LO_2.rindex("p") + 1
                for c in range(KC):
                    if c in (2, 4):
                        low_to(58 + c, l)
                    m = A2 + 2 * KC + c
                    dve.wait_ge(xb_ready, l * KC + (c + 1))
                    chunk_wait(dve, m, l)
                    v.scalar_tensor_tensor(res[:, c, :], chunk_out(m, l), col(BOUT + c), xb[:, c, :], ALU.add, ALU.add).then_inc(taken_dve, 1)
                dve.wait_ge(means, l + 1)
                for c in range(KC):
                    v.tensor_tensor(res[:, c, :], res[:, c, :], aux[:, 0, 0:T], ALU.subtract).then_inc(centred, 1)
                dve.wait_ge(ln_std, l + 1)
                chain.link(v.reciprocal(rstd[:, :], rstd[:, :]))
                for c in range(KC):
                    v.scalar_tensor_tensor(res[:, c, :], res[:, c, :], col(LNG + c), rstd[:, :], ALU.mult, ALU.mult).then_inc(ln_scaled, 1)
            chain.leave(LAYERS)


def kernel(**inputs):
    import numpy as np
    import concourse.bacc as bacc
    from concourse.bass_utils import run_bass_kernel_spmd

    x = {k: np.ascontiguousarray(z) for k, z in inputs.items()}

    def units(plan, w):
        out = []
        for name, at, width, chunks in plan:
            z = w[name][:, at:at + width]
            out.append(z.reshape(chunks, P, width).transpose(1, 0, 2).reshape(P, chunks * width))
        return np.concatenate(out, 1)

    def col(z):
        return z.reshape(-1, P).T

    w_in = x["w_in"]
    part = {n: w_in[:, 512 * i:512 * i + 512] for i, n in enumerate(["q", "k", "v", "cb", "cc", "cx", "iq"])}
    ik, iw = w_in[:, 3584:3648], w_in[:, 3648:3656]
    w2, b2 = x["w_in_2"], x["b_in_2"]
    order = np.concatenate([np.arange(64) + 64 * h for c in range(4) for h in (c, c + 4)])
    order1 = np.concatenate([np.arange(DH) + DH * head1(h) for h in range(HEADS)])
    at2 = dict(k=512, v=640, za=768, ug=1280, vg=1792, zg=2304, ga=2816, gg=3840, end=4864)

    def cut(z, n, width):
        return z[..., at2[n]:at2[n] + width]

    arrays = {
        "xT": x["x"][0].T.reshape(KC, P, T),
        "c": x["c"],
        "w_ada": x["w_ada"].T.reshape(ADA_TILES, P, D),
        "w1": units(UNITS_1, part | {
            "idx": np.concatenate([ik, ik, iw], 1), "out": np.concatenate([x["w_out"][:512][order1], x["w_out"][512:]]),
            "wq": x["peer_wq"],
            "sub": x["peer_subkeys"].reshape(2 * EXPERT_HEADS, KEYS, P).transpose(2, 0, 1).reshape(P, -1)}),
        "peer_u": x["peer_u"],
        "peer_v": x["peer_v"],
        "cols": np.concatenate([col(x["norm1_w"]), col(x["norm2_w"]), col(x["b_ada"]), col(x["conv_w"].reshape(-1)), col(x["conv_b"]),
                                col(x["attn_out_norm_w"][order1]), col(x["conv_out_norm_w"]),
                                col(np.concatenate([x["q_norm_w"]] * 2)), col(np.concatenate([x["k_norm_w"]] * 2))], 1),
        "w2": np.stack([units(UNITS_2, {n: cut(w2[l], n, z) for n, z in dict(k=P, v=P, vg=512, ug=512, zg=512, za=512, ga=D, gg=D).items()} | {
            "q": w2[l][:, order], "ba": x["w_branch_attn_2"][l], "bg": x["w_branch_gmlp_2"][l], "out": x["w_out_2"][l]}) for l in range(LAYERS)]),
        "wsT": x["w_spatial_2"].reshape(LAYERS * 4, P, P).transpose(0, 2, 1),
        "lnv": np.stack([x["gmlp_ln_g_2"], x["gmlp_ln_b_2"]], 1).reshape(1, -1),
        "brow": np.concatenate([cut(b2, "v", 128), cut(b2, "vg", 512), x["b_spatial_2"].reshape(LAYERS, -1)], 1).reshape(1, -1),
        "sink": x["attn_sinks_2"].reshape(1, -1),
        "lcol": np.stack([np.concatenate([col(z) for z in (b2[l][order], b2[l][512:640], cut(b2[l], "ug", 512), cut(b2[l], "zg", 512),
                                                           cut(b2[l], "za", 512), cut(b2[l], "ga", D), cut(b2[l], "gg", D),
                                                           x["b_out_2"][l], x["ln_g_2"][l], x["ln_b_2"][l])], 1)
                          for l in range(LAYERS)], 1),
    }
    nc = bacc.Bacc("TRN2", target_bir_lowering=False, num_devices=1)
    aps = {}
    for name, z in arrays.items():
        arrays[name] = z = np.ascontiguousarray(z)
        aps[name] = nc.dram_tensor("in_" + name, z.shape, mybir.dt.from_np(z.dtype), kind="ExternalInput").ap()
    out = nc.dram_tensor("out_T", (KC, P, T), F32, kind="ExternalOutput").ap()
    build(nc, aps, out)
    done = run_bass_kernel_spmd(nc, [{"in_" + n: z for n, z in arrays.items()}], core_ids=[0])
    return done.results[0]["out_T"].reshape(D, T).T.reshape(1, T, D)
```

```python
from collections import namedtuple
from contextlib import ExitStack

import concourse.bass as bass
from concourse import mybir

ALU = mybir.AluOpType
ACT = mybir.ActivationFunctionType
AX = mybir.AxisListType.X
F32 = mybir.dt.float32
F32R = mybir.dt.float32r
I32 = mybir.dt.int32
U32 = mybir.dt.uint32

P = 128
T = 256
NT = T // P
D = 1024
KC = D // P
HEADS, DH = 8, 64
HC = HEADS * DH // P
TOPK = 64
IDX_SCALE = (64 ** -0.5) * (8 ** -0.5)
ATT_SCALE = DH ** -0.5
EXPERT_HEADS, KEYS, PICKS = 8, 128, 16
LAYERS = 2
ALPHA = (2 * LAYERS) ** 0.25
RMS_EPS, LN_EPS = 1e-6, 1e-5
LOW = -3.0e38
MASKED = -1.0e30

RING = 4
PRING = 4
WUNIT = KC * 256
WPIECE = KC * P
ADA_RING = 5
UNIT_0_AFTER = 12
ADA_TILES = 6 * D // P
ROWS = 8
U_LEAD = 3
ROUTE_AT = 8

N1W, N2W, B_ADA, CONV_W, CONV_B, ATT_W, CNV_W, Q_W, K_W, COLS = 0, 8, 16, 64, 76, 80, 84, 88, 89, 90
BQ, BK, BUG, BZG, BZA, BGA, BGG, BOUT, LNG, LNB, LCOLS = 0, 4, 5, 9, 13, 17, 25, 33, 41, 49, 57
RV, RVG, RSP, LROWS = 0, 128, 640, 1152

def halves(name, n=512, chunks=KC, width=256):
    return [(name, at, min(width, n - at), chunks) for at in range(0, n, width)]


UNITS_1 = halves("iq") + [("idx", 0, 136, KC)]
for name in ("q", "k", "v", "cc", "cx", "cb"):
    UNITS_1 += halves(name)
UNITS_1 += halves("out", D)
MIX_UNITS = len(UNITS_1)



def queries_of(h):
    return ("wq", h * 2 * KEYS, 2 * KEYS, KC)


def keys_of(h):
    return ("sub", h * 2 * KEYS, 4 * KEYS, 1)


PARKED = (2, 3, 4)
UNITS_1 += [queries_of(0), queries_of(1), keys_of(0), keys_of(2), queries_of(5), queries_of(6), keys_of(4), keys_of(6), queries_of(7)]
UNITS_2 = halves("q") + [("k", 0, P, KC), ("v", 0, P, KC)] + halves("vg") + halves("ug") + halves("zg") + halves("za") + \
    halves("ga", D) + halves("gg", D) + halves("ba", D, HC) + halves("bg", D, HC) + halves("out", D)
N1, N2 = len(UNITS_1), len(UNITS_2)
ALL_UNITS_1 = UNITS_1 + [queries_of(h) for h in PARKED]
Piece = namedtuple("Piece", "unit column chunks place")


def pieces(units):
    out, place = [], 0
    for n, (name, at, width, chunks) in enumerate(units):
        for j in range(width // P):
            out.append(Piece(n, j * P, chunks, place))
            place += 1
        place += name == "idx"
    return out, -(-place // PRING) * PRING


ADA_AFTER = {3: range(16, 21), 6: (21, 22), 7: (23, 24), 8: (25, 26), 9: (27, 28), 18: range(29, 34), 22: range(40, 48)}
ADA_AFTER_PARKED = range(34, 40)
PIECES_1, SPAN_1 = pieces(UNITS_1[:MIX_UNITS])
PIECES_2, SPAN_2 = pieces(UNITS_2)
LO_1 = "d" * 4 + "p" * 17 + "d" * 16
HI_2 = "paap" + "a" * 10 + "pa" * 4 + "a" * 40
LO_2 = "p" + "d" * 37 + "p" * 20 + "d" * 4
assert len(LO_1) == len(PIECES_1) and len(LO_2) == len(PIECES_2)


def ada_column(n):
    return n if n >= 2 * KC else n // 2 + (KC if n % 2 == 0 else 0)


def starts(units):
    at = [0]
    for _, _, width, chunks in units:
        at.append(at[-1] + width * chunks)
    return at


AT_1, AT_2 = starts(ALL_UNITS_1), starts(UNITS_2)
SHARED = 6
EARLY_HEADS = 6
ROUTE_STEPS = 24
LAYER_STEPS = 32
assert N2 % RING == 0


def head1(h):
    return 2 * (h % 4) + h // 4


class Chain:

    def __init__(self, eng, sem, spare=None):
        self.eng, self.sem, self.base, self.n, self.spare = eng, sem, 0, 0, spare

    def mark(self, ins):
        self.n += 1
        ins.then_inc(self.sem, 1)

    def wait(self, back=0):
        self.eng.wait_ge(self.sem, self.base + self.n - back)
        if self.spare is not None:
            self.eng.sem_inc(self.spare)

    def link(self, ins):
        self.mark(ins)
        self.wait()

    def enter(self, i, per):
        self.start = self.base + self.n
        self.base, self.n, self.per = i * per + self.start, 0, per

    def leave(self, trips):
        assert self.n == self.per, (self.n, self.per)
        self.base, self.n, self.spare = self.start + trips * self.per, 0, None


def build(nc, a, out):
    ctx = ExitStack()
    with ctx:
        def sb(name, shape, dt=F32):
            return ctx.enter_context(nc.sbuf_tensor(name, shape, dt))

        def sem(name):
            return ctx.enter_context(nc.semaphore(name))

        wring = sb("wring", [P, RING, WUNIT])
        whi = sb("whi", [P, PRING, WPIECE], F32R)
        wlo = sb("wlo", [P, PRING, WPIECE], F32R)
        xh = sb("xh", [P, KC, T], F32R)
        xl = sb("xl", [P, KC, T], F32R)
        rows = sb("rows", [P, 2 * ROWS, D])
        xT = sb("xT", [P, KC, T])
        hT = sb("hT", [P, KC, T])
        work = sb("work", [P, 8192])
        wsT = sb("wsT", [P, LAYERS * 4, P])
        pq = sb("pq", [P, 2, 2, T])
        sink = sb("sink", [P, LAYERS, HEADS])
        cols = sb("cols", [P, COLS])
        lcol = sb("lcol", [P, LAYERS, LCOLS])
        mod = sb("mod", [P, 48])
        gain = sb("gain", [P, KC])
        eps = sb("eps", [P, 2])
        ident = sb("ident", [P, P])
        ones = sb("ones", [P, P])
        mean = sb("mean", [P, P])
        zeros = sb("zeros", [P, P])
        blk = sb("blk", [P, P])
        rstd = sb("rstd", [P, T])
        smax = sb("smax", [P, NT, HEADS])
        ssum = sb("ssum", [P, NT, HEADS])
        ssink = sb("ssink", [P, NT, HEADS])
        warm = sb("warm", [P, 1])
        ystat = sb("ystat", [P, NT, 2])
        top8 = sb("top8", [P, NT, 8])
        bn = sb("bn", [P, NT, 6])
        mv = sb("mv", [P, NT, 2])

        flat = rows[:, :, :].rearrange("p r d -> p (r d)")

        class Area:

            def __init__(self, ap, at=0):
                self.ap, self.at = ap, at

            def take(self, n):
                self.at += n
                assert self.at <= self.ap.shape[1]
                return self.ap[:, self.at - n:self.at]

        r1 = Area(flat)
        ada = r1.take(ADA_RING * D).rearrange("p (s d) -> p s d", s=ADA_RING)
        cbc = r1.take(D)
        sq = r1.take(KC * T).rearrange("p (c t) -> p c t", t=T)
        p_buf = [r1.take(HEADS * P), r1.take(HEADS * T)]
        pt_buf = [r1.take(HEADS * P), r1.take(HEADS * T)]
        cc = r1.take(HC * T).rearrange("p (c t) -> p c t", t=T)
        ytok = r1.take(NT * 512).rearrange("p (n f) -> p n f", n=NT)
        parked = [flat[:, (ROWS + 2 * k) * D:(ROWS + 2 * k + 2) * D] for k in range(len(PARKED))]
        w1 = Area(work[:, :])
        iqT = w1.take(HC * T).rearrange("p (c t) -> p c t", t=T)
        ikT = w1.take(T)
        iw = w1.take(NT * HEADS).rearrange("p (n h) -> p n h", n=NT)
        qn = w1.take(HC * T).rearrange("p (c t) -> p c t", t=T)
        kn = w1.take(HC * T).rearrange("p (c t) -> p c t", t=T)
        v1 = w1.take(NT * 512).rearrange("p (n f) -> p n f", n=NT)
        score = [w1.take(P), w1.take(T)]
        left = [w1.take(P), w1.take(T)]
        keep = [w1.take(P), w1.take(T)]
        u = w1.take(HC * (T + 2)).rearrange("p (c t) -> p c t", t=T + 2)
        cb = w1.take(HC * T).rearrange("p (c t) -> p c t", t=T)
        yaT = iqT
        relu = p_buf
        w2 = Area(work[:, :])
        w2.take(4096)
        s_all = w2.take(NT * EXPERT_HEADS * 2 * KEYS).rearrange("p (g k) -> p g k", k=2 * KEYS)
        w3 = Area(work[:, :])
        diag = w3.take(PICKS * P).rearrange("p (j q) -> p j q", q=P)
        s_cur = w3.take(2 * KEYS).rearrange("p (s k) -> p s k", s=2)
        s_left = w3.take(2 * KEYS).rearrange("p (s k) -> p s k", s=2)
        half_top = w3.take(2 * PICKS).rearrange("p (s k) -> p s k", s=2)
        half_idx = w3.take(2 * PICKS).bitcast(U32).rearrange("p (s k) -> p s k", s=2)
        combo = w3.take(PICKS * PICKS)
        combo_left = w3.take(PICKS * PICKS)
        top = w3.take(PICKS)
        pos = w3.take(PICKS).bitcast(U32)
        place = w3.take(2 * PICKS).bitcast(U32).rearrange("p (s k) -> p s k", s=2)
        hit = w3.take(2 * PICKS * PICKS).rearrange("p (s k n) -> p s k n", s=2, n=PICKS)
        picked = w3.take(2 * PICKS).rearrange("p (s k) -> p s k", s=2)
        expert = [w3.take(PICKS).bitcast(I32) for _ in range(2)]
        negtop = w3.take(1)
        gate = w3.take(PICKS)
        gate_sum = w3.take(1)
        gate_inv = w3.take(1)
        dots = w3.take(PICKS)
        act_dots = w3.take(PICKS)
        weight = w3.take(PICKS)
        assert w3.at <= 4096
        count16 = sb("count16", [P, PICKS], I32)
        peer_tok = pq[:, :, :, :].rearrange("p h s t -> p (h s t)")
        r4 = Area(flat)
        qT = r4.take(HC * T).rearrange("p (c t) -> p c t", t=T)
        kT = r4.take(T)
        v2 = r4.take(NT * P).rearrange("p (n f) -> p n f", n=NT)
        vg = r4.take(NT * 512).rearrange("p (n f) -> p n f", n=NT)
        p2 = r4.take(HEADS * (P + T))
        p2_buf = [p2[:, 0:HEADS * P], p2[:, HEADS * P:]]
        pt2 = r4.take(HEADS * (P + T))
        pt2_buf = [pt2[:, 0:HEADS * P], pt2[:, HEADS * P:]]
        za = r4.take(HC * T).rearrange("p (c t) -> p c t", t=T)
        ug = r4.take(HC * T).rearrange("p (c t) -> p c t", t=T)
        zg = r4.take(HC * T).rearrange("p (c t) -> p c t", t=T)
        ytok2 = r4.take(NT * 512).rearrange("p (n f) -> p n f", n=NT)
        sgg = p2[:, 0:KC * T].rearrange("p (c t) -> p c t", t=T)
        brow = r4.take(LAYERS * LROWS)[0:1].rearrange("o (l n) -> o l n", l=LAYERS)
        ya2T = qT
        sga = hT
        w4 = Area(work[:, :])
        xb = w4.take(KC * T).rearrange("p (c t) -> p c t", t=T)
        res = w4.take(KC * T).rearrange("p (c t) -> p c t", t=T)
        bias8 = w4.take(HEADS * T).rearrange("p (h k) -> p h k", k=T)
        sq2 = pt2[:, 0:KC * T].rearrange("p (c t) -> p c t", t=T)
        lnv = w4.take(LAYERS * 2 * 512).rearrange("p (l k f) -> p l k f", l=LAYERS, k=2)
        distance = rstd[:, :].bitcast(I32)

        def full(ap):
            return ap.bitcast(F32)

        pj = ctx.enter_context(nc.psum_tensor("pj", [P, 2, 512], F32))
        aux = ctx.enter_context(nc.psum_tensor("aux", [P, 6, 512], F32))
        h2_tok = [pj[:, :, :].rearrange("p b n -> p (b n)"), aux[:, 0:2, :].rearrange("p b n -> p (b n)")]

        x_loaded, c_loaded, cols_loaded, par_loaded = sem("x_loaded"), sem("c_loaded"), sem("cols_loaded"), sem("par_loaded")
        w_loaded = [sem(f"w_loaded{s}") for s in range(RING)]
        parked_loaded = [sem(f"parked_loaded{k}") for k in range(len(PARKED))]
        ada_loaded = [sem(f"ada_loaded{s}") for s in range(ADA_RING)]
        ada_used = sem("ada_used")
        pool_chain, dve_chain, act_chain = sem("pool_chain"), sem("dve_chain"), sem("act_chain")
        pool_spare, dve_spare, sp_spare = sem("pool_spare"), sem("dve_spare"), sem("sp_spare")
        const_ready = sem("const_ready")
        c_silu = sem("c_silu")
        squares = sem("squares")
        sums = sem("sums")
        h_weighted, rstd_ready, mod_ready = sem("h_weighted"), sem("rstd_ready"), sem("mod_ready")
        std_ready = sem("std_ready")
        h_ready = sem("h_ready")
        h_scaled = sem("h_scaled")
        proj = sem("proj")
        w_hi = {"a": sem("w_hi_act"), "p": sem("w_hi_pool")}
        w_lo = {"d": sem("w_lo_dve"), "p": sem("w_lo_pool")}
        h_split, mix_hi, mix_split = sem("h_split"), sem("mix_hi"), sem("mix_split")
        xh_ready, x_split = sem("xh_ready"), sem("x_split")
        y_hi, y_split, merged_hi, merged_split = sem("y_hi"), sem("y_split"), sem("merged_hi"), sem("merged_split")
        taken_act, taken_dve = sem("taken_act"), sem("taken_dve")
        idx_raw, idx_relu, idx_score, idx_causal, keep_ready = (
            sem("idx_raw"), sem("idx_relu"), sem("idx_score"), sem("idx_causal"), sem("keep_ready"))
        qk_sq, qk_sum, qk_std, qk_ready = sem("qk_sq"), sem("qk_sum"), sem("qk_std"), sem("qk_ready")
        u_ready, conv_y, conv_sq, conv_sum, conv_std, conv_done = (
            sem("u_ready"), sem("conv_y"), sem("conv_sq"), sem("conv_sum"), sem("conv_std"), sem("conv_done"))

        def at(l, per, k):
            return k if l is None else l * per + k

        names = ("logits", "negmax", "probs", "p_turned", "p_out", "summed", "y_ready",
                 "y_sq", "y_std", "y_turned", "y_done", "sink_in", "sink_exp")
        att1 = {s: sem(f"att1_{s}") for s in names}
        att2 = {s: sem(f"att2_{s}") for s in names}
        queries, queries_out = sem("queries"), sem("queries_out")
        expert_scores, scores_out = sem("expert_scores"), sem("scores_out")
        late_loaded = sem("late_loaded")
        h2_turned = sem("h2_turned")
        s_taken, routed, gate_exp, dots_act, diag_ready = (
            sem("s_taken"), sem("routed"), sem("gate_exp"), sem("dots_act"), sem("diag_ready"))
        u_loaded = [sem(f"u_loaded{s}") for s in range(ROWS)]
        v_loaded = [sem(f"v_loaded{s}") for s in range(ROWS)]
        u_used, v_used = sem("u_used"), sem("v_used")
        peer_out, peer_turned, x_ready = sem("peer_out"), sem("peer_turned"), sem("x_ready")
        bias_iota, bias_lin, bias_ready = sem("bias_iota"), sem("bias_lin"), sem("bias_ready")
        vn_ready, vn_std, vn_stat = sem("vn_ready"), sem("vn_std"), sem("vn_stat")
        mixed, yg_ready, gated = sem("mixed"), sem("yg_ready"), sem("gated")
        xb_ready = sem("xb_ready")
        means, centred, centred_sq, variances, ln_std, ln_scaled = (
            sem("means"), sem("centred"), sem("centred_sq"), sem("variances"), sem("ln_std"), sem("ln_scaled"))
        stored = sem("stored")

        BANKS_1 = [2] * 3 + [2, 1, 1] + [2] * 2 + [1] * NT + [2] * 6 + [2] * 4
        BANKS_2 = [2] * 2 + [1] * 2 + [1] * NT + [2] * 6 + [2] * 8 + [2] * 12
        OWN_1 = ["a"] * (4 + 2 + 4 + 4 + NT + 4 + 4 + 4) + ["d"] * 8
        OWN_2 = ["a"] * (4 + 1 + 1 + NT + 4 + 4 + 4 + 8 + 8) + ["d"] * 24
        M1, M2 = len(OWN_1), len(OWN_2)
        assert len(BANKS_1) % 2 == 0 and len(BANKS_2) % 2 == 0

        def seats(banks):
            out, m = [], 0
            for b, n in enumerate(banks):
                out += [(b, j, m, m + n) for j in range(n)]
                m += n
            return out

        SEATS_1, SEATS_2 = seats(BANKS_1), seats(BANKS_2)
        assert len(SEATS_1) == M1 and len(SEATS_2) == M2

        def chunk_out(m, l=None, width=T):
            b, j, _, _ = (SEATS_1 if l is None else SEATS_2)[m]
            return pj[:, b % 2, j * T:j * T + width]

        def chunk_wait(eng, m, l=None):
            if l is None:
                eng.wait_ge(proj, SEATS_1[m][3])
            else:
                eng.wait_ge(proj, l * M2 + (M1 + SEATS_2[m][3]))

        def done(units, token_major):
            n, out = 0, []
            for name, at, width, _ in units:
                for j in range(width // P):
                    if name not in token_major:
                        n += 1
                        out.append(n)
                    else:
                        n += NT if at and j == 0 else 0
                        out.append(n if at else n + 1)
                n += name == "idx"
            return out

        DONE_1 = done(UNITS_1[:MIX_UNITS], ("v",))
        DONE_2 = done(UNITS_2, ("vg",))
        assert DONE_1[-1] == M1 and DONE_2[-1] == M2
        A1, D1 = OWN_1.count("a"), OWN_1.count("d")
        A2, D2 = OWN_2.count("a"), OWN_2.count("d")

        def bank_free(pe, m, l=None):
            own, at_ = (OWN_1, SEATS_1) if l is None else (OWN_2, SEATS_2)
            b, j, first, _ = at_[m]
            if j == 0 and b >= 2:
                last = at_[first - 1][2]
                who = own[last - 1]
                n = own[:last].count(who)
                taken_ = {"a": taken_act, "d": taken_dve}[who]
                if l is None:
                    pe.wait_ge(taken_, n)
                else:
                    pe.wait_ge(taken_, l * {"a": A2, "d": D2}[who] + {"a": A1, "d": D1}[who] + n)

        def w_wait(eng, n, l=None):
            if l is None:
                eng.wait_ge(w_loaded[n % RING], 16 * (n // RING + 1))
            else:
                eng.wait_ge(w_loaded[(N1 + n) % RING], l * (16 * N2 // RING) + 16 * ((N1 + n) // RING + 1))

        def w_slot(n, l=None):
            _, _, width, chunks = (UNITS_1 if l is None else UNITS_2)[n]
            s = n % RING if l is None else (N1 + n) % RING
            return wring[:, s, 0:chunks * width].rearrange("p (k n) -> p k n", n=width)

        def parts(n, l=None):
            piece = (PIECES_1 if l is None else PIECES_2)[n]
            return [z[:, piece.place % PRING, 0:piece.chunks * P].rearrange("p (k n) -> p k n", n=P) for z in (whi, wlo)]

        def part_pairs(n):
            def at_(k, l):
                s = (PIECES_1 if l is None else PIECES_2)[n].place % PRING
                return [z[:, s:s + 2, k * P:(k + 1) * P] for z in (whi, wlo)]
            return at_

        def piece_of_unit(n, l=None):
            piece = (PIECES_1 if l is None else PIECES_2)[n]
            return w_slot(piece.unit, l)[:, :, piece.column:piece.column + P]

        def split_hi(eng, n, l=None):
            plan, span = (PIECES_1, 0) if l is None else (PIECES_2, SPAN_2)
            if plan[n].column == 0 or (l is not None and HI_2[n - 1] != HI_2[n]):
                w_wait(eng, plan[n].unit, l)
            before = [k for k, z in enumerate(plan) if z.place <= plan[n].place - PRING]
            if before:
                if l is None:
                    eng.wait_ge(proj, DONE_1[before[-1]])
                else:
                    eng.wait_ge(proj, l * M2 + (M1 + DONE_2[before[-1]]))
            elif l is not None:
                last = [k for k, z in enumerate(plan) if z.place <= plan[n].place - PRING + span][-1]
                eng.wait_ge(proj, l * M2 + (M1 + DONE_2[last] - M2))
            if l is None or HI_2[n] == "a":
                nc.scalar.copy(parts(n, l)[0], piece_of_unit(n, l)).then_inc(w_hi["a"], 1)
            else:
                eng.sem_inc(pool_spare)
                eng.tensor_copy(parts(n, l)[0], piece_of_unit(n, l)).then_inc(w_hi["p"], 1)

        def split_lo(eng, who, n, l=None):
            assert (LO_1 if l is None else LO_2)[n] == who
            if l is None:
                eng.wait_ge(w_hi["a"], n + 1)
            else:
                by = HI_2[n]
                eng.wait_ge(w_hi[by], l * HI_2.count(by) + ((len(LO_1) if by == "a" else 0) + HI_2[:n + 1].count(by)))
            hi, lo = parts(n, l)
            eng.tensor_tensor(lo, piece_of_unit(n, l), full(hi), ALU.subtract).then_inc(w_lo[who], 1)

        def split_wait(eng, n, l=None):
            if l is None:
                eng.wait_ge(w_lo[LO_1[n]], LO_1[:n + 1].count(LO_1[n]))
            else:
                who = LO_2[n]
                eng.wait_ge(w_lo[who], l * LO_2.count(who) + (LO_1.count(who) + LO_2[:n + 1].count(who)))

        def last_piece(u, plan):
            return max(n for n, z in enumerate(plan) if z.unit == u)

        def q1(h, t):
            return qn[64 * (h // 4):64 * (h // 4) + 64, h % 4, t * P:(t + 1) * P]

        def k1(h, s):
            return kn[64 * (h // 4):64 * (h // 4) + 64, h % 4, 0:s]

        def q2(h, t):
            return qT[64 * (h // 4):64 * (h // 4) + 64, h % 4, t * P:(t + 1) * P]

        def k2(h, s):
            return kT[64 * (h // 4):64 * (h // 4) + 64, 0:s]

        def probs(buf, t, h):
            s = (t + 1) * P
            return buf[t][:, h * s:(h + 1) * s]

        def probs_T(buf, t, s):
            return buf[t][:, s * HEADS * P:(s + 1) * HEADS * P].rearrange("p (h q) -> p h q", q=P)

        def logit_bank(t, h):
            return aux[:, h // 4, (h % 4) * P:(h % 4 + 1) * P] if t == 0 else \
                aux[:, 2 + h // 2, (h % 2) * T:(h % 2 + 1) * T]

        block = ctx.enter_context(nc.Block())

        @block.sync
        def _(sp):
            sp.dma_start(xT[:, :, :], a["xT"].rearrange("c p t -> p c t")).then_inc(x_loaded, 16)

            def load_ada(n):
                if n >= ADA_RING:
                    sp.wait_ge(ada_used, n - ADA_RING + 1)
                sp.dma_start(ada[:, n % ADA_RING, :], a["w_ada"][ada_column(n)]).then_inc(ada_loaded[n % ADA_RING], 16)

            def load_unit(n):
                sp.dma_start(wring[:, n % RING, 0:AT_1[n + 1] - AT_1[n]], a["w1"][:, AT_1[n]:AT_1[n + 1]]).then_inc(w_loaded[n % RING], 16)

            for n in range(2 * KC):
                load_ada(n)
                if n == UNIT_0_AFTER - 1:
                    load_unit(0)
            for n, (name, at, width, chunks) in enumerate(UNITS_1):
                if n >= RING:
                    was = n - RING
                    if was < MIX_UNITS:
                        split_wait(sp, last_piece(was, PIECES_1))
                        if UNITS_1[was][0] == "idx":
                            sp.wait_ge(proj, DONE_1[last_piece(was, PIECES_1)] + 1)
                    elif UNITS_1[was][0] == "wq":
                        sp.wait_ge(queries, UNITS_1[was][1] // P + 2)
                    else:
                        sp.wait_ge(expert_scores, UNITS_1[was][1] // (2 * KEYS) + 2)
                if n:
                    load_unit(n)
                for k in ADA_AFTER.get(n, ()):
                    load_ada(k)
                if n == MIX_UNITS - 1:
                    sp.wait_ge(mix_split, NT + HC)
                    for k in range(len(PARKED)):
                        sp.dma_start(parked[k], a["w1"][:, AT_1[N1 + k]:AT_1[N1 + k + 1]]).then_inc(parked_loaded[k], 16)
                    for k in ADA_AFTER_PARKED:
                        load_ada(k)
            sp.wait_ge(queries, 2 * EXPERT_HEADS)
            sp.wait_ge(expert_scores, EXPERT_HEADS)
            with sp.Fori(0, LAYERS) as l:
                for n, (name, at, width, chunks) in enumerate(UNITS_2):
                    slot = (N1 + n) % RING
                    if n == 1:
                        sp.wait_ge(v_loaded[ROWS - 1], 16 * NT * EXPERT_HEADS * PICKS // ROWS)
                        sp.sem_inc(sp_spare)
                    if n >= RING:
                        last = last_piece(n - RING, PIECES_2)
                        if last and PIECES_2[last - 1].unit == n - RING and LO_2[last - 1] != LO_2[last]:
                            split_wait(sp, last - 1, l)
                            sp.sem_inc(sp_spare)
                        split_wait(sp, last, l)
                    else:
                        k = last_piece(n - RING + N2, PIECES_2)
                        who = LO_2[k]
                        sp.wait_ge(w_lo[who], l * LO_2.count(who) + (LO_1.count(who) - LO_2[k + 1:].count(who)))
                    sp.dma_start(wring[:, slot, 0:width * chunks],
                                 a["w2"][bass.ds(l, 1), :, AT_2[n]:AT_2[n + 1]].rearrange("o p n -> (o p) n")).then_inc(w_loaded[slot], 16)
            sp.wait_ge(x_ready, KC * (1 + LAYERS))
            sp.dma_start(out.rearrange("c p t -> p c t"), xT[:, :, :]).then_inc(stored, 16)
            sp.wait_ge(stored, 16)

        @block.gpsimd
        def _(pool):
            chain = Chain(pool, pool_chain)
            spare = pool_spare
            pool.memset(eps[:, 0:1], RMS_EPS).then_inc(const_ready, 1)
            pool.memset(eps[:, 1:2], LN_EPS).then_inc(const_ready, 1)
            pool.memset(ones[:, :], 1.0).then_inc(const_ready, 1)
            pool.memset(zeros[:, 0:1], 0.0).then_inc(u_used, ROWS)
            pool.memset(zeros[:, 1:], 0.0).then_inc(v_used, ROWS)

            pool.memset(mean[:, :], 1.0 / D).then_inc(const_ready, 1)
            chain.link(pool.memset(ident[:, :], 0.0))
            pool.affine_select(out=ident[:, :], in_=ident[:, :], compare_op=ALU.not_equal, fill=1.0, base=0,
                               pattern=[[-1, P]], channel_multiplier=1).then_inc(const_ready, 1)
            chain.link(pool.memset(blk[:, :], 1.0))
            pool.affine_select(out=blk[:, 0:DH], in_=blk[:, 0:DH], compare_op=ALU.is_ge, fill=0.0, base=DH - 1,
                               pattern=[[0, DH]], channel_multiplier=-1).then_inc(const_ready, 1)
            pool.affine_select(out=blk[:, DH:], in_=blk[:, DH:], compare_op=ALU.is_ge, fill=0.0, base=-DH,
                               pattern=[[0, DH]], channel_multiplier=1).then_inc(const_ready, 1)
            pool.iota(count16[:, :], pattern=[[1, PICKS]], base=0, channel_multiplier=0).then_inc(const_ready, 1)
            pool.memset(u[:, :, 0:2], 0.0).then_inc(const_ready, 1)
            pool.wait_ge(rstd_ready, 1)
            for c in range(KC):
                pool.wait_ge(h_weighted, c + 1)
                pool.tensor_tensor(hT[:, c, :], hT[:, c, :], rstd[:, :], ALU.mult).then_inc(h_scaled, 1)
            for n in range(4, 12):
                split_lo(pool, "p", n)
            for t in range(NT):
                pool.wait_ge(idx_score, t + 1)
                pool.affine_select(out=score[t], in_=score[t], compare_op=ALU.is_ge, fill=LOW, base=t * P,
                                   pattern=[[-1, (t + 1) * P]], channel_multiplier=1).then_inc(idx_causal, 1)
                split_lo(pool, "p", 12 + t)
            for n in range(14, LO_1.rindex("p") + 1):
                split_lo(pool, "p", n)
            pool.wait_ge(par_loaded, 48)
            pool.affine_select(out=wsT[:, :, :], in_=wsT[:, :, :], compare_op=ALU.is_ge, fill=0.0, base=0,
                               pattern=[[0, LAYERS * 4], [1, P]], channel_multiplier=-1).then_inc(const_ready, 1)
            base = 4 + 2 + 4 + 4 + NT
            for c in range(HC):
                pool.wait_ge(taken_act, base + 4 + c + 1)
                pool.tensor_tensor(u[:, c, 2:], u[:, c, 2:], cc[:, c, :], ALU.mult).then_inc(u_ready, 1)
            def gather(which, par, i, j):
                table, at, loaded, used = (a["peer_u"], 0, u_loaded, u_used) if which == "u" else (a["peer_v"], ROWS, v_loaded, v_used)
                if which == "v" and j < 2 * len(PARKED):
                    pool.wait_ge(queries, 2 * PARKED[j // 2] + 2)
                pool.wait_ge(used, i * (2 * PICKS) + (par * PICKS + j + 1))
                pool.sem_inc(spare)
                pool.indirect_dma_start(
                    out=rows[:, at + j % ROWS, :], out_offset=None, in_=table,
                    in_offset=bass.IndirectOffsetOnAxis(ap=expert[par % 2][:, j:j + 1], axis=0)) \
                    .then_inc(loaded[j % ROWS], 16)

            def picked_rows(par, i, more=True):
                for j in range(ROWS):
                    gather("v", par, i, j)
                if more:
                    pool.wait_ge(routed, 2 * i + (par + 2))
                    pool.sem_inc(spare)
                for k in range(PICKS):
                    if more:
                        gather("u", par + 1, i, k)
                    if 0 <= k - U_LEAD + 1 < PICKS - ROWS:
                        gather("v", par, i, ROWS + k - U_LEAD + 1)

            pool.wait_ge(routed, 1)
            for j in range(PICKS):
                gather("u", 0, 0, j)
            pairs = NT * EXPERT_HEADS // 2
            with pool.Fori(0, pairs - 1) as i:
                for par in range(2):
                    picked_rows(par, i)
            picked_rows(0, pairs - 1)
            pool.wait_ge(s_taken, NT * EXPERT_HEADS)
            pool.iota(distance, pattern=[[-1, T]], base=P, channel_multiplier=1).then_inc(bias_iota, 1)
            picked_rows(1, pairs - 1, more=False)
            pool.wait_ge(bias_lin, HEADS)
            chain.link(pool.affine_select(out=bias8[:, :, :], in_=bias8[:, :, :], compare_op=ALU.is_ge, fill=MASKED,
                                          base=P, pattern=[[0, HEADS], [-1, T]], channel_multiplier=1))
            pool.affine_select(out=bias8[:, :, :], in_=bias8[:, :, :], compare_op=ALU.is_ge, fill=MASKED,
                               base=-1, pattern=[[0, HEADS], [1, T]], channel_multiplier=-1).then_inc(bias_ready, 1)
            with pool.Fori(0, LAYERS) as l:
                split_hi(pool, 0, l)
                split_lo(pool, "p", 0, l)
                split_hi(pool, 3, l)
                pool.wait_ge(x_ready, l * KC + KC)
                pool.wait_ge(taken_dve, l * D2 + D1)
                pool.sem_inc(spare)
                for c in range(KC):
                    ins = pool.tensor_scalar(xb[:, c, :], xT[:, c, :], ALPHA, None, ALU.mult)
                    ins.then_inc(xb_ready, 1)
                for n in range(14, 22, 2):
                    split_hi(pool, n, l)
                for n in range(38, 58):
                    split_lo(pool, "p", n, l)

        @block.scalar
        def _(act):
            chain = Chain(act, act_chain)
            act.dma_start(cbc, a["c"].partition_broadcast(P).rearrange("p o d -> p (o d)")).then_inc(c_loaded, 16)
            act.dma_start(cols[:, :], a["cols"]).then_inc(cols_loaded, 16)
            act.wait_ge(c_loaded, 16)
            nc.scalar.activation(cbc, cbc, ACT.Silu).then_inc(c_silu, 1)

            act.wait_ge(x_loaded, 16)
            for c in range(KC):
                nc.scalar.activation(sq[:, c, :], xT[:, c, :], ACT.Square).then_inc(squares, 1)
            act.wait_ge(cols_loaded, 16)
            for c in range(KC):
                nc.scalar.activation(hT[:, c, :], xT[:, c, :], ACT.Copy, scale=cols[:, N1W + c:N1W + c + 1]).then_inc(h_weighted, 1)
            act.wait_ge(const_ready, 2)
            act.wait_ge(sums, 1)
            nc.scalar.activation(rstd[:, :], aux[:, 0, 0:T], ACT.Sqrt, bias=eps[:, 0:1], scale=1.0 / D).then_inc(std_ready, 1)
            rounded = [0]

            def round_to(n, l=None):
                for k in range(rounded[0], n):
                    if l is None or HI_2[k] == "a":
                        split_hi(act, k, l)
                rounded[0] = n

            for c in range(KC):
                if 2 * c == UNIT_0_AFTER:
                    round_to(2)
                act.wait_ge(h_scaled, c + 1)
                act.wait_ge(mod_ready, 2 * c + 2)
                for h in (xh, hT):
                    ins = nc.scalar.activation(h[:, c, :], hT[:, c, :], ACT.Identity, bias=mod[:, c:c + 1], scale=gain[:, c:c + 1])
                ins.then_inc(h_ready, 1)
            round_to(PRING)
            act.dma_start(wsT[:, :, :], a["wsT"].rearrange("g s t -> s g t")).then_inc(par_loaded, 16)
            act.dma_start(sink[:, :, :].rearrange("p l h -> p (l h)"),
                          a["sink"].partition_broadcast(P).rearrange("p o d -> p (o d)")).then_inc(par_loaded, 16)
            act.dma_start(lcol[:, :, :], a["lcol"]).then_inc(par_loaded, 16)

            taken = [0]

            def take(dst, func=ACT.Copy, l=None, width=T, sq_to=None, **kw):
                m = taken[0]
                taken[0] += 1
                chunk_wait(act, m, l)
                if sq_to is not None:
                    nc.scalar.activation(sq_to, chunk_out(m, l, width), ACT.Square).then_inc(qk_sq, 1)
                nc.scalar.activation(dst, chunk_out(m, l, width), func, **kw).then_inc(taken_act, 1)

            for c in range(4):
                take(iqT[:, c, :])
                if c % 2:
                    round_to(6 + c // 2)
            take(ikT)
            take(iw[:, :, :].rearrange("p n h -> p (n h)"), width=NT * HEADS)
            round_to(9)
            for b in range(6):
                act.wait_ge(idx_raw, b + 1)
                dst = relu[0][:, b * 512:(b + 1) * 512] if b < 2 else relu[1][:, (b - 2) * 512:(b - 1) * 512]
                nc.scalar.activation(dst, aux[:, b, :], ACT.Relu).then_inc(idx_relu, 1)
            for c in range(4):
                take(qn[:, c, :], sq_to=sq[:, c, :])
                if c % 2:
                    round_to(c + 10)
            for c in range(4):
                take(kn[:, c, :], sq_to=sq[:, 4 + c, :])
                if c % 2:
                    round_to(c + 14)

            def qk_root(n):
                for b in range(2):
                    act.wait_ge(qk_sum, 2 * n + b + 1)
                    nc.scalar.activation(sq[:, 4 * n + 2 * b:4 * n + 2 * b + 2, :].rearrange("p c t -> p (c t)"),
                                         aux[:, 2 * n + b, :], ACT.Sqrt, bias=eps[:, 0:1], scale=1.0 / DH).then_inc(qk_std, 1)

            qk_root(0)
            for t in range(NT):
                take(v1[:, t, :], width=512)
                round_to(19 + 2 * t)
            qk_root(1)
            for c in range(4):
                take(cc[:, c, :])
                if c % 2:
                    round_to(c + 22)

            def exps(s, buf, t, l=None):
                act.wait_ge(s["negmax"], at(l, NT, t + 1))
                for h in range(HEADS):
                    nc.scalar.activation(probs(buf, t, h), probs(buf, t, h), ACT.Exp, bias=smax[:, t, h:h + 1],
                                         accum_out=ssum[:, t, h:h + 1]).then_inc(s["probs"], 1)

            def p_out(s, buf, t, l=None):
                for k in range(t + 1):
                    for hh in range(2):
                        b = 2 * t + 2 * k + hh
                        act.wait_ge(s["p_turned"], at(l, 6, b + 1))
                        nc.scalar.copy(probs_T(buf, t, k)[:, 4 * hh:4 * hh + 4, :].rearrange("p h q -> p (h q)"), aux[:, b, :]) \
                            .then_inc(s["p_out"], 1)

            for t in range(NT):
                for c in range(2):
                    take(u[:, 2 * t + c, 2:T + 2])
                round_to(27 + 2 * t)
                exps(att1, p_buf, t)
            nc.scalar.activation(warm[:, :], eps[:, 0:1], ACT.Sqrt)
            for c in range(4):
                take(cb[:, c, :])
                if c == 1:
                    round_to(c + 30)
            for t in range(NT):
                p_out(att1, pt_buf, t)
            round_to(33)
            for c in range(HC):
                act.wait_ge(conv_y, c + 1)
                nc.scalar.activation(sq[:, c, :], cc[:, c, :], ACT.Square).then_inc(conv_sq, 1)
            for t in range(NT):
                act.wait_ge(att1["y_sq"], t + 1)
                nc.scalar.activation(ystat[:, t, 1:2], ystat[:, t, 0:1], ACT.Sqrt, bias=eps[:, 0:1], scale=1.0 / 512) \
                    .then_inc(att1["y_std"], 1)
            act.wait_ge(conv_sum, 1)
            nc.scalar.activation(rstd[:, :], aux[:, 4, 0:T], ACT.Sqrt, bias=eps[:, 0:1], scale=1.0 / 512).then_inc(conv_std, 1)
            for t in range(NT):
                ts = slice(t * P, (t + 1) * P)
                act.wait_ge(att1["y_turned"], t + 1)
                for c in range(HC):
                    nc.scalar.activation(yaT[:, c, ts], aux[:, 2 + t, c * P:(c + 1) * P], ACT.Copy,
                                         scale=cols[:, ATT_W + c:ATT_W + c + 1]).then_inc(att1["y_done"], 1)
                act.wait_ge(att1["y_done"], (t + 1) * HC)
                nc.scalar.copy(xh[:, 0:HC, ts], yaT[:, :, ts]).then_inc(mix_hi, 1)
            for c in range(HC):
                act.wait_ge(conv_done, c + 1)
                nc.scalar.copy(xh[:, HC + c, :], cc[:, c, :]).then_inc(mix_hi, 1)
            for c in range(KC):
                act.wait_ge(taken_dve, c + 1)
                nc.scalar.activation(sq[:, c, :], xT[:, c, :], ACT.Square).then_inc(squares, 1)
                if c in (1, 3):
                    round_to(c + 34)
            act.wait_ge(sums, 2)
            nc.scalar.activation(rstd[:, :], aux[:, 5, 0:T], ACT.Sqrt, bias=eps[:, 0:1], scale=1.0 / D).then_inc(std_ready, 1)
            for c in range(KC):
                act.wait_ge(h_scaled, KC + c + 1)
                nc.scalar.activation(hT[:, c, :], hT[:, c, :], ACT.Identity, bias=mod[:, 3 * KC + c:3 * KC + c + 1]).then_inc(h_ready, 1)
            def next_head(g):
                nc.scalar.copy(s_cur[:, :, :].rearrange("p s k -> p (s k)"),
                               s_all[:, bass.ds(g, 1), :].rearrange("p o k -> p (o k)")).then_inc(s_taken, 1)

            def scored(lo, hi):
                for h in range(lo, hi):
                    for s in range(2):
                        act.wait_ge(queries, 2 * h + s + 1)
                        if h >= 2:
                            act.wait_ge(expert_scores, h - 1)
                        nc.scalar.copy(pq[:, h % 2, s, :], aux[:, 4 + s, 0:T]).then_inc(queries_out, 1)
                    act.wait_ge(expert_scores, h + 1)
                    nc.scalar.copy(s_all[:, h::EXPERT_HEADS, :], aux[:, h % 2, :].rearrange("p (n k) -> p n k", n=NT)).then_inc(scores_out, 1)

            def gate_exps(t, par, i, first=False, last=False):
                g = t * EXPERT_HEADS + par
                if first:
                    act.wait_ge(routed, 1)
                else:
                    act.wait_ge(diag_ready, 2 * i + g)
                nc.scalar.activation(gate, top, ACT.Exp, bias=negtop, accum_out=gate_sum).then_inc(gate_exp, 1)
                if not last:
                    next_head(2 * i + (g + 1))

            def gelus(t, par, i):
                g = t * EXPERT_HEADS + par
                act.wait_ge(u_used, i * (2 * PICKS) + ((g + 1) * PICKS + ROWS))
                nc.scalar.activation(act_dots, dots, ACT.Gelu_apprx_tanh).then_inc(dots_act, 1)

            scored(0, 1)
            act.wait_ge(scores_out, 1)
            next_head(0)
            scored(1, 2)
            act.wait_ge(scores_out, 2)
            gate_exps(0, 0, 0, first=True)
            scored(2, EARLY_HEADS)
            gelus(0, 0, 0)
            act.wait_ge(scores_out, EARLY_HEADS)
            gate_exps(0, 1, 0)
            scored(EARLY_HEADS, EXPERT_HEADS)
            gelus(0, 1, 0)
            act.wait_ge(scores_out, EXPERT_HEADS)
            with act.Fori(1, EXPERT_HEADS // 2) as i:
                for par in range(2):
                    gate_exps(0, par, i)
                    gelus(0, par, i)
            act.wait_ge(v_used, EXPERT_HEADS * PICKS + ROWS)
            for b in range(2):
                nc.scalar.copy(peer_tok[:, b * 512:(b + 1) * 512], aux[:, 2 + b, :]).then_inc(peer_out, 1)
            with act.Fori(0, EXPERT_HEADS // 2 - 1) as i:
                for par in range(2):
                    gate_exps(1, par, i)
                    gelus(1, par, i)
            for par in range(2):
                gate_exps(1, par, EXPERT_HEADS // 2 - 1, last=par == 1)
                gelus(1, par, EXPERT_HEADS // 2 - 1)
            act.wait_ge(peer_out, 4)
            act.dma_start(brow.rearrange("o l n -> o (l n)"), a["brow"]).then_inc(late_loaded, 16)
            act.wait_ge(s_taken, NT * EXPERT_HEADS)
            act.dma_start(lnv.rearrange("p l k f -> p (l k f)"),
                          a["lnv"].partition_broadcast(P).rearrange("p o d -> p (o d)")).then_inc(late_loaded, 16)

            def input_hi(l):
                for c in range(KC):
                    act.wait_ge(x_ready, l * KC + (c + 1))
                    nc.scalar.copy(xh[:, c, :], xT[:, c, :]).then_inc(xh_ready, 1)

            input_hi(0)
            with act.Fori(0, LAYERS) as l:
                taken[0] = 0

                def col(n):
                    return lcol[:, bass.ds(l, 1), n:n + 1].rearrange("p o n -> p (o n)")

                rounded[0] = 0
                round_to(PRING, l)
                for c in range(4):
                    take(qT[:, c, :], ACT.Identity, l, bias=col(BQ + c))
                    if c % 2:
                        round_to(c + 5, l)
                take(kT, ACT.Identity, l, bias=col(BK))
                round_to(9, l)
                take(v2[:, :, :].rearrange("p n f -> p (n f)"), ACT.Copy, l)
                round_to(10, l)
                for t in range(NT):
                    take(vg[:, t, :], ACT.Gelu, l, width=512)
                    round_to(12 + 2 * t, l)
                for c in range(4):
                    take(ug[:, c, :], ACT.Gelu, l, bias=col(BUG + c))
                    if c % 2:
                        round_to(c + 15, l)
                for t in range(NT):
                    exps(att2, p2_buf, t, l)
                for t in range(NT):
                    act.wait_ge(att2["sink_in"], l * NT + (t + 1))
                    nc.scalar.activation(ssink[:, t, :], ssink[:, t, :], ACT.Exp).then_inc(att2["sink_exp"], 1)
                for c in range(4):
                    take(zg[:, c, :], ACT.Silu, l, bias=col(BZG + c))
                    if c % 2:
                        round_to(c + 19, l)
                for t in range(NT):
                    p_out(att2, pt2_buf, t, l)
                for c in range(4):
                    take(za[:, c, :], ACT.Silu, l, bias=col(BZA + c))
                    if c % 2:
                        round_to(c + 23, l)
                for t in range(NT):
                    act.wait_ge(vn_stat, l * NT + (t + 1))
                    nc.scalar.activation(mv[:, t, 1:2], mv[:, t, 1:2], ACT.Sqrt, bias=eps[:, 1:2]).then_inc(vn_std, 1)
                for c in range(KC):
                    take(sga[:, c, :], ACT.Sigmoid, l, bias=col(BGA + c))
                    if c % 2:
                        round_to(c + 27, l)
                for c in range(KC - 2):
                    take(sgg[:, c, :], ACT.Sigmoid, l, bias=col(BGG + c))
                    if c % 2:
                        round_to(c + 35, l)
                act.wait_ge(att2["y_done"], l * NT + NT)
                chunk_wait(act, A2 - 1, l)
                for c in range(HC):
                    nc.scalar.copy(xh[:, c, :], ya2T[:, c, :]).then_inc(y_hi, 1)
                for c in range(KC - 2, KC):
                    take(sgg[:, c, :], ACT.Sigmoid, l, bias=col(BGG + c))
                round_to(44, l)
                act.wait_ge(yg_ready, l * NT + NT)
                for c in range(HC):
                    nc.scalar.copy(xh[:, HC + c, :], ug[:, c, :]).then_inc(y_hi, 1)
                for n in range(46, 52, 2):
                    round_to(n, l)
                for c in range(KC):
                    if c % 2 == 0:
                        round_to(52 + c, l)
                    if c < HC:
                        act.wait_ge(gated, l * KC + (c + 1))
                        nc.scalar.copy(xh[:, c, :], sga[:, c, :]).then_inc(merged_hi, 1)
                for c in range(HC, KC):
                    act.wait_ge(gated, l * KC + (c + 1))
                    nc.scalar.copy(xh[:, c, :], sga[:, c, :]).then_inc(merged_hi, 1)
                nc.scalar.activation(warm[:, :], eps[:, 0:1], ACT.Sqrt)
                round_to(60, l)
                round_to(62, l)
                for c in range(KC):
                    act.wait_ge(centred, l * KC + (c + 1))
                    nc.scalar.activation(sq2[:, c, :], res[:, c, :], ACT.Square).then_inc(centred_sq, 1)
                act.wait_ge(variances, l + 1)
                nc.scalar.activation(rstd[:, :], aux[:, 1, 0:T], ACT.Sqrt, bias=eps[:, 1:2]).then_inc(ln_std, 1)
                for c in range(KC):
                    act.wait_ge(ln_scaled, l * KC + (c + 1))
                    nc.scalar.activation(xT[:, c, :], res[:, c, :], ACT.Identity, bias=col(LNB + c)).then_inc(x_ready, 1)
                input_hi(l + 1)

        @block.tensor
        def _(pe):
            mm = nc.tensor.matmul
            chunk = [0]

            piece = [0]

            def next_pieces(n, l=None):
                first = piece[0]
                piece[0] += n
                for k in range(first, first + n):
                    split_wait(pe, k, l)
                return first

            def by_parts(o, w, x, start=True, stop=True):
                mm(o, w[0], x[0], start=start, stop=False)
                mm(o, w[0], x[1], start=False, stop=False)
                return mm(o, w[1], x[0], start=False, stop=stop)

            def input_parts(ready, count, at=0):
                seen = set()

                def chunk_parts(k):
                    if k not in seen:
                        pe.wait_ge(ready, count(k))
                        seen.add(k)
                    return xh[:, at + k, :], xl[:, at + k, :]
                return chunk_parts

            def whole(x, n, l=None, between=None, done=1):
                for _ in range(n):
                    hi, lo = parts(next_pieces(1, l), l)
                    chunks = hi.shape[1]
                    m = chunk[0]
                    chunk[0] += 1
                    bank_free(pe, m, l)
                    for k in range(chunks):
                        ins = by_parts(chunk_out(m, l), (hi[:, k, :], lo[:, k, :]), x(k), k == 0, k == chunks - 1)
                        if between:
                            between(k)
                    ins.then_inc(proj, done)

            def token_major(x, bias=None, l=None):
                m = chunk[0]
                chunk[0] += NT
                for half in range(2):
                    w = part_pairs(next_pieces(2, l))
                    for t in range(NT):
                        if half == 0:
                            bank_free(pe, m + t, l)
                        o = chunk_out(m + t, l, 512)[:, half * 256:half * 256 + 256]
                        for k in range(KC):
                            ins = by_parts(o.rearrange("p (s n) -> p s n", s=2), [z[:, t * P:(t + 1) * P] for z in x(k)], w(k, l),
                                           k == 0, k == KC - 1 and bias is None)
                        if bias is not None:
                            ins = mm(o, ones[0:1, :], bias(half * 256, 256), start=False, stop=True)
                        if half == 1:
                            ins.then_inc(proj, 1)

            pe.wait_ge(const_ready, 7)
            for c in range(KC):
                pe.wait_ge(squares, c + 1)
                ins = mm(aux[:, 0, 0:T], ones[:, :], sq[:, c, :], start=(c == 0), stop=(c == KC - 1))
            ins.then_inc(sums, 1)
            h_in = input_parts(h_split, lambda k: k + 1)
            whole(h_in, 3)
            small = chunk[0] + 2
            w = w_slot(2)
            w_wait(pe, 2)
            bank_free(pe, small - 1)

            def index_weights(step):
                t = step // (KC // NT)
                for k in range(NT * step - t * KC, NT * (step + 1) - t * KC):
                    mm(chunk_out(small)[:, t * HEADS:(t + 1) * HEADS], hT[:, k, t * P:(t + 1) * P], w[:, k, P:P + HEADS],
                       start=(k == 0), stop=(k == KC - 1))

            whole(h_in, 1, between=index_weights)
            whole(h_in, 1, done=2)
            chunk[0] += 1
            pe.wait_ge(taken_act, 5)
            for t in range(NT):
                for h in range(HEADS):
                    r = slice(64 * (h // 4), 64 * (h // 4) + 64)
                    ins = mm(logit_bank(t, h), iqT[r, h % 4, t * P:(t + 1) * P], ikT[r, 0:(t + 1) * P], start=True, stop=True)
                    if h % (4 >> t) == (4 >> t) - 1:
                        ins.then_inc(idx_raw, 1)
            whole(h_in, 4)
            whole(h_in, 4)

            def qk_sums(n):
                pe.wait_ge(qk_sq, 4 * n + 4)
                pe.wait_ge(idx_relu, 2 + 2 * n)
                for b in range(2):
                    mm(aux[:, 2 * n + b, :], blk[:, :], sq[:, 4 * n + 2 * b:4 * n + 2 * b + 2, :].rearrange("p c t -> p (c t)"),
                       start=True, stop=True).then_inc(qk_sum, 1)

            qk_sums(0)
            token_major(h_in)
            qk_sums(1)
            whole(h_in, 4)

            def logits(s, q, k, l=None):
                for t in range(NT):
                    for h in range(HEADS):
                        ins = mm(logit_bank(t, h), q(h, t), k(h, (t + 1) * P), start=True, stop=True)
                        if h % (4 >> t) == (4 >> t) - 1:
                            ins.then_inc(s["logits"], 1)

            def turn_p(s, buf, l=None):
                for t in range(NT):
                    pe.wait_ge(s["probs"], at(l, NT * HEADS, (t + 1) * HEADS))
                    for k in range(t + 1):
                        for h in range(HEADS):
                            b = 2 * t + 2 * k + h // 4
                            ins = nc.tensor.transpose(aux[:, b, (h % 4) * P:(h % 4 + 1) * P], probs(buf, t, h)[:, k * P:(k + 1) * P], ident[:, :])
                            if h % 4 == 3:
                                ins.then_inc(s["p_turned"], 1)

            def sum_v(s, buf, v, l=None):
                for t in range(NT):
                    pe.wait_ge(s["p_out"], at(l, 6, 2 if t == 0 else 6))
                    for h in range(HEADS):
                        for k in range(t + 1):
                            ins = mm(aux[:, t, h * DH:(h + 1) * DH], probs_T(buf, t, k)[:, h, :], v(h, k), start=(k == 0), stop=(k == t))
                    ins.then_inc(s["summed"], 1)

            def turn_y(s, y, l=None):
                for t in range(NT):
                    pe.wait_ge(s["y_ready"], at(l, NT, t + 1))
                    for c in range(HC):
                        ins = nc.tensor.transpose(aux[:, 2 + t, c * P:(c + 1) * P], y[:, t, c * P:(c + 1) * P], ident[:, :])
                    ins.then_inc(s["y_turned"], 1)

            pe.wait_ge(qk_ready, 2)
            pe.wait_ge(idx_relu, 6)
            pe.wait_ge(qk_std, 4)
            logits(att1, q1, k1)
            whole(h_in, 4)
            whole(h_in, 4)
            turn_p(att1, p_buf)
            sum_v(att1, pt_buf, lambda h, k: v1[:, k, head1(h) * DH:(head1(h) + 1) * DH])
            for c in range(HC):
                pe.wait_ge(conv_sq, c + 1)
                ins = mm(aux[:, 4, 0:T], ones[:, :], sq[:, c, :], start=(c == 0), stop=(c == HC - 1))
            ins.then_inc(conv_sum, 1)
            turn_y(att1, ytok)
            whole(input_parts(mix_split, lambda k: max(k + 1 + NT - HC, NT)), KC)
            for c in range(KC):
                pe.wait_ge(squares, KC + c + 1)
                ins = mm(aux[:, 5, 0:T], ones[:, :], sq[:, c, :], start=(c == 0), stop=(c == KC - 1))
            ins.then_inc(sums, 1)
            pe.wait_ge(h_ready, 2 * KC)
            def turn_h2(t):
                for c in range(KC):
                    ins = nc.tensor.transpose(h2_tok[t][:, c * P:(c + 1) * P], hT[:, c, t * P:(t + 1) * P], ident[:, :])
                ins.then_inc(h2_turned, 1)

            def score_heads(lo, hi):
                for h in range(lo, hi):
                    if h in PARKED:
                        k = PARKED.index(h)
                        pe.wait_ge(parked_loaded[k], 16)
                        w = parked[k].rearrange("p (k n) -> p k n", k=KC)
                    else:
                        n = UNITS_1.index(queries_of(h))
                        w_wait(pe, n)
                        w = w_slot(n)
                    for s in range(2):
                        if h:
                            pe.wait_ge(queries_out, 2 * h + s - 1)
                        for k in range(KC):
                            ins = mm(aux[:, 4 + s, 0:T], w[:, k, s * P:(s + 1) * P], hT[:, k, :], start=(k == 0), stop=(k == KC - 1))
                        ins.then_inc(queries, 1)
                    if h % 2 == 0:
                        n = UNITS_1.index(keys_of(h))
                        w_wait(pe, n)
                        sub[0] = w_slot(n)
                    pe.wait_ge(queries_out, 2 * h + 2)
                    if h >= 2:
                        pe.wait_ge(scores_out, h - 1)
                    for t in range(NT):
                        for s in range(2):
                            ins = mm(aux[:, h % 2, (2 * t + s) * KEYS:(2 * t + s + 1) * KEYS], pq[:, h % 2, s, t * P:(t + 1) * P],
                                     sub[0][:, 0, (2 * (h % 2) + s) * KEYS:(2 * (h % 2) + s + 1) * KEYS], start=True, stop=True)
                    ins.then_inc(expert_scores, 1)

            def zero_sums(t):
                for b in range(2):
                    mm(aux[:, 2 + 2 * t + b, :], zeros[:, :], hT[:, 0:2, :].rearrange("p c t -> p (c t)"),
                       start=True, stop=False, skip_group_check=True)

            def sum_rows(t, par, i, picks=PICKS):
                g = t * EXPERT_HEADS + par
                pe.wait_ge(diag_ready, 2 * i + (g + 1))
                for j in range(picks):
                    pe.wait_ge(v_loaded[j % ROWS], i * 64 + 16 * (2 * g + j // ROWS + 1))
                    for b in range(2):
                        ins = mm(aux[:, 2 + 2 * t + b, :], diag[:, j, :], rows[:, ROWS + j % ROWS, b * 512:(b + 1) * 512],
                                 start=False, stop=False, skip_group_check=True)
                    ins.then_inc(v_used, 1)

            def turn_sums(t):
                for b in range(2):
                    pe.wait_ge(peer_out, 2 * t + b + 1)
                    for c in range(4):
                        ins = nc.tensor.transpose(h2_tok[t][:, (4 * b + c) * P:(4 * b + c + 1) * P],
                                                  peer_tok[:, (4 * b + c) * P:(4 * b + c + 1) * P], ident[:, :])
                    ins.then_inc(peer_turned, 1)

            sub = [None]
            score_heads(0, 1)
            turn_h2(0)
            score_heads(1, EARLY_HEADS)
            zero_sums(0)
            sum_rows(0, 0, 0)
            score_heads(EARLY_HEADS, EXPERT_HEADS)
            pe.wait_ge(scores_out, EXPERT_HEADS)
            turn_h2(1)
            sum_rows(0, 1, 0)
            with pe.Fori(1, EXPERT_HEADS // 2) as i:
                for par in range(2):
                    sum_rows(0, par, i)
            zero_sums(1)
            turn_sums(0)
            with pe.Fori(0, EXPERT_HEADS // 2 - 1) as i:
                for par in range(2):
                    sum_rows(1, par, i)
            sum_rows(1, 0, EXPERT_HEADS // 2 - 1)
            sum_rows(1, 1, EXPERT_HEADS // 2 - 1, PICKS - SHARED)
            turn_sums(1)

            with pe.Fori(0, LAYERS) as l:
                chunk[0], piece[0] = 0, 0
                pe.wait_ge(const_ready, 10)

                def bias_row(n, width):
                    return brow[:, bass.ds(l, 1), n:n + width].rearrange("o l n -> o (l n)")

                x = input_parts(x_split, lambda k: l * KC + (k + 1))
                whole(x, 4, l)
                whole(x, 1, l)
                pe.wait_ge(late_loaded, 32)
                hi, lo = parts(next_pieces(1, l), l)
                m = chunk[0]
                chunk[0] += 1
                bank_free(pe, m, l)
                for t in range(NT):
                    ts = slice(t * P, (t + 1) * P)
                    for k in range(KC):
                        by_parts(chunk_out(m, l)[:, ts], [z[:, ts] for z in x(k)], (hi[:, k, :], lo[:, k, :]), k == 0, False)
                    ins = mm(chunk_out(m, l)[:, ts], ones[0:1, :], bias_row(RV, P), start=False, stop=True)
                ins.then_inc(proj, 1)
                token_major(x, lambda at, n: bias_row(RVG + at, n), l)
                pe.wait_ge(taken_act, l * A2 + (A1 + 6))
                logits(att2, q2, k2, l)
                whole(x, 4, l)
                whole(x, 4, l)
                turn_p(att2, p2_buf, l)
                whole(x, 4, l)
                sum_v(att2, pt2_buf, lambda h, k: v2[:, k, (h // 4) * DH:(h // 4 + 1) * DH], l)
                whole(x, 8, l)
                turn_y(att2, ytok2, l)
                for t in range(NT):
                    pe.wait_ge(vn_ready, l * NT + (t + 1))
                    for g in range(4):
                        o = aux[:, 4 + t, g * P:(g + 1) * P]
                        mm(o, vg[:, t, g * P:(g + 1) * P], wsT[:, bass.ds(l * 4 + g, 1), :].rearrange("p o t -> p (o t)"), start=True, stop=False)
                        ins = mm(o, ones[0:1, :], bias_row(RSP + g * P, P), start=False, stop=True)
                    ins.then_inc(mixed, 1)
                whole(x, 8, l)
                whole(input_parts(y_split, lambda k: l * 2 * HC + (k + 1)), KC, l)
                whole(input_parts(y_split, lambda k: l * 2 * HC + (HC + k + 1), HC), KC, l)
                merged = input_parts(merged_split, lambda k: l * KC + (k + 1))
                for c in range(0, KC + 2, 2):
                    if c < KC:
                        whole(merged, 2, l)
                    for k in range(max(c - 2, 0), c):
                        pe.wait_ge(taken_dve, l * D2 + (D1 + 2 * KC + k + 1))
                        ins = mm(aux[:, 0, 0:T], mean[:, :], res[:, k, :], start=(k == 0), stop=(k == KC - 1))
                ins.then_inc(means, 1)
                for c in range(KC):
                    pe.wait_ge(centred_sq, l * KC + (c + 1))
                    ins = mm(aux[:, 1, 0:T], mean[:, :], sq2[:, c, :], start=(c == 0), stop=(c == KC - 1))
                ins.then_inc(variances, 1)

        @block.vector
        def _(dve):
            v = nc.vector
            spare = dve_spare
            chain = Chain(dve, dve_chain)

            def ada_dots(lo, hi):
                for n in range(lo, hi):
                    dve.wait_ge(ada_loaded[n % ADA_RING], 16 * (n // ADA_RING + 1))
                    tile = ada[:, n % ADA_RING, :]
                    v.tensor_tensor_reduce(tile, tile, cbc, 1.0, 0.0, ALU.mult, ALU.add,
                                           mod[:, ada_column(n):ada_column(n) + 1]).then_inc(ada_used, 1)

            def ada_bias(lo, hi):
                dve.wait_ge(ada_used, hi)
                chain.link(v.tensor_tensor(mod[:, lo:hi], mod[:, lo:hi], cols[:, B_ADA + lo:B_ADA + hi], ALU.add))

            def ada_tiles(lo, hi):
                ada_dots(lo, hi)
                ada_bias(lo, hi)

            def part(n):
                return mod[:, n * KC:(n + 1) * KC]

            def norm(n, weight, scale):
                chain.link(v.tensor_scalar(gain[:, :], part(scale), 1.0, None, ALU.add))
                chain.link(v.tensor_tensor(gain[:, :], gain[:, :], cols[:, weight:weight + KC], ALU.mult))
                dve.wait_ge(std_ready, n + 1)
                chain.link(v.reciprocal(rstd[:, :], rstd[:, :]))
                for c in range(KC):
                    v.scalar_tensor_tensor(hT[:, c, :], xT[:, c, :], gain[:, c:c + 1], rstd[:, :], ALU.mult, ALU.mult).then_inc(h_scaled, 1)

            dve.wait_ge(c_silu, 1)
            dve.wait_ge(cols_loaded, 16)
            lowered = [0]

            def low_to(n, l=None):
                for k in range(lowered[0], n):
                    split_lo(dve, "d", k, l)
                lowered[0] = n

            def h_low(c):
                dve.wait_ge(h_ready, c + 1)
                v.tensor_tensor(xl[:, c, :], hT[:, c, :], full(xh[:, c, :]), ALU.subtract).then_inc(h_split, 1)

            dve.wait_ge(const_ready, 3)
            for c in range(KC):
                ada_dots(2 * c, 2 * c + 2)
                if c == 2:
                    dve.wait_ge(std_ready, 1)
                    v.reciprocal(rstd[:, :], rstd[:, :]).then_inc(rstd_ready, 1)
                dve.wait_ge(ada_used, 2 * c + 2)
                v.tensor_scalar(gain[:, c:c + 1], mod[:, KC + c:KC + c + 1], cols[:, B_ADA + KC + c:B_ADA + KC + c + 1], ones[:, 0:1],
                                ALU.add, ALU.add).then_inc(mod_ready, 1)
                v.tensor_tensor(mod[:, c:c + 1], mod[:, c:c + 1], cols[:, B_ADA + c:B_ADA + c + 1], ALU.add).then_inc(mod_ready, 1)
                for k in {3: (0, 1), 4: (2, 3), 5: (4,), 6: (5,), 7: (6,)}.get(c, ()):
                    h_low(k)
                if 2 * c == UNIT_0_AFTER:
                    low_to(1)
            h_low(KC - 1)
            low_to(4)
            ada_tiles(2 * KC, 3 * KC)

            dve.wait_ge(taken_act, 6)
            for h in range(HEADS):
                for t in range(NT):
                    dve.wait_ge(idx_relu, 2 * t + h // (4 >> t) + 1)
                    w, r = iw[:, t, head1(h):head1(h) + 1], probs(relu, t, h)
                    if h == 0:
                        chain.mark(v.tensor_scalar(score[t], r, w, None, ALU.mult))
                    else:
                        chain.wait(back=1)
                        chain.mark(v.scalar_tensor_tensor(score[t], r, w, score[t], ALU.mult, ALU.add))
            for t in range(NT):
                chain.wait(back=1 - t)
                v.tensor_scalar(score[t], score[t], IDX_SCALE, None, ALU.mult).then_inc(idx_score, 1)
            dve.wait_ge(idx_causal, NT)
            for n in range(TOPK // 8):
                for t in range(NT):
                    if n:
                        chain.wait(back=1)
                    chain.mark(v.max(top8[:, t, :], score[t] if n == 0 else left[t]))
                for t in range(NT):
                    chain.wait(back=1)
                    chain.mark(v.match_replace(left[t], top8[:, t, :], score[t] if n == 0 else left[t], LOW))
            for t in range(NT):
                chain.wait(back=1)
                chain.mark(v.tensor_tensor(keep[t], score[t], left[t], ALU.is_gt))
            for t in range(NT):
                chain.wait(back=1 - t)
                v.tensor_scalar(keep[t], keep[t], 1.0, -MASKED, ALU.subtract, ALU.mult).then_inc(keep_ready, 1)
            for n, (z, w) in enumerate(((qn, Q_W), (kn, K_W))):
                dve.wait_ge(qk_std, 2 * n + 2)
                r = sq[:, 4 * n:4 * n + 4, :].rearrange("p c t -> p (c t)")
                z = z.rearrange("p c t -> p (c t)")
                chain.link(v.reciprocal(r, r))
                v.scalar_tensor_tensor(z, z, cols[:, w:w + 1], r, ALU.mult, ALU.mult).then_inc(qk_ready, 1)

            def mask_logits(s, buf, bias, t, l=None):
                for h in range(HEADS):
                    dve.wait_ge(s["logits"], at(l, 6, 2 * t + h // (4 >> t) + 1))
                    if l is not None:
                        dve.sem_inc(spare)
                    chain.mark(v.tensor_tensor_reduce(probs(buf, t, h), logit_bank(t, h), bias(t, h), ATT_SCALE, LOW,
                                                      ALU.add, ALU.max, smax[:, t, h:h + 1]))
                chain.wait()

            lowered[0] = LO_1.rindex("p") + 1
            low_to(25)
            ada_dots(3 * KC, 3 * KC + ADA_RING)
            dve.wait_ge(keep_ready, 2)
            for t in range(NT):
                mask_logits(att1, p_buf, lambda t, h: keep[t], t)
                v.tensor_scalar(smax[:, t, :], smax[:, t, :], -1.0, None, ALU.mult).then_inc(att1["negmax"], 1)
                low_to(27 + 2 * t)

            def over_sums(s, y, t, l=None):
                chain.link(v.reciprocal(ssum[:, t, :], ssum[:, t, :]))
                dve.wait_ge(s["summed"], at(l, NT, t + 1))
                return v.tensor_tensor(y[:, t, :].rearrange("p (h d) -> p h d", d=DH),
                                       aux[:, t, :].rearrange("p (h d) -> p h d", d=DH),
                                       ssum[:, t, :].unsqueeze(2).broadcast_to([P, HEADS, DH]), ALU.mult)

            for c in range(HC):
                dve.wait_ge(u_ready, c + 1)
                chain.mark(v.tensor_scalar(cc[:, c, :], u[:, c, 2:T + 2], cols[:, CONV_W + 2 * HC + c:CONV_W + 2 * HC + c + 1],
                                           cols[:, CONV_B + c:CONV_B + c + 1], ALU.mult, ALU.add))
            for tap in (1, 0):
                for c in range(HC):
                    chain.wait(back=HC - 1)
                    chain.mark(v.scalar_tensor_tensor(cc[:, c, :], u[:, c, tap:T + tap], cols[:, CONV_W + tap * HC + c:CONV_W + tap * HC + c + 1],
                                                      cc[:, c, :], ALU.mult, ALU.add))
            low_to(31)
            base = 4 + 2 + 4 + 4 + NT
            for c in range(HC):
                dve.wait_ge(taken_act, base + 8 + c + 1)
                chain.wait(back=HC - 1 - c)
                v.tensor_tensor(cc[:, c, :], cc[:, c, :], cb[:, c, :], ALU.mult).then_inc(conv_y, 1)
            for t in range(NT):
                dve.wait_ge(att1["probs"], (t + 1) * HEADS)
                chain.link(over_sums(att1, ytok, t))
                v.tensor_tensor_reduce(p_buf[t][:, 0:512], ytok[:, t, :], ytok[:, t, :], 1.0, 0.0, ALU.mult, ALU.add,
                                       ystat[:, t, 0:1]).then_inc(att1["y_sq"], 1)
                if t == 0:
                    low_to(33)
            for t in range(NT):
                dve.wait_ge(att1["y_std"], t + 1)
                chain.link(v.reciprocal(ystat[:, t, 1:2], ystat[:, t, 1:2]))
                v.tensor_scalar(ytok[:, t, :], ytok[:, t, :], ystat[:, t, 1:2], None, ALU.mult).then_inc(att1["y_ready"], 1)
            dve.wait_ge(conv_std, 1)
            chain.link(v.reciprocal(rstd[:, :], rstd[:, :]))
            for c in range(HC):
                v.scalar_tensor_tensor(cc[:, c, :], cc[:, c, :], cols[:, CNV_W + c:CNV_W + c + 1], rstd[:, :], ALU.mult, ALU.mult) \
                    .then_inc(conv_done, 1)
            for t in range(NT):
                ts = slice(t * P, (t + 1) * P)
                dve.wait_ge(mix_hi, t + 1)
                v.tensor_tensor(xl[:, 0:HC, ts], yaT[:, :, ts], full(xh[:, 0:HC, ts]), ALU.subtract).then_inc(mix_split, 1)
            for c in range(HC):
                dve.wait_ge(mix_hi, NT + c + 1)
                v.tensor_tensor(xl[:, HC + c, :], cc[:, c, :], full(xh[:, HC + c, :]), ALU.subtract).then_inc(mix_split, 1)
            late = 4 * KC
            ada_dots(3 * KC + ADA_RING, late)
            for c in range(KC):
                if c in (2, 4):
                    low_to(33 + c)
                m = M1 - KC + c
                chunk_wait(dve, m)
                v.scalar_tensor_tensor(xT[:, c, :], chunk_out(m), mod[:, 2 * KC + c:2 * KC + c + 1], xT[:, c, :], ALU.mult, ALU.add) \
                    .then_inc(taken_dve, 1)
                ada_dots(late + c, late + c + 1)
            ada_bias(3 * KC, 5 * KC)
            dve.wait_ge(taken_dve, KC)
            norm(1, N2W, 4)
            ada_tiles(5 * KC, 6 * KC)

            def flat2(ap):
                return ap.rearrange("p s k -> p (s k)")

            def top16(*lists):
                n = len(lists)
                for half in range(2):
                    hs = slice(8 * half, 8 * half + 8)
                    for k, (src, rest, values, index) in enumerate(lists):
                        if half:
                            chain.wait(back=2 * (n - 1) - k)
                        chain.mark(v.max(values[:, hs], rest if half else src))
                    for k, (src, rest, values, index) in enumerate(lists):
                        chain.wait(back=n - 1 + (k if half == 0 else 0))
                        chain.mark(v.max_index(index[:, hs], values[:, hs], rest if half else src))
                        if half == 0:
                            chain.mark(v.match_replace(rest, values[:, hs], src, LOW))
                chain.wait()

            def route(i, g):
                dve.wait_ge(s_taken, 2 * i + (g + 1))
                dve.sem_inc(spare)
                top16(*[(s_cur[:, s, :], s_left[:, s, :], half_top[:, s, :], half_idx[:, s, :]) for s in range(2)])
                chain.link(v.tensor_tensor(combo.rearrange("p (k n) -> p k n", n=PICKS),
                                           half_top[:, 0, :].unsqueeze(2).broadcast_to([P, PICKS, PICKS]),
                                           half_top[:, 1, :].unsqueeze(1).broadcast_to([P, PICKS, PICKS]), ALU.add))
                top16((combo, combo_left, top, pos))
                chain.mark(v.tensor_scalar(negtop, top[:, 0:1], -1.0, None, ALU.mult))
                chain.mark(v.tensor_scalar(place[:, 0, :], pos, 4, None, ALU.logical_shift_right))
                chain.link(v.tensor_scalar(place[:, 1, :], pos, PICKS - 1, None, ALU.bitwise_and))
                rows_ = hit.rearrange("p s k n -> p (s k) n")
                chain.link(v.tensor_tensor(rows_, count16[:, :].unsqueeze(1).broadcast_to([P, 2 * PICKS, PICKS]),
                                           flat2(place).unsqueeze(2).broadcast_to([P, 2 * PICKS, PICKS]), ALU.is_equal))
                chain.link(v.tensor_tensor(hit, hit, half_idx.unsqueeze(2).broadcast_to([P, 2, PICKS, PICKS]), ALU.mult))
                chain.link(v.tensor_reduce(flat2(picked), rows_, AX, ALU.add))
                if g:
                    dve.wait_ge(v_used, i * (2 * PICKS) + ((g - 1) * PICKS + ROWS))
                v.scalar_tensor_tensor(expert[g % 2], picked[:, 0, :], float(KEYS), picked[:, 1, :], ALU.mult, ALU.add).then_inc(routed, 1)

            def picked_head(t, par, i, more=True):
                g = t * EXPERT_HEADS + par
                for j in range(PICKS):
                    if more and j == ROUTE_AT:
                        route(i, g + 1)
                    dve.wait_ge(u_loaded[j % ROWS], i * 64 + 16 * (2 * g + j // ROWS + 1))
                    row = rows[:, j % ROWS, :]
                    v.tensor_tensor_reduce(row, row, h2_tok[t], 1.0, 0.0, ALU.mult, ALU.add, dots[:, j:j + 1]).then_inc(u_used, 1)
                dve.wait_ge(gate_exp, 2 * i + (g + 1))
                chain.link(v.reciprocal(gate_inv, gate_sum))
                dve.wait_ge(dots_act, 2 * i + (g + 1))
                chain.link(v.scalar_tensor_tensor(weight, act_dots, gate_inv, gate, ALU.mult, ALU.mult))
                dve.wait_ge(v_used, i * (2 * PICKS) + (g * PICKS + ROWS))
                v.tensor_tensor(diag, ident[:, :].unsqueeze(1).broadcast_to([P, PICKS, P]),
                                weight.unsqueeze(2).broadcast_to([P, PICKS, P]), ALU.mult).then_inc(diag_ready, 1)

            route(0, 0)
            for t in range(NT):
                dve.wait_ge(h2_turned, t + 1)
                trips = EXPERT_HEADS // 2 - (t == NT - 1)
                with dve.Fori(0, trips) as i:
                    chain.enter(i, 2 * ROUTE_STEPS)
                    chain.spare = spare
                    for par in range(2):
                        picked_head(t, par, i)
                chain.leave(trips)
            for par in range(2):
                picked_head(NT - 1, par, EXPERT_HEADS // 2 - 1, more=par == 0)
            def join(t, b):
                dve.wait_ge(peer_turned, 2 * t + b + 1)
                for c in range(4 * b, 4 * b + 4):
                    x = xT[:, c, t * P:(t + 1) * P]
                    ins = v.scalar_tensor_tensor(x, h2_tok[t][:, c * P:(c + 1) * P], mod[:, 5 * KC + c:5 * KC + c + 1], x, ALU.mult, ALU.add)
                    if t:
                        ins.then_inc(x_ready, 1)

            dve.wait_ge(bias_iota, 1)
            for h in range(HEADS):
                v.tensor_scalar(bias8[:, h, :], distance, -(2.0 ** -(h + 1)) / ATT_SCALE, None, ALU.mult).then_inc(bias_lin, 1)
            for b in range(2):
                join(0, b)
            for j in range(PICKS - SHARED, PICKS):
                dve.wait_ge(v_loaded[j % ROWS], 16 * (NT * EXPERT_HEADS * PICKS // ROWS - (j < PICKS - ROWS)))
                row, before = rows[:, ROWS + j % ROWS, :], rows[:, ROWS + (j - 1) % ROWS, :]
                if j == PICKS - SHARED:
                    chain.link(v.tensor_scalar(row, row, weight[:, j:j + 1], None, ALU.mult))
                else:
                    chain.link(v.scalar_tensor_tensor(row, row, weight[:, j:j + 1], before, ALU.mult, ALU.add))
            dve.wait_ge(v_used, (NT * EXPERT_HEADS * PICKS - SHARED) + ROWS)
            for b in range(2):
                half = slice(b * 512, (b + 1) * 512)
                v.tensor_tensor(peer_tok[:, half], aux[:, 4 + b, :], row[:, half], ALU.add).then_inc(peer_out, 1)
            for b in range(2):
                join(1, b)

            with dve.Fori(0, LAYERS) as l:
                chain.enter(l, LAYER_STEPS)
                chain.spare = spare

                def taken(n):
                    dve.wait_ge(taken_act, l * A2 + (A1 + n))

                def col(n):
                    return lcol[:, bass.ds(l, 1), n:n + 1].rearrange("p o n -> p (o n)")

                lowered[0] = 1

                def merged_low(c):
                    dve.wait_ge(merged_hi, l * KC + (c + 1))
                    v.tensor_tensor(xl[:, c, :], sga[:, c, :], full(xh[:, c, :]), ALU.subtract).then_inc(merged_split, 1)

                low_to(1, l)
                for c in range(KC):
                    dve.wait_ge(xh_ready, l * KC + (c + 1))
                    v.tensor_tensor(xl[:, c, :], xT[:, c, :], full(xh[:, c, :]), ALU.subtract).then_inc(x_split, 1)
                low_to(12, l)
                for t in range(NT):
                    taken(6 + t + 1)
                    chain.link(v.bn_stats(bn[:, t, :], vg[:, t, :]))
                    v.bn_aggr(mv[:, t, :], bn[:, t, :]).then_inc(vn_stat, 1)
                low_to(14, l)
                dve.wait_ge(bias_ready, 1)
                for t in range(NT):
                    mask_logits(att2, p2_buf, lambda t, h: bias8[:, h, (NT - 1 - t) * P:], t, l)
                    sk = sink[:, bass.ds(l, 1), :].rearrange("p o h -> p (o h)")
                    chain.link(v.tensor_tensor(smax[:, t, :], smax[:, t, :], sk, ALU.max))
                    v.tensor_scalar(smax[:, t, :], smax[:, t, :], -1.0, None, ALU.mult).then_inc(att2["negmax"], 1)
                    dve.wait_ge(att2["negmax"], l * NT + (t + 1))
                    v.tensor_tensor(ssink[:, t, :], smax[:, t, :], sk, ALU.add).then_inc(att2["sink_in"], 1)
                    low_to(16 + 2 * t, l)
                low_to(26, l)
                for t in range(NT):
                    dve.wait_ge(att2["sink_exp"], l * NT + (t + 1))
                    chain.link(v.tensor_tensor(ssum[:, t, :], ssum[:, t, :], ssink[:, t, :], ALU.add))
                    over_sums(att2, ytok2, t, l).then_inc(att2["y_ready"], 1)
                low_to(28, l)
                for t in range(NT):
                    dve.wait_ge(vn_std, l * NT + (t + 1))
                    chain.link(v.reciprocal(mv[:, t, 1:2], mv[:, t, 1:2]))
                    chain.link(v.tensor_scalar(vg[:, t, :], vg[:, t, :], mv[:, t, 0:1], mv[:, t, 1:2], ALU.subtract, ALU.mult))
                    chain.link(v.tensor_tensor(vg[:, t, :], vg[:, t, :], lnv[:, bass.ds(l, 1), 0, :].rearrange("p o f -> p (o f)"), ALU.mult))
                    v.tensor_tensor(vg[:, t, :], vg[:, t, :], lnv[:, bass.ds(l, 1), 1, :].rearrange("p o f -> p (o f)"), ALU.add) \
                        .then_inc(vn_ready, 1)
                taken(8 + 8)
                chain.link(v.tensor_tensor(ug.rearrange("p c t -> p (c t)"), ug.rearrange("p c t -> p (c t)"), zg.rearrange("p c t -> p (c t)"), ALU.mult))
                low_to(32, l)
                taken(8 + 12)
                for t in range(NT):
                    ts = slice(t * P, (t + 1) * P)
                    dve.wait_ge(att2["y_turned"], l * NT + (t + 1))
                    v.tensor_tensor(ya2T[:, :, ts], aux[:, 2 + t, :].rearrange("p (c q) -> p c q", q=P), za[:, :, ts], ALU.mult) \
                        .then_inc(att2["y_done"], 1)
                for t in range(NT):
                    ts = slice(t * P, (t + 1) * P)
                    dve.wait_ge(mixed, l * NT + (t + 1))
                    v.tensor_tensor(ug[:, :, ts], aux[:, 4 + t, :].rearrange("p (c q) -> p c q", q=P), ug[:, :, ts], ALU.mult) \
                        .then_inc(yg_ready, 1)
                low_to(LO_2.index("p", 1), l)
                for c in range(2 * HC):
                    dve.wait_ge(y_hi, l * 2 * HC + (c + 1))
                    v.tensor_tensor(xl[:, c, :], (ya2T if c < HC else ug)[:, c % HC, :], full(xh[:, c, :]), ALU.subtract).then_inc(y_split, 1)
                taken(A2)
                for c in range(2 * KC):
                    m = A2 + c
                    chunk_wait(dve, m, l)
                    gate_ = (sga if c < KC else sgg)[:, c % KC, :]
                    v.tensor_tensor(gate_, chunk_out(m, l), gate_, ALU.mult).then_inc(taken_dve, 1)
                    if c >= KC:
                        dve.wait_ge(taken_dve, l * D2 + (D1 + c + 1))
                        v.tensor_tensor(sga[:, c % KC, :], sga[:, c % KC, :], gate_, ALU.add).then_inc(gated, 1)
                    if KC + 2 <= c < KC + 2 + HC:
                        merged_low(c - KC - 2)
                for c in range(HC, KC):
                    merged_low(c)
                lowered[0] = LO_2.rindex("p") + 1
                for c in range(KC):
                    if c in (2, 4):
                        low_to(58 + c, l)
                    m = A2 + 2 * KC + c
                    dve.wait_ge(xb_ready, l * KC + (c + 1))
                    chunk_wait(dve, m, l)
                    v.scalar_tensor_tensor(res[:, c, :], chunk_out(m, l), col(BOUT + c), xb[:, c, :], ALU.add, ALU.add).then_inc(taken_dve, 1)
                dve.wait_ge(means, l + 1)
                for c in range(KC):
                    v.tensor_tensor(res[:, c, :], res[:, c, :], aux[:, 0, 0:T], ALU.subtract).then_inc(centred, 1)
                dve.wait_ge(ln_std, l + 1)
                chain.link(v.reciprocal(rstd[:, :], rstd[:, :]))
                for c in range(KC):
                    v.scalar_tensor_tensor(res[:, c, :], res[:, c, :], col(LNG + c), rstd[:, :], ALU.mult, ALU.mult).then_inc(ln_scaled, 1)
            chain.leave(LAYERS)


def kernel(**inputs):
    import numpy as np
    import concourse.bacc as bacc
    from concourse.bass_utils import run_bass_kernel_spmd

    x = {k: np.ascontiguousarray(z) for k, z in inputs.items()}

    def units(plan, w):
        out = []
        for name, at, width, chunks in plan:
            z = w[name][:, at:at + width]
            out.append(z.reshape(chunks, P, width).transpose(1, 0, 2).reshape(P, chunks * width))
        return np.concatenate(out, 1)

    def col(z):
        return z.reshape(-1, P).T

    w_in = x["w_in"]
    part = {n: w_in[:, 512 * i:512 * i + 512] for i, n in enumerate(["q", "k", "v", "cb", "cc", "cx", "iq"])}
    ik, iw = w_in[:, 3584:3648], w_in[:, 3648:3656]
    w2, b2 = x["w_in_2"], x["b_in_2"]
    order = np.concatenate([np.arange(64) + 64 * h for c in range(4) for h in (c, c + 4)])
    order1 = np.concatenate([np.arange(DH) + DH * head1(h) for h in range(HEADS)])
    at2 = dict(k=512, v=640, za=768, ug=1280, vg=1792, zg=2304, ga=2816, gg=3840, end=4864)

    def cut(z, n, width):
        return z[..., at2[n]:at2[n] + width]

    arrays = {
        "xT": x["x"][0].T.reshape(KC, P, T),
        "c": x["c"],
        "w_ada": x["w_ada"].T.reshape(ADA_TILES, P, D),
        "w1": units(ALL_UNITS_1, part | {
            "idx": np.concatenate([ik, ik, iw], 1), "out": np.concatenate([x["w_out"][:512][order1], x["w_out"][512:]]),
            "wq": x["peer_wq"],
            "sub": x["peer_subkeys"].reshape(2 * EXPERT_HEADS, KEYS, P).transpose(2, 0, 1).reshape(P, -1)}),
        "peer_u": x["peer_u"],
        "peer_v": x["peer_v"],
        "cols": np.concatenate([col(x["norm1_w"]), col(x["norm2_w"]), col(x["b_ada"]), col(x["conv_w"].reshape(-1)), col(x["conv_b"]),
                                col(x["attn_out_norm_w"][order1]), col(x["conv_out_norm_w"]),
                                col(np.concatenate([x["q_norm_w"]] * 2)), col(np.concatenate([x["k_norm_w"]] * 2))], 1),
        "w2": np.stack([units(UNITS_2, {n: cut(w2[l], n, z) for n, z in dict(k=P, v=P, vg=512, ug=512, zg=512, za=512, ga=D, gg=D).items()} | {
            "q": w2[l][:, order], "ba": x["w_branch_attn_2"][l], "bg": x["w_branch_gmlp_2"][l], "out": x["w_out_2"][l]}) for l in range(LAYERS)]),
        "wsT": x["w_spatial_2"].reshape(LAYERS * 4, P, P).transpose(0, 2, 1),
        "lnv": np.stack([x["gmlp_ln_g_2"], x["gmlp_ln_b_2"]], 1).reshape(1, -1),
        "brow": np.concatenate([cut(b2, "v", 128), cut(b2, "vg", 512), x["b_spatial_2"].reshape(LAYERS, -1)], 1).reshape(1, -1),
        "sink": x["attn_sinks_2"].reshape(1, -1),
        "lcol": np.stack([np.concatenate([col(z) for z in (b2[l][order], b2[l][512:640], cut(b2[l], "ug", 512), cut(b2[l], "zg", 512),
                                                           cut(b2[l], "za", 512), cut(b2[l], "ga", D), cut(b2[l], "gg", D),
                                                           x["b_out_2"][l], x["ln_g_2"][l], x["ln_b_2"][l])], 1)
                          for l in range(LAYERS)], 1),
    }
    nc = bacc.Bacc("TRN2", target_bir_lowering=False, num_devices=1)
    aps = {}
    for name, z in arrays.items():
        arrays[name] = z = np.ascontiguousarray(z)
        aps[name] = nc.dram_tensor("in_" + name, z.shape, mybir.dt.from_np(z.dtype), kind="ExternalInput").ap()
    out = nc.dram_tensor("out_T", (KC, P, T), F32, kind="ExternalOutput").ap()
    build(nc, aps, out)
    done = run_bass_kernel_spmd(nc, [{"in_" + n: z for n, z in arrays.items()}], core_ids=[0])
    return done.results[0]["out_T"].reshape(D, T).T.reshape(1, T, D)
```
